# Optimizing a Trainium2 kernel written in Bass

```python
import jax, jax.numpy as jnp
from jax import lax
import numpy as np

D_MODEL = 1024
BATCH = 1
SEQ = 512
DEPTH = 1

CHUNK = 64
Q_BLOCK = 128
SB_HEADS = 8
SB_HD = 64
SB_DIM = SB_HEADS * SB_HD
ML_HEADS = 4
ML_HD = 128
ML_DIM = ML_HEADS * ML_HD
CONV_W = 4
MEM_LEN = 256
MEM_HEADS = 4
MEM_HD = 128
MEM_DIM = MEM_HEADS * MEM_HD
N_BRANCH = 3
N_KEYS = 128
N_EXPERTS = N_KEYS * N_KEYS
PEER_HEADS = 8
PEER_QDIM = 256
PEER_HALF = PEER_QDIM // 2
PEER_TOPK = 16
PEER_BLOCK = 128
EPS = 1e-6
IN_COLS = 3 * SB_DIM + 3 * ML_DIM + 2 * ML_HEADS + ML_DIM + MEM_DIM + N_BRANCH * D_MODEL

kernel_name = "hybrid_stickbreak_mlstm_memxattn_peer"

def _rmsnorm(x, g):
    xf = x.astype(jnp.float32)
    y = xf * lax.rsqrt(jnp.mean(xf * xf, axis=-1, keepdims=True) + EPS)
    return (y * g.astype(jnp.float32)).astype(x.dtype)

def _heads(t, n_heads, hd):
    b, s, _ = t.shape
    return t.reshape(b, s, n_heads, hd).transpose(0, 2, 1, 3)

def _merge(t):
    b, h, s, d = t.shape
    return t.transpose(0, 2, 1, 3).reshape(b, s, h * d)

def _split_points():
    sizes = [SB_DIM] * 3 + [ML_DIM] * 3 + [ML_HEADS, ML_HEADS, ML_DIM, MEM_DIM, N_BRANCH * D_MODEL]
    return [int(c) for c in np.cumsum(sizes)[:-1]]

def _causal_conv(x, w, b):
    s = x.shape[1]
    xp = jnp.pad(x, ((0, 0), (CONV_W - 1, 0), (0, 0)))
    y = b
    for k in range(CONV_W):
        y = y + w[k] * xp[:, k:k + s]
    return y

def _stick_breaking(q, k, v):
    b, h, s, d = q.shape
    nb = s // Q_BLOCK
    scale = d ** -0.5
    qb = q.astype(jnp.float32).reshape(b, h, nb, Q_BLOCK, d).transpose(2, 0, 1, 3, 4)
    starts = jnp.arange(nb, dtype=jnp.int32) * Q_BLOCK
    kf = k.astype(jnp.float32)
    vf = v.astype(jnp.float32)
    s_idx = jnp.arange(s, dtype=jnp.int32)

    def block(args):
        qi, start = args
        z = jnp.einsum('bhqd,bhkd->bhqk', qi, kf) * scale
        t_idx = start + jnp.arange(Q_BLOCK, dtype=jnp.int32)
        mask = s_idx[None, :] < t_idx[:, None]
        log_keep = jnp.where(mask, jax.nn.log_sigmoid(-z), 0.0)
        suffix = lax.cumsum(log_keep, axis=3, reverse=True) - log_keep
        a = jnp.where(mask, jnp.exp(jax.nn.log_sigmoid(z) + suffix), 0.0)
        return jnp.einsum('bhqk,bhkd->bhqd', a, vf)

    out = lax.map(block, (qb, starts))
    return out.transpose(1, 2, 0, 3, 4).reshape(b, h, s, d)

def _mlstm_step(carry, inp):
    c_st, n_st, m_st = carry
    q, k, v, ig, lf = inp
    l = q.shape[2]
    causal = jnp.tril(jnp.ones((l, l), dtype=bool))
    bcum = jnp.cumsum(lf, axis=-1)
    dmat = jnp.where(causal, bcum[..., :, None] - bcum[..., None, :] + ig[..., None, :], -jnp.inf)
    m_inter = bcum + m_st[..., None]
    m_t = jnp.maximum(m_inter, jnp.max(dmat, axis=-1))
    w = jnp.einsum('bhtd,bhsd->bhts', q, k) * jnp.exp(dmat - m_t[..., None])
    inter = jnp.exp(m_inter - m_t)
    num = jnp.einsum('bhts,bhse->bhte', w, v) + inter[..., None] * jnp.einsum('bhtd,bhde->bhte', q, c_st)
    den = jnp.sum(w, axis=-1) + inter * jnp.einsum('bhtd,bhd->bht', q, n_st)
    h = num / jnp.maximum(jnp.abs(den), jnp.exp(-m_t))[..., None]
    b_last = bcum[..., -1]
    g = b_last[..., None] - bcum + ig
    m_new = jnp.maximum(b_last + m_st, jnp.max(g, axis=-1))
    ws = jnp.exp(g - m_new[..., None])
    decay = jnp.exp(b_last + m_st - m_new)
    c_new = decay[..., None, None] * c_st + jnp.einsum('bhs,bhsd,bhse->bhde', ws, k, v)
    n_new = decay[..., None] * n_st + jnp.einsum('bhs,bhsd->bhd', ws, k)
    return (c_new, n_new, m_new), h

def _mlstm(q, k, v, ig, lf):
    b, h, s, d = q.shape
    nc = s // CHUNK

    def chunks(t):
        return jnp.moveaxis(t.reshape(b, h, nc, CHUNK, *t.shape[3:]), 2, 0)

    init = (jnp.zeros((b, h, d, d), jnp.float32), jnp.zeros((b, h, d), jnp.float32),
            jnp.zeros((b, h), jnp.float32))
    _, hs = lax.scan(_mlstm_step, init, (chunks(q), chunks(k), chunks(v), chunks(ig), chunks(lf)))
    return jnp.moveaxis(hs, 0, 2).reshape(b, h, s, d)

def _memory_attention(q, memn, w_kv, q_g, k_g):
    kv = memn @ w_kv
    km, vm = jnp.split(kv, 2, axis=-1)
    qh = _rmsnorm(_heads(q, MEM_HEADS, MEM_HD), q_g).astype(jnp.float32)
    kh = _rmsnorm(_heads(km, MEM_HEADS, MEM_HD), k_g).astype(jnp.float32)
    vh = _heads(vm, MEM_HEADS, MEM_HD).astype(jnp.float32)
    sc = jnp.einsum('bhqd,bhkd->bhqk', qh, kh) * (MEM_HD ** -0.5)
    p = jax.nn.softmax(sc, axis=-1)
    return _merge(jnp.einsum('bhqk,bhkd->bhqd', p, vh)).astype(q.dtype)

def _peer(xn, w_q, k1, k2, u_tab, v_tab):
    b, s, d = xn.shape
    t = b * s
    xf = xn.reshape(t, d)
    qry = (xf @ w_q).reshape(t, PEER_HEADS, 2, PEER_HALF).astype(jnp.float32)
    s1 = jnp.einsum('thd,hkd->thk', qry[:, :, 0], k1.astype(jnp.float32))
    s2 = jnp.einsum('thd,hkd->thk', qry[:, :, 1], k2.astype(jnp.float32))
    v1, i1 = lax.top_k(s1, PEER_TOPK)
    v2, i2 = lax.top_k(s2, PEER_TOPK)
    cand = (v1[..., :, None] + v2[..., None, :]).reshape(t, PEER_HEADS, PEER_TOPK * PEER_TOPK)
    top_v, top_c = lax.top_k(cand, PEER_TOPK)
    e1 = jnp.take_along_axis(i1, top_c // PEER_TOPK, axis=-1)
    e2 = jnp.take_along_axis(i2, top_c % PEER_TOPK, axis=-1)
    idx = e1 * N_KEYS + e2
    gates = jax.nn.softmax(top_v, axis=-1).astype(xn.dtype)
    nb = t // PEER_BLOCK

    def block(args):
        xb, ib, gb = args
        u = u_tab[ib]
        act = jax.nn.gelu(jnp.einsum('phkd,pd->phk', u, xb), approximate=False)
        return jnp.einsum('phk,phkd->pd', gb * act, v_tab[ib])

    out = lax.map(block, (xf.reshape(nb, PEER_BLOCK, d), idx.reshape(nb, PEER_BLOCK, PEER_HEADS, PEER_TOPK),
                          gates.reshape(nb, PEER_BLOCK, PEER_HEADS, PEER_TOPK)))
    return out.reshape(b, s, d)

def setup_inputs(seed: int = 0) -> dict:
    key = jax.random.key(seed)
    ks = jax.random.split(key, 26)

    def nrm(k, shape, scale):
        return jax.random.normal(k, shape, jnp.float32) * scale

    L = DEPTH
    return {
        "x": nrm(ks[0], (BATCH, SEQ, D_MODEL), 1.0),
        "mem": nrm(ks[1], (BATCH, MEM_LEN, D_MODEL), 1.0),
        "g_mix": 1.0 + nrm(ks[2], (L, D_MODEL), 0.1),
        "w_in": nrm(ks[3], (L, D_MODEL, IN_COLS), D_MODEL ** -0.5),
        "b_igate": nrm(ks[4], (L, ML_HEADS), 0.1),
        "b_fgate": 3.0 + nrm(ks[5], (L, ML_HEADS), 0.5),
        "conv_w": nrm(ks[6], (L, CONV_W, 2 * ML_DIM), 0.5),
        "conv_b": nrm(ks[7], (L, 2 * ML_DIM), 0.02),
        "ml_norm_g": 1.0 + nrm(ks[8], (L, ML_HD), 0.1),
        "mem_norm_g": 1.0 + nrm(ks[9], (L, D_MODEL), 0.1),
        "w_mem_kv": nrm(ks[10], (L, D_MODEL, 2 * MEM_DIM), D_MODEL ** -0.5),
        "q_norm_g": 1.0 + nrm(ks[11], (L, MEM_HD), 0.1),
        "k_norm_g": 1.0 + nrm(ks[12], (L, MEM_HD), 0.1),
        "w_sb_o": nrm(ks[13], (L, SB_DIM, D_MODEL), SB_DIM ** -0.5),
        "w_ml_o": nrm(ks[14], (L, ML_DIM, D_MODEL), ML_DIM ** -0.5),
        "w_mem_o": nrm(ks[15], (L, MEM_DIM, D_MODEL), MEM_DIM ** -0.5),
        "b_gate": nrm(ks[16], (L, N_BRANCH * D_MODEL), 0.1),
        "w_out": nrm(ks[17], (L, D_MODEL, D_MODEL), D_MODEL ** -0.5),
        "g_ffn": 1.0 + nrm(ks[18], (L, D_MODEL), 0.1),
        "w_peer_q": nrm(ks[19], (L, D_MODEL, PEER_HEADS * PEER_QDIM), D_MODEL ** -0.5),
        "peer_k1": nrm(ks[20], (L, PEER_HEADS, N_KEYS, PEER_HALF), PEER_HALF ** -0.5),
        "peer_k2": nrm(ks[21], (L, PEER_HEADS, N_KEYS, PEER_HALF), PEER_HALF ** -0.5),
        "peer_u": nrm(ks[22], (L, N_EXPERTS, D_MODEL), D_MODEL ** -0.5),
        "peer_v": nrm(ks[23], (L, N_EXPERTS, D_MODEL), 0.5),
    }

def reference(x, mem, g_mix, w_in, b_igate, b_fgate, conv_w, conv_b, ml_norm_g, mem_norm_g, w_mem_kv,
              q_norm_g, k_norm_g, w_sb_o, w_ml_o, w_mem_o, b_gate, w_out, g_ffn, w_peer_q, peer_k1,
              peer_k2, peer_u, peer_v):
    bsz, s, _ = x.shape
    h = x
    splits = _split_points()
    for l in range(DEPTH):
        xn = _rmsnorm(h, g_mix[l])
        proj = xn @ w_in[l]
        (sb_q, sb_k, sb_v, ml_q, ml_k, ml_v, ml_i, ml_f, ml_o, mem_q, gate_pre) = jnp.split(proj, splits, axis=-1)

        y_sb = _stick_breaking(_heads(sb_q, SB_HEADS, SB_HD), _heads(sb_k, SB_HEADS, SB_HD),
                               _heads(sb_v, SB_HEADS, SB_HD))
        y_sb = _merge(y_sb).astype(x.dtype)

        qk = jax.nn.silu(_causal_conv(jnp.concatenate([ml_q, ml_k], axis=-1), conv_w[l], conv_b[l]))
        mq, mk = jnp.split(qk, 2, axis=-1)
        qh = _heads(mq, ML_HEADS, ML_HD).astype(jnp.float32)
        kh = _heads(mk, ML_HEADS, ML_HD).astype(jnp.float32) * (ML_HD ** -0.5)
        vh = _heads(ml_v, ML_HEADS, ML_HD).astype(jnp.float32)
        ig = (ml_i + b_igate[l]).astype(jnp.float32).transpose(0, 2, 1)
        lf = jax.nn.log_sigmoid((ml_f + b_fgate[l]).astype(jnp.float32)).transpose(0, 2, 1)
        hm = _mlstm(qh, kh, vh, ig, lf)
        hm = _rmsnorm(hm, ml_norm_g[l])
        y_ml = (_merge(hm) * jax.nn.sigmoid(ml_o.astype(jnp.float32))).astype(x.dtype)

        memn = _rmsnorm(mem, mem_norm_g[l])
        y_mem = _memory_attention(mem_q, memn, w_mem_kv[l], q_norm_g[l], k_norm_g[l])

        gates = jax.nn.sigmoid(gate_pre + b_gate[l]).reshape(bsz, s, N_BRANCH, D_MODEL)
        merged = (gates[:, :, 0] * (y_sb @ w_sb_o[l]) + gates[:, :, 1] * (y_ml @ w_ml_o[l])
                  + gates[:, :, 2] * (y_mem @ w_mem_o[l]))
        h = h + merged @ w_out[l]

        hn = _rmsnorm(h, g_ffn[l])
        h = h + _peer(hn, w_peer_q[l], peer_k1[l], peer_k2[l], peer_u[l], peer_v[l])
    return h


_drawn_inputs = setup_inputs


def setup_inputs(seed=0):
    import zlib

    import numpy as np

    out = dict(_drawn_inputs(seed))
    spreads = {}
    factors = {'b_igate': 64.0, 'conv_b': 3.348, 'q_norm_g': 3.16, 'k_norm_g': 3.259}
    for name, (base, spread) in spreads.items():
        noise = np.random.default_rng([zlib.crc32(name.encode()), seed]).standard_normal(out[name].shape)
        drawn = base * np.exp(spread * noise) if base else spread * noise
        out[name] = __import__('jax').numpy.asarray(drawn.astype(out[name].dtype))
    for name, factor in factors.items():
        out[name] = (out[name] * factor).astype(out[name].dtype)
    return out
```

```python
from contextlib import ExitStack

import concourse.bass as bass
import numpy as np
from concourse import mybir

F32 = mybir.dt.float32
BF16 = mybir.dt.bfloat16
U32 = mybir.dt.uint32
ALU = mybir.AluOpType
ACT = mybir.ActivationFunctionType
AX = mybir.AxisListType

P = 128
T = 512
TT = T // P
D = 1024
KD = D // P
MEM = 256
MT = MEM // P
SBH, SBD = 8, 64
MLH = 4
NH = 4
HD = 128
BANK = 512
CAUSAL_AT = [0, 512, 1024, 896]
CAUSAL = 1280
EPS = 1e-6
HD_SCALE = HD ** -0.5
PH = 8
TOPK = 16
NKEYS = 128
NEG = -3.0e38
HALF = T // 2

C_MIX, C_MEM, C_FFN, C_BGATE, C_CONVW, C_CONVB, C_MLG, C_QG, C_KG, NCOLS = 0, 8, 16, 24, 48, 80, 88, 89, 90, 91


def at_least(eng, sem, value):
    if isinstance(value, int) and value <= 0:
        return
    eng.wait_ge(sem, value)


def build(nc, A, out):
    ctx = ExitStack()
    with ctx:
        def sb(name, cols, dt=F32, rows=P):
            return ctx.enter_context(nc.sbuf_tensor(name, [rows, cols], dt))

        def sem(name):
            return ctx.enter_context(nc.semaphore(name))

        ident = sb("ident", P)
        neg_tri = sb("neg_tri", P)
        neg_ones = sb("neg_ones", P)
        iota_key = sb("iota_key", NKEYS, BF16)
        iota_top = sb("iota_top", TOPK)
        zero_bf = sb("zero_bf", P, BF16)
        eps_col = sb("eps_col", 1)
        cols = sb("cols", NCOLS)
        qg_scaled = sb("qg_scaled", 1)
        bif = sb("bif", 2, rows=4)
        sums = sb("sums", 64)
        roots = sb("roots", 64)
        rstd = sb("rstd", 64)
        key_cols = sb("key_cols", 32)
        thr_cols = sb("thr_cols", 16)
        den = sb("den", 32)

        STORE = 52240
        store = sb("store", STORE)
        place = {}

        def carve(name, at, size):
            assert at + size <= STORE, (name, at + size)
            place[name] = store[:, at:at + size]
            return place[name]

        xs = carve("xs", 0, 4096)
        mems = carve("mems", 4096, 2048)
        xT = carve("xT", 6144, 4096)
        wt = carve("wt", 10240, 4096)
        wn = carve("wn", 14336, 8192)
        projT = carve("projT", 22528, 8192)
        sb_v = carve("sb_v", 30720, 2048)
        ml_v = carve("ml_v", 32768, TT * MLH * (HD + 1))
        ml_o = carve("ml_o", 34832, 2048)
        mem_q = carve("mem_q", 36880, 2048)
        y_sbT = carve("y_sbT", 38928, 2048)
        y_mlT = carve("y_mlT", 40976, 2048)
        y_memT = carve("y_memT", 43024, 2048)
        rows = carve("rows", 40976, 4096)
        work = carve("work", 45072, 5120)
        memT = carve("memT", 50192, 2048)
        mem_qT = carve("mem_qT", 0, 2048)
        mem_kT = carve("mem_kT", 2048, 1024)
        mem_k = carve("mem_k", 3072, 1024)
        mem_v = carve("mem_v", 4096, 1024)
        gate_s = carve("gate_s", 5120, 1024)
        qk_squares = carve("qk_squares", 0, 3072)
        y_ml = carve("y_ml", 14336, 2048)
        squares = carve("squares", 16384, 2048)
        mergedT = carve("mergedT", 22528, 4096)
        x_again = carve("x_again", 26624, 4096)
        h_res = carve("h_res", 0, 4096)
        hT = carve("hT", 6144, 4096)
        junk = carve("junk", 45072, 1024)
        h_scaled = carve("h_scaled", 30720, 4096)
        qryT = carve("qryT", 34816, 8192)
        keysT = carve("keysT", 14336, 2048)
        scores = carve("scores", 16384, 4096)
        top_in = carve("top_in", 22528, 2048)
        cand = carve("cand", 24576, 2048)
        cand2 = carve("cand2", 26624, 2048)
        pick = carve("pick", 28672, 2048)
        top_small = carve("top_small", 43008, 3072)
        G = carve("G", 19456, NKEYS * HALF)
        ubuf = carve("ubuf", 10240, 2048)
        vbuf = carve("vbuf", 12288, 2048)
        onehot = carve("onehot", 14336, 2 * 4 * 3 * P // 2)
        act_g = carve("act_g", 17408, 512)
        act_w = carve("act_w", 17920, 512)
        eT = carve("eT", 4096, 3 * T)
        gate_hi = carve("gate_hi", 18432, T)
        gate_lo = carve("gate_lo", 18944, T)

        xs3 = xs.rearrange("p (t d) -> p t d", d=D)
        mems3 = mems.rearrange("p (t d) -> p t d", d=D)
        xT3 = xT.rearrange("p (k t) -> p k t", t=T)
        memT3 = memT.rearrange("p (k t) -> p k t", t=MEM)
        hT3 = hT.rearrange("p (k t) -> p k t", t=T)
        h3 = h_res.rearrange("p (t d) -> p t d", d=D)
        hs3 = h_scaled.rearrange("p (t d) -> p t d", d=D)
        xa3 = x_again.rearrange("p (t d) -> p t d", d=D)
        wt4 = wt.rearrange("p (s k c) -> p s k c", s=4, c=P)
        wn4 = wn.rearrange("p (s k c) -> p s k c", s=2, c=BANK)
        projT3 = projT.rearrange("p (g t) -> p g t", t=T)
        mergedT3 = mergedT.rearrange("p (g t) -> p g t", t=T)
        qryT3 = qryT.rearrange("p (g t) -> p g t", t=T)
        keysT3 = keysT.rearrange("p (g k) -> p g k", k=NKEYS)
        sb_v3 = sb_v.rearrange("p (t c) -> p t c", c=512)
        ml_v4 = ml_v.rearrange("p (t h c) -> p t h c", t=TT, c=HD + 1)
        ml_o3 = ml_o.rearrange("p (t c) -> p t c", c=512)
        mem_q3 = mem_q.rearrange("p (t c) -> p t c", c=512)
        mem_k3 = mem_k.rearrange("p (t c) -> p t c", c=512)
        mem_v3 = mem_v.rearrange("p (t c) -> p t c", c=512)
        mem_qT3 = mem_qT.rearrange("p (h t) -> p h t", t=T)
        mem_kT3 = mem_kT.rearrange("p (h t) -> p h t", t=MEM)
        y_ml4 = y_ml.rearrange("p (t h c) -> p t h c", t=TT, c=HD)
        y_ml3 = y_ml.rearrange("p (t c) -> p t c", c=512)
        yT = [y.rearrange("p (g t) -> p g t", t=T) for y in (y_sbT, y_mlT, y_memT)]
        gate_s3 = gate_s.rearrange("p (s t) -> p s t", t=T)
        eT3 = eT[:, :].rearrange("p (s t) -> p s t", t=T)
        w_if = work[:, 2048:2048 + KD * 8].rearrange("p (k c) -> p k c", c=8)
        conv_out = work[:, 0:1024].rearrange("p (s t) -> p s t", t=T)

        lk = [work[:, 0:CAUSAL], work[:, CAUSAL:2 * CAUSAL]]
        aw = [work[:, 2 * CAUSAL:3 * CAUSAL], work[:, 3 * CAUSAL:4 * CAUSAL]]
        probs = [work[:, 0:1024], work[:, 1024:2048]]
        probsT = work[:, 2048:4096].rearrange("p (s m t) -> p s m t", s=2, t=T)

        def row(n):
            return rows[0:4, n * T:(n + 1) * T]
        r_abs, r_f, r_lf, r_b, r_a, r_max, r_m, r_zero = (row(n) for n in range(8))
        sel = store[0:4, 50192:50192 + 4 * P]
        sel3 = sel.rearrange("p (h c) -> p h c", c=P)

        sc3 = scores.rearrange("p (s c) -> p s c", c=16 * NKEYS)
        S_X, S_Q, S_K, S_ML, S_H = 0, 6, 22, 30, 46
        top_v = top_small[:, 0:256]
        top_i = top_small[:, 256:512].bitcast(U32)
        top_if = top_small[:, 512:768]
        best_v = top_small[:, 768:896]
        best_c = top_small[:, 896:1024].bitcast(U32)
        best_i = top_small[:, 1024:1152].bitcast(U32)
        best_j = top_small[:, 1152:1280].bitcast(U32)
        best_if = top_small[:, 1280:1408]
        best_jf = top_small[:, 1408:1536]
        g_exp = top_small[:, 1536:1664]
        lists = top_small[:, 1664:2048].rearrange("p (s c) -> p s c", c=P)
        g_sum = top_small[:, 2048:2056]
        g_rec = top_small[:, 2056:2064]
        Gk = G.rearrange("p (k t) -> p k t", t=HALF)
        ub = ubuf.rearrange("p (s k c) -> p s k c", s=2, c=P)
        vb = vbuf.rearrange("p (s c) -> p s c", c=D)
        oh = onehot.bitcast(BF16).rearrange("p (s j w c) -> p s j w c", s=2, j=4, c=P)
        ga = act_g.rearrange("p (s t) -> p s t", t=HALF)
        gw = act_w.rearrange("p (s t) -> p s t", t=HALF)

        ps = ctx.enter_context(nc.psum_tensor("ps", [P, 8 * BANK], F32))

        def bank(b, n=1):
            return ps[:, b * BANK:(b + n) * BANK]

        const_set, const_made = sem("const_set"), sem("const_made")
        sel_made = sem("sel_made")
        params_in, wif_in, keys_in, xa_in = sem("params_in"), sem("wif_in"), sem("keys_in"), sem("xa_in")
        x_in = [sem(f"x_in{i}") for i in range(TT)]
        mem_in = sem("mem_in")
        squared, rooted, scaled = sem("squared"), sem("rooted"), sem("scaled")
        turned, xT_out, memT_out = sem("turned"), sem("xT_out"), sem("memT_out")
        act_step, dve_step, pool_step = sem("act_step"), sem("dve_step"), sem("pool_step")
        wt_in = [sem(f"wt_in{s}") for s in range(4)]
        t_done = [sem(f"t_done{s}") for s in range(4)]
        t_out = [sem(f"t_out{s}") for s in range(4)]
        wn_in = [sem(f"wn_in{s}") for s in range(2)]
        n_done = [sem(f"n_done{s}") for s in range(4)]
        n_out = [sem(f"n_out{s}") for s in range(4)]
        if_done, if_ln = sem("if_done"), sem("if_ln")
        rows_made, thr_made, cols_turned, cols_out = sem("rows_made"), sem("thr_made"), sem("cols_turned"), sem("cols_out")
        q_scaled, conv_done, silu_done, sig_o = sem("q_scaled"), sem("conv_done"), sem("silu_done"), sem("sig_o")
        qk_squared, qk_rooted, qk_normed = sem("qk_squared"), sem("qk_rooted"), sem("qk_normed")
        z_ready, ln_ready, keep_ready, keep_masked = sem("z_ready"), sem("ln_ready"), sem("keep_ready"), sem("keep_masked")
        suffix_done, a_ready, a_masked, y_done, y_out = (
            sem("suffix_done"), sem("a_ready"), sem("a_masked"), sem("y_done"), sem("y_out"))
        s_ready, d_ready, e_ready, w_ready, w_masked, num_done, num_out = (
            sem("s_ready"), sem("d_ready"), sem("e_ready"), sem("w_ready"), sem("w_masked"), sem("num_done"),
            sem("num_out"))
        ml_squared, ml_rooted, ml_normed, mlT_done, mlT_out = (
            sem("ml_squared"), sem("ml_rooted"), sem("ml_normed"), sem("mlT_done"), sem("mlT_out"))
        qkT_done, qkT_out = sem("qkT_done"), sem("qkT_out")
        ms_ready, mmax_ready, mexp_ready, mp_ready, mpT_done, mpT_out, my_done, my_out = (
            sem("ms_ready"), sem("mmax_ready"), sem("mexp_ready"), sem("mp_ready"), sem("mpT_done"),
            sem("mpT_out"), sem("my_done"), sem("my_out"))
        gated = [sem(f"gated{s}") for s in range(2)]
        h_squared, h_rooted, h_normed, hT_done, hT_out = (
            sem("h_squared"), sem("h_rooted"), sem("h_normed"), sem("hT_done"), sem("hT_out"))
        score_done, score_out, score_used = sem("score_done"), sem("score_out"), sem("score_used")
        cand_top, cand_exp, list_ready, list_turned, list_out = (
            sem("cand_top"), sem("cand_exp"), sem("list_ready"), sem("list_turned"), sem("list_out"))
        oh_ready, gate_done, gate_out = sem("oh_ready"), sem("gate_done"), sem("gate_out")
        u_in = [sem(f"u_in{s}") for s in range(2)]
        v_in = [sem(f"v_in{s}") for s in range(2)]
        u_done, gelu_done, gated_act, v_done = sem("u_done"), sem("gelu_done"), sem("gated_act"), sem("v_done")
        acc_zero, acc_done, acc_out, out_ready, stored = (
            sem("acc_zero"), sem("acc_done"), sem("acc_out"), sem("out_ready"), sem("stored"))

        PROJ_I = 4
        BR_I = 12
        PQ_I = 4
        BR_BASE, PQ_BASE = PROJ_I, PROJ_I + BR_I
        CONSTS = 6

        block = ctx.enter_context(nc.Block())

        @block.gpsimd
        def _(pool):
            pool.memset(ident[:, :], 0.0).then_inc(const_set, 1)
            pool.memset(neg_tri[:, :], -1.0).then_inc(const_set, 1)
            pool.memset(neg_ones[:, :], -1.0).then_inc(const_set, 1)
            pool.memset(zero_bf[:, :], 0.0).then_inc(const_set, 1)
            pool.memset(eps_col[:, :], EPS).then_inc(const_set, 1)
            pool.memset(ml_v4[:, :, :, HD:HD + 1], 1.0).then_inc(const_set, 1)
            pool.wait_ge(const_set, CONSTS)
            pool.affine_select(out=ident[:, :], in_=ident[:, :], compare_op=ALU.not_equal, fill=1.0, base=0,
                               pattern=[[-1, P]], channel_multiplier=1).then_inc(const_made, 1)
            pool.affine_select(out=neg_tri[:, :], in_=neg_tri[:, :], compare_op=ALU.is_ge, fill=0.0, base=0,
                               pattern=[[-1, P]], channel_multiplier=1).then_inc(const_made, 1)
            pool.iota(iota_key[:, :], pattern=[[1, NKEYS]], base=0, channel_multiplier=0,
                      allow_small_or_imprecise_dtypes=True).then_inc(const_made, 1)
            pool.iota(iota_top[:, :], pattern=[[1, TOPK]], base=0, channel_multiplier=0,
                      allow_small_or_imprecise_dtypes=True).then_inc(const_made, 1)

            def keep_causal(buf, strict, done):
                for kt in range(TT):
                    block_ = buf[:, CAUSAL_AT[kt]:CAUSAL_AT[kt] + P]
                    ins = pool.affine_select(out=block_, in_=block_, compare_op=ALU.is_gt if strict else ALU.is_ge,
                                             fill=0.0, base=0, pattern=[[1, P]], channel_multiplier=-1)
                ins.then_inc(done, 1)

            def mask_keep(h):
                pool.wait_ge(keep_ready, h + 1)
                keep_causal(lk[h % 2], True, keep_masked)

            def mask_a(h):
                pool.wait_ge(a_ready, h + 1)
                keep_causal(aw[h % 2], True, a_masked)

            pool.wait_ge(n_done[3], 5)
            pool.wait_ge(n_done[1], 5)
            pool.memset(sel, 0.0).then_inc(sel_made, 1)
            pool.wait_ge(sel_made, 1)
            pool.affine_select(out=sel3, in_=sel3, compare_op=ALU.not_equal, fill=1.0, base=0,
                               pattern=[[-1, 4], [0, P]], channel_multiplier=1).then_inc(sel_made, 1)
            mask_keep(0)
            mask_keep(1)
            for h in range(SBH):
                mask_a(h)
                if h + 2 < SBH:
                    mask_keep(h + 2)
            for h in range(MLH):
                pool.wait_ge(w_ready, h + 1)
                keep_causal(lk[h % 2], False, w_masked)

        @block.sync
        def _(sp):
            for i in range(TT):
                sp.dma_start(xs3[:, i, :], A["x"][i * P:(i + 1) * P, :]).then_inc(x_in[i], 16)
            sp.dma_start(mems3, A["mem"].rearrange("(t p) d -> p t d", p=P)).then_inc(mem_in, 16)
            sp.dma_start(cols[:, :], A["cols"]).then_inc(params_in, 16)
            sp.dma_start(bif[:, :], A["bif"]).then_inc(params_in, 16)

            def load_t(s, use, src, k=KD):
                at_least(sp, t_done[s], use)
                sp.dma_start(wt4[:, s, 0:k, :], src).then_inc(wt_in[s], 16)

            def load_n(b, src):
                sp.dma_start(wn4[:, b, :, :], src).then_inc(wn_in[b], 16)

            for s in range(4):
                load_t(s, 0, A["w_t"][s])
            sp.dma_start(w_if, A["w_if"]).then_inc(wif_in, 16)
            load_n(0, A["w_n"][0])
            load_n(1, A["w_n"][1])
            with sp.Fori(1, PROJ_I) as i:
                for s in range(4):
                    load_t(s, i, A["w_t"][i * 4 + s])
            for n, src in enumerate((A["w_n"][2], A["w_n"][3], A["w_kv"][0], A["w_kv"][1])):
                sp.wait_ge(n_done[3], n + 1)
                load_n(n % 2, src)
            for b in range(3):
                with sp.Fori(0, 4) as i:
                    for s in range(4):
                        src = A["w_gate"] if s % 2 == 0 else A["w_br"]
                        load_t(s, i + (BR_BASE + b * 4), src[i * 2 + (b * 8 + s // 2)], KD if s % 2 == 0 else 4)
            sp.wait_ge(my_done, NH)
            sp.dma_start(xa3, A["x"].rearrange("(t p) d -> p t d", p=P)).then_inc(xa_in, 16)
            sp.wait_ge(mlT_done, MLH)
            load_n(0, A["w_out"][0])
            load_n(1, A["w_out"][1])
            with sp.Fori(0, PQ_I) as i:
                for s in range(4):
                    load_t(s, i + PQ_BASE, A["w_pq"][i * 4 + s])
            sp.wait_ge(n_done[3], 7)
            sp.dma_start(keysT3, A["keysT"]).then_inc(keys_in, 16)

            for s in range(4):
                sp.wait_ge(t_done[s], PQ_BASE + PQ_I)
            for half in range(2):
                def load_uv(j, s):
                    n = j * 2 + (half * NKEYS + s)
                    at_least(sp, u_done, n - 1)
                    sp.dma_start(ub[:, s, :, :], A["u"][j * 2 + s]).then_inc(u_in[s], 16)
                    at_least(sp, v_done, n - 1)
                    sp.dma_start(vb[:, s, :], A["v"][j * 2 + s]).then_inc(v_in[s], 16)

                for s in range(2):
                    load_uv(0, s)
                with sp.Fori(1, NKEYS // 2) as j:
                    for s in range(2):
                        load_uv(j, s)
                for t in range(2):
                    sp.wait_ge(out_ready, half * 2 + t + 1)
                    sp.dma_start(out[(half * 2 + t) * P:(half * 2 + t + 1) * P, :],
                                 h3[:, half * 2 + t, :]).then_inc(stored, 16)
            sp.wait_ge(stored, 16 * TT)

        @block.tensor
        def _(pe):
            def turn(dst, src, rows_=P):
                return pe.transpose(dst, src, ident[0:rows_, 0:rows_])

            def t_group(s, use, k, act):
                pe.wait_ge(wt_in[s], (use + 1) * 16)
                at_least(pe, t_out[s], use)
                for n in range(k):
                    ins = pe.matmul(bank(s), wt4[:, s, n, :], act[:, n, :], start=n == 0, stop=n == k - 1)
                ins.then_inc(t_done[s], 1)

            def n_group(t, use, b, act, tile):
                at_least(pe, n_out[t], use)
                for n in range(KD):
                    ins = pe.matmul(bank(4 + t), act[:, n, tile * P:(tile + 1) * P], wn4[:, b, n, :],
                                    start=n == 0, stop=n == KD - 1)
                ins.then_inc(n_done[t], 1)

            pe.wait_ge(const_set, CONSTS)
            pe.wait_ge(const_made, 4)
            pe.wait_ge(scaled, TT)
            for k in range(KD):
                for i in range(TT):
                    ins = turn(bank(k)[:, i * P:(i + 1) * P], xs3[:, i, k * P:(k + 1) * P])
                ins.then_inc(turned, 1)
            pe.wait_ge(scaled, TT + MT)
            for k in range(KD):
                pe.wait_ge(xT_out, k + 1)
                for i in range(MT):
                    ins = turn(bank(k)[:, i * P:(i + 1) * P], mems3[:, i, k * P:(k + 1) * P])
                ins.then_inc(turned, 1)
            pe.wait_ge(memT_out, KD)

            for s in range(4):
                t_group(s, 0, KD, xT3)
            with pe.Fori(1, PROJ_I) as i:
                for s in range(4):
                    t_group(s, i, KD, xT3)
            pe.wait_ge(wif_in, 16)
            for g in range(2):
                pe.wait_ge(t_out[g], PROJ_I)
                for n in range(KD):
                    ins = pe.matmul(bank(g)[0:4, :], w_if[:, n, g * 4:(g + 1) * 4], xT3[:, n, :],
                                    start=n == 0, stop=n == KD - 1)
            ins.then_inc(if_done, 1)
            for b in range(4):
                pe.wait_ge(wn_in[b % 2], 16 * (b // 2 + 1))
                for t in range(TT):
                    n_group(t, b, b % 2, xT3, t)
            for b in range(2):
                pe.wait_ge(wn_in[b], 16 * 3)
                for m in range(MT):
                    n_group(b * MT + m, 4, b, memT3, m)
            pe.wait_ge(rows_made, 1)
            pe.wait_ge(thr_made, 1)
            pe.wait_ge(t_out[2], PROJ_I)
            for i, r in enumerate((r_a, r_m)):
                for t in range(TT):
                    ins = turn(bank(2)[:, (i * TT + t) * 4:(i * TT + t) * 4 + 4], r[:, t * P:(t + 1) * P], 4)
            ins.then_inc(cols_turned, 1)
            pe.wait_ge(cols_out, 1)
            pe.wait_ge(t_out[3], PROJ_I)
            for t in range(TT):
                pe.wait_ge(n_out[t], 5)

            def causal(s, kt, q0=None):
                q0 = kt if q0 is None else q0
                at = s * 3 * BANK + CAUSAL_AT[kt] + (q0 - kt) * P
                return ps[:, at:at + T - q0 * P]

            def part(buf, kt, q0=None, q1=TT):
                q0 = kt if q0 is None else q0
                return buf[:, CAUSAL_AT[kt] + (q0 - kt) * P:CAUSAL_AT[kt] + (q1 - kt) * P]

            def sb_scores(h):
                at_least(pe, a_ready, h - 1)
                r = slice(SBD * (h % 2), SBD * (h % 2) + SBD)
                for kt in range(TT):
                    ins = pe.matmul(causal(h % 2, kt), projT3[r, 4 + h // 2, kt * P:(kt + 1) * P],
                                    projT3[r, h // 2, kt * P:T], start=kt != 3, stop=False, skip_group_check=True)
                ins.then_inc(z_ready, 1)

            def sb_suffix(h):
                pe.wait_ge(keep_masked, h + 1)
                for kt in range(TT):
                    for k2 in range(kt, TT):
                        ins = pe.matmul(causal(h % 2, kt, k2), neg_tri[:, :] if k2 == kt else neg_ones[:, :],
                                        part(lk[h % 2], k2), start=False, stop=k2 == TT - 1, skip_group_check=True)
                ins.then_inc(suffix_done, 1)

            def sb_values(h):
                pe.wait_ge(a_masked, h + 1)
                at_least(pe, y_out, h - 1)
                r = slice(SBD * (h % 2), SBD * (h % 2) + SBD)
                for kt in range(TT):
                    ins = pe.matmul(bank(6 + h % 2)[r, kt * P:T], sb_v3[:, kt, h * SBD:(h + 1) * SBD],
                                    part(aw[h % 2], kt), start=kt == 0, stop=kt == TT - 1)
                ins.then_inc(y_done, 1)

            sb_scores(0)
            sb_scores(1)
            for h in range(SBH):
                sb_suffix(h)
                if h >= 1:
                    sb_values(h - 1)
                    if h + 1 < SBH:
                        sb_scores(h + 1)
            sb_values(SBH - 1)

            pe.wait_ge(silu_done, 8)
            pe.wait_ge(sel_made, 2)
            pe.wait_ge(y_out, SBH)

            def ml_scores(h):
                at_least(pe, num_out, h - 1)
                at_least(pe, d_ready, h - 1)
                pe.matmul(bank(6 + h % 2), sel3[:, h, :], r_max, start=True, stop=True)
                for kt in range(TT):
                    ins = pe.matmul(causal(h % 2, kt), projT3[:, 12 + h, kt * P:(kt + 1) * P],
                                    projT3[:, 8 + h, kt * P:T], start=kt != 3, stop=True, skip_group_check=True)
                ins.then_inc(s_ready, 1)

            def ml_values(h):
                pe.wait_ge(w_masked, h + 1)
                for t in range(TT):
                    at = (h % 2 * 3 + t // 2) * BANK + (t % 2) * (HD + 1)
                    for kt in range(t + 1):
                        ins = pe.matmul(ps[:, at:at + HD + 1], part(lk[h % 2], kt, t, t + 1), ml_v4[:, kt, h, :],
                                        start=kt == 0, stop=kt == t)
                ins.then_inc(num_done, 1)

            ml_scores(0)
            ml_scores(1)
            for h in range(MLH):
                ml_values(h)
                if h + 2 < MLH:
                    ml_scores(h + 2)
            pe.wait_ge(num_out, MLH)
            pe.wait_ge(ml_normed, 1)
            for h in range(MLH):
                for t in range(TT):
                    ins = turn(bank(h)[:, t * P:(t + 1) * P], y_ml4[:, t, h, :])
                ins.then_inc(mlT_done, 1)

            pe.wait_ge(qk_normed, 1)
            for h in range(NH):
                pe.wait_ge(mlT_out, h + 1)
                for t in range(TT):
                    ins = turn(bank(h)[:, t * P:(t + 1) * P], mem_q3[:, t, h * HD:(h + 1) * HD])
                ins.then_inc(qkT_done, 1)
            for h in range(NH):
                for t in range(MT):
                    ins = turn(bank(4 + h // 2)[:, (h % 2 * MT + t) * P:(h % 2 * MT + t + 1) * P],
                               mem_k3[:, t, h * HD:(h + 1) * HD])
            ins.then_inc(qkT_done, 1)
            pe.wait_ge(qkT_out, NH + 1)

            def mem_scores(h):
                at_least(pe, mexp_ready, h - 1)
                for t in range(TT):
                    at = (h % 2) * 2 * BANK + t * MEM
                    ins = pe.matmul(ps[:, at:at + MEM], mem_qT3[:, h, t * P:(t + 1) * P], mem_kT3[:, h, :],
                                    start=True, stop=True)
                ins.then_inc(ms_ready, 1)

            mem_scores(0)
            for h in range(NH):
                if h + 1 < NH:
                    mem_scores(h + 1)
                pe.wait_ge(mp_ready, h + 1)
                at_least(pe, mpT_out, h)
                for m in range(MT):
                    for t in range(TT):
                        ins = turn(bank(4 + m)[:, t * P:(t + 1) * P],
                                   probs[h % 2][:, t * MEM + m * P:t * MEM + (m + 1) * P])
                ins.then_inc(mpT_done, 1)
                pe.wait_ge(mpT_out, h + 1)
                at_least(pe, my_out, h - 1)
                for m in range(MT):
                    ins = pe.matmul(bank(6 + h % 2), mem_v3[:, m, h * HD:(h + 1) * HD], probsT[:, h % 2, m, :],
                                    start=m == 0, stop=m == MT - 1)
                ins.then_inc(my_done, 1)
            pe.wait_ge(my_out, NH)

            for b in range(3):
                with pe.Fori(0, 4) as i:
                    for s in range(4):
                        t_group(s, i + (BR_BASE + b * 4), KD if s % 2 == 0 else 4, xT3 if s % 2 == 0 else yT[b])
            for s in range(2):
                pe.wait_ge(gated[s], BR_I)
            for b in range(2):
                pe.wait_ge(wn_in[b], 16 * 4)
                for t in range(TT):
                    n_group(t, 5 + b, b, mergedT3, t)

            pe.wait_ge(h_normed, 1)
            for s in range(4):
                pe.wait_ge(t_out[s], BR_BASE + BR_I)
            for k in range(KD):
                for i in range(TT):
                    ins = turn(bank(k)[:, i * P:(i + 1) * P], hs3[:, i, k * P:(k + 1) * P])
                ins.then_inc(hT_done, 1)
            pe.wait_ge(hT_out, KD)
            with pe.Fori(0, PQ_I) as i:
                for s in range(4):
                    t_group(s, i + PQ_BASE, KD, hT3)
            pe.wait_ge(keys_in, 16)
            for s in range(4):
                pe.wait_ge(t_out[s], PQ_BASE + PQ_I)
            for t in range(TT):
                at_least(pe, score_out, t)
                for g in range(2 * PH):
                    ins = pe.matmul(ps[:, 4 * BANK + g * NKEYS:4 * BANK + (g + 1) * NKEYS],
                                    qryT3[:, g, t * P:(t + 1) * P], keysT3[:, g, :], start=True, stop=True)
                ins.then_inc(score_done, 1)
            for t in range(TT):
                pe.wait_ge(list_ready, t + 1)
                at_least(pe, list_out, t)
                for n in range(3):
                    ins = turn(bank(0)[:, n * P:(n + 1) * P], lists[:, n, :])
                ins.then_inc(list_turned, 1)
            pe.wait_ge(list_out, TT)
            pe.wait_ge(score_out, TT)

            for half in range(2):
                def gate_group(j, s):
                    n = j * 2 + (half * HALF // 4 + s)
                    pe.wait_ge(oh_ready, n + 1)
                    at_least(pe, gate_out, n - 1)
                    for q in range(4):
                        for w in range(2):
                            ins = pe.matmul(bank(2 + s)[:, q * P:(q + 1) * P], oh[:, s, q, 0, :],
                                            oh[:, s, q, 1 + w, :], start=w == 0, stop=w == 1)
                    ins.then_inc(gate_done, 1)

                for s in range(2):
                    gate_group(0, s)
                with pe.Fori(1, HALF // 8) as j:
                    for s in range(2):
                        gate_group(j, s)
                at_least(pe, out_ready, half * 2)
                for b in range(4):
                    pe.matmul(bank(4 + b), zero_bf[:, :], iota_key[:, :].unsqueeze(1).broadcast_to([P, 4, P]), start=True, stop=False,
                              skip_group_check=True)

                def up(j, s):
                    n = j * 2 + (half * NKEYS + s)
                    pe.wait_ge(u_in[s], (j + (half * NKEYS // 2 + 1)) * 16)
                    at_least(pe, gelu_done, n - 1)
                    for k in range(KD):
                        ins = pe.matmul(bank(s)[:, 0:HALF], ub[:, s, k, :], hT3[:, k, half * HALF:(half + 1) * HALF],
                                        start=k == 0, stop=k == KD - 1)
                    ins.then_inc(u_done, 1)

                def down(j, s, stop=False):
                    n = j * 2 + (half * NKEYS + s)
                    pe.wait_ge(v_in[s], (j + (half * NKEYS // 2 + 1)) * 16)
                    pe.wait_ge(gated_act, n + 1)
                    for t in range(2):
                        for c in range(2):
                            ins = pe.matmul(bank(4 + 2 * t + c), gw[:, s, t * P:(t + 1) * P],
                                            vb[:, s, c * BANK:(c + 1) * BANK], start=False, stop=stop,
                                            skip_group_check=True)
                    ins.then_inc(v_done, 1)

                up(0, 0)
                up(0, 1)
                down(0, 0)
                with pe.Fori(1, NKEYS // 2) as j:
                    up(j, 0)
                    down(j - 1, 1)
                    up(j, 1)
                    down(j, 0)
                down(NKEYS // 2 - 1, 1, stop=True)

        @block.scalar
        def _(act):
            steps = [0]

            def link(ins):
                steps[0] += 1
                ins.then_inc(act_step, 1)
                act.wait_ge(act_step, steps[0])

            act.wait_ge(const_set, CONSTS)
            for i in range(TT):
                act.wait_ge(x_in[i], 16)
                link(act.activation(junk, xs3[:, i, :], ACT.Square, accum_out=sums[:, i:i + 1]))
            act.wait_ge(mem_in, 16)
            for i in range(MT):
                link(act.activation(junk, mems3[:, i, :], ACT.Square, accum_out=sums[:, TT + i:TT + i + 1]))
            act.activation(roots[:, S_X:S_Q], sums[:, S_X:S_Q], ACT.Sqrt, bias=eps_col[:, :],
                           scale=1.0 / D).then_inc(rooted, 1)
            act.wait_ge(params_in, 32)
            for k in range(KD):
                act.wait_ge(turned, k + 1)
                act.activation(xT3[:, k, :], bank(k), ACT.Copy,
                               scale=cols[:, C_MIX + k:C_MIX + k + 1]).then_inc(xT_out, 1)
            for s in range(4):
                act.wait_ge(t_done[s], 1)
                act.activation(projT3[:, s, :], bank(s), ACT.Copy, scale=SBD ** -0.5).then_inc(t_out[s], 1)
            with act.Fori(1, PROJ_I) as i:
                for s in range(4):
                    act.wait_ge(t_done[s], i + 1)
                    act.activation(projT[:, bass.ds((i * 4 + s) * T, T)], bank(s), ACT.Copy).then_inc(t_out[s], 1)
            act.wait_ge(if_done, 1)
            link(act.activation(r_abs, bank(1)[0:4, :], ACT.Abs, bias=bif[:, 1:2]))
            link(act.activation(r_abs, r_abs, ACT.Exp, scale=-1.0))
            act.activation(r_abs, r_abs, ACT.Ln, bias=1.0).then_inc(if_ln, 1)
            for g in range(8):
                act.wait_ge(conv_done, g + 1)
                act.activation(projT3[:, 8 + g, :], conv_out[:, g % 2, :], ACT.Silu).then_inc(silu_done, 1)
            for t in range(TT):
                act.wait_ge(n_out[t], 3)
            act.activation(ml_o, ml_o, ACT.Sigmoid).then_inc(sig_o, 1)
            act.wait_ge(rows_made, 1)
            act.activation(r_m, r_m, ACT.Exp, scale=-1.0).then_inc(thr_made, 1)
            act.wait_ge(qk_squared, 1)
            act.activation(roots[:, S_Q:S_ML], sums[:, S_Q:S_ML], ACT.Sqrt, bias=eps_col[:, :],
                           scale=1.0 / HD).then_inc(qk_rooted, 1)

            def region(s):
                return ps[:, s * 3 * BANK:s * 3 * BANK + CAUSAL]

            def ln_part(h):
                act.wait_ge(z_ready, h + 1)
                at_least(act, suffix_done, h - 1)
                link(act.activation(lk[h % 2], region(h % 2), ACT.Abs))
                link(act.activation(lk[h % 2], lk[h % 2], ACT.Exp, scale=-1.0))
                act.activation(lk[h % 2], lk[h % 2], ACT.Ln, bias=1.0).then_inc(ln_ready, 1)

            ln_part(0)
            ln_part(1)
            for h in range(SBH):
                act.wait_ge(suffix_done, h + 1)
                at_least(act, y_done, h - 1)
                act.activation(aw[h % 2], region(h % 2), ACT.Exp).then_inc(a_ready, 1)
                if h + 2 < SBH:
                    ln_part(h + 2)

            for h in range(MLH):
                act.wait_ge(d_ready, h + 1)
                act.activation(lk[h % 2], lk[h % 2], ACT.Exp, scale=-1.0).then_inc(e_ready, 1)
            act.wait_ge(ml_squared, 1)
            act.activation(roots[:, S_ML:S_H], sums[:, S_ML:S_H], ACT.Sqrt, bias=eps_col[:, :],
                           scale=1.0 / HD).then_inc(ml_rooted, 1)
            for h in range(MLH):
                act.wait_ge(mlT_done, h + 1)
                act.activation(yT[1][:, h, :], bank(h), ACT.Copy, scale=cols[:, C_MLG:C_MLG + 1]).then_inc(mlT_out, 1)
            act.wait_ge(qk_normed, 1)
            for h in range(NH):
                act.wait_ge(qkT_done, h + 1)
                act.activation(mem_qT3[:, h, :], bank(h), ACT.Copy, scale=qg_scaled[:, 0:1]).then_inc(qkT_out, 1)
            act.wait_ge(qkT_done, NH + 1)
            act.activation(mem_kT, bank(4, 2), ACT.Copy, scale=cols[:, C_KG:C_KG + 1]).then_inc(qkT_out, 1)
            for h in range(NH):
                act.wait_ge(mmax_ready, h + 1)
                at_least(act, mpT_done, h - 1)
                for t in range(TT):
                    at = (h % 2) * 2 * BANK + t * MEM
                    d = 8 + (h % 2) * 4 + t
                    ins = act.activation(probs[h % 2][:, t * MEM:(t + 1) * MEM], ps[:, at:at + MEM], ACT.Exp,
                                         bias=den[:, (h % 2) * 4 + t:(h % 2) * 4 + t + 1], accum_out=den[:, d:d + 1])
                ins.then_inc(mexp_ready, 1)
                act.wait_ge(mpT_done, h + 1)
                at_least(act, my_done, h - 1)
                act.activation(probsT[:, h % 2, :, :], bank(4, 2).rearrange("p (m t) -> p m t", t=T),
                               ACT.Copy).then_inc(mpT_out, 1)

            def branch_gates(b, i):
                for s in (0, 2):
                    act.wait_ge(t_done[s], i + (BR_BASE + b * 4 + 1))
                    at_least(act, gated[s // 2], i + b * 4)
                    act.activation(gate_s3[:, s // 2, :], bank(s), ACT.Sigmoid,
                                   bias=cols[:, bass.ds(i * 2 + (C_BGATE + b * 8 + s // 2), 1)]).then_inc(t_out[s], 1)

            branch_gates(0, 0)
            for b in range(3):
                with act.Fori(1 if b == 0 else 0, 4) as i:
                    branch_gates(b, i)

            for t in range(TT):
                act.wait_ge(n_out[t], 7)
                link(act.activation(junk, h3[:, t, :], ACT.Square, accum_out=sums[:, S_H + t:S_H + t + 1]))
            act.activation(roots[:, S_H:S_H + TT], sums[:, S_H:S_H + TT], ACT.Sqrt, bias=eps_col[:, :],
                           scale=1.0 / D).then_inc(h_rooted, 1)
            for k in range(KD):
                act.wait_ge(hT_done, k + 1)
                act.activation(hT3[:, k, :], bank(k), ACT.Copy,
                               scale=cols[:, C_FFN + k:C_FFN + k + 1]).then_inc(hT_out, 1)
            with act.Fori(0, PQ_I) as i:
                for s in range(4):
                    act.wait_ge(t_done[s], i + (PQ_BASE + 1))
                    act.activation(qryT[:, bass.ds((i * 4 + s) * T, T)], bank(s), ACT.Copy).then_inc(t_out[s], 1)
            for t in range(2):
                act.wait_ge(score_done, t + 1)
                act.activation(sc3[:, t % 2, :], bank(4, 4), ACT.Copy).then_inc(score_out, 1)
            for t in range(TT):
                act.wait_ge(cand_top, t + 1)
                act.activation(g_exp, g_exp, ACT.Exp).then_inc(cand_exp, 1)
                if t + 2 < TT:
                    act.wait_ge(score_done, t + 3)
                    act.wait_ge(score_used, t + 1)
                    act.activation(sc3[:, t % 2, :], bank(4, 4), ACT.Copy).then_inc(score_out, 1)

            for half in range(2):
                at_least(act, gated_act, half * NKEYS)

                def gate_copy(j, s):
                    act.wait_ge(gate_done, j * 2 + (half * HALF // 4 + s + 1))
                    act.activation(G_tokens(j * 8 + s * 4), bank(2 + s).rearrange("p (q k) -> p k q", k=NKEYS),
                                   ACT.Copy).then_inc(gate_out, 1)

                def G_tokens(t0):
                    return Gk[:, :, bass.ds(t0, 4)]

                with act.Fori(0, HALF // 8) as j:
                    for s in range(2):
                        gate_copy(j, s)

                def gelu(j, s):
                    n = j * 2 + (half * NKEYS + s)
                    act.wait_ge(u_done, n + 1)
                    at_least(act, gated_act, n - 1)
                    act.activation(ga[:, s, :], bank(s)[:, 0:HALF], ACT.Gelu).then_inc(gelu_done, 1)

                for s in range(2):
                    gelu(0, s)
                with act.Fori(1, NKEYS // 2) as j:
                    for s in range(2):
                        gelu(j, s)

        @block.vector
        def _(dve):
            steps = [0]

            def link(ins):
                steps[0] += 1
                ins.then_inc(dve_step, 1)
                dve.wait_ge(dve_step, steps[0])

            dve.wait_ge(rooted, 1)
            link(dve.reciprocal(rstd[:, S_X:S_Q], roots[:, S_X:S_Q]))
            for i in range(TT):
                dve.tensor_scalar(xs3[:, i, :], xs3[:, i, :], rstd[:, i:i + 1], None, ALU.mult).then_inc(scaled, 1)
            for i in range(MT):
                dve.tensor_scalar(mems3[:, i, :], mems3[:, i, :], rstd[:, TT + i:TT + i + 1], None,
                                  ALU.mult).then_inc(scaled, 1)
            dve.wait_ge(params_in, 32)
            dve.tensor_scalar(qg_scaled[:, :], cols[:, C_QG:C_QG + 1], HD_SCALE, None, ALU.mult).then_inc(q_scaled, 1)
            for k in range(KD):
                dve.wait_ge(turned, KD + k + 1)
                dve.tensor_scalar(memT3[:, k, :], bank(k)[:, 0:MEM], cols[:, C_MEM + k:C_MEM + k + 1], None,
                                  ALU.mult).then_inc(memT_out, 1)

            def conv(g):
                dve.wait_ge(t_out[g % 4], (8 + g) // 4 + 1)
                at_least(dve, silu_done, g - 1)
                x_, y_ = projT3[:, 8 + g, :], conv_out[:, g % 2, :]
                w = [cols[:, C_CONVW + g * 4 + k:C_CONVW + g * 4 + k + 1] for k in range(4)]
                link(dve.tensor_scalar(y_, x_, w[3], cols[:, C_CONVB + g:C_CONVB + g + 1], ALU.mult, ALU.add))
                for k in range(3):
                    lag = 3 - k
                    ins = dve.scalar_tensor_tensor(out=y_[:, lag:T], in0=x_[:, 0:T - lag], scalar=w[k],
                                                   in1=y_[:, lag:T], op0=ALU.mult, op1=ALU.add)
                    if k < 2:
                        link(ins)
                ins.then_inc(conv_done, 1)

            natural = [sb_v3, None, ml_o3, mem_q3]
            for b in range(4):
                for t in range(TT):
                    dve.wait_ge(n_done[t], b + 1)
                    if b == 1:
                        ins = dve.tensor_copy(ml_v4[:, t, :, 0:HD], bank(4 + t).rearrange("p (h c) -> p h c", c=HD))
                    else:
                        ins = dve.tensor_copy(natural[b][:, t, :], bank(4 + t))
                    ins.then_inc(n_out[t], 1)
                conv(2 * b)
                conv(2 * b + 1)
            dve.wait_ge(if_ln, 1)
            dve.memset(r_zero, 0.0)
            link(dve.tensor_scalar(r_f, bank(1)[0:4, :], bif[:, 1:2], 0.0, ALU.add, ALU.min))
            link(dve.tensor_tensor(r_lf, r_f, r_abs, ALU.subtract))
            link(dve.tensor_tensor_scan(r_b, r_lf, r_zero, 0.0, ALU.add, ALU.add))
            link(dve.scalar_tensor_tensor(out=r_a, in0=bank(0)[0:4, :], scalar=bif[:, 0:1], in1=r_b,
                                          op0=ALU.add, op1=ALU.subtract))
            link(dve.tensor_tensor_scan(r_max, r_a, r_a, 0.0, ALU.max, ALU.max))
            dve.tensor_tensor(r_m, r_b, r_max, ALU.add).then_inc(rows_made, 1)
            for t in range(TT):
                dve.wait_ge(n_done[t], 5)
                dst = mem_k3 if t < MT else mem_v3
                dve.tensor_copy(dst[:, t % MT, :], bank(4 + t)).then_inc(n_out[t], 1)
            dve.wait_ge(n_out[3], 5)
            dve.tensor_tensor(qk_squares[:, 0:2048], mem_q, mem_q, ALU.mult)
            link(dve.tensor_tensor(qk_squares[:, 2048:3072], mem_k, mem_k, ALU.mult))
            dve.tensor_reduce(sums[:, S_Q:S_ML], qk_squares.rearrange("p (g c) -> p g c", c=HD), AX.X,
                              ALU.add).then_inc(qk_squared, 1)
            dve.wait_ge(qk_rooted, 1)
            link(dve.reciprocal(rstd[:, S_Q:S_ML], roots[:, S_Q:S_ML]))

            def spread(col, n, m):
                return col.unsqueeze(2).broadcast_to([P, n, m])

            q_ = mem_q.rearrange("p (g c) -> p g c", c=HD)
            k_ = mem_k.rearrange("p (g c) -> p g c", c=HD)
            dve.tensor_tensor(q_, q_, spread(rstd[:, S_Q:S_K], 16, HD), ALU.mult)
            dve.tensor_tensor(k_, k_, spread(rstd[:, S_K:S_ML], 8, HD), ALU.mult).then_inc(qk_normed, 1)
            dve.wait_ge(cols_turned, 1)
            dve.tensor_copy(key_cols[:, :], bank(2)[:, 0:32]).then_inc(cols_out, 1)

            def region(s):
                return ps[:, s * 3 * BANK:s * 3 * BANK + CAUSAL]

            def keep(h):
                dve.wait_ge(ln_ready, h + 1)
                dve.scalar_tensor_tensor(out=lk[h % 2], in0=region(h % 2), scalar=0.0, in1=lk[h % 2],
                                         op0=ALU.max, op1=ALU.add).then_inc(keep_ready, 1)

            keep(0)
            keep(1)
            for h in range(SBH):
                r = slice(SBD * (h % 2), SBD * (h % 2) + SBD)
                dve.wait_ge(y_done, h + 1)
                dve.tensor_copy(yT[0][r, h // 2, :], bank(6 + h % 2)[r, :]).then_inc(y_out, 1)
                if h + 2 < SBH:
                    keep(h + 2)

            def decay(h):
                dve.wait_ge(s_ready, h + 1)
                at_least(dve, num_done, h - 1)
                for kt in range(TT):
                    ins = dve.tensor_scalar(lk[h % 2][:, CAUSAL_AT[kt]:CAUSAL_AT[kt] + T - kt * P],
                                            bank(6 + h % 2)[:, kt * P:T],
                                            key_cols[:, kt * 4 + h:kt * 4 + h + 1], 0.0, ALU.subtract, ALU.max)
                ins.then_inc(d_ready, 1)

            def weigh(h):
                dve.wait_ge(e_ready, h + 1)
                dve.scalar_tensor_tensor(out=lk[h % 2], in0=region(h % 2), scalar=HD_SCALE, in1=lk[h % 2],
                                         op0=ALU.mult, op1=ALU.mult).then_inc(w_ready, 1)

            def divide(h):
                dve.wait_ge(num_done, h + 1)
                base = h % 2 * 3 * BANK
                d_ = ps[:, base:base + 2 * BANK].rearrange("p (a b) -> p a b", b=BANK)[:, :, HD:2 * HD + 2:HD + 1]
                m_ = key_cols[:, 16 + h:32:4].rearrange("p (a b) -> p a b", b=2)
                o_ = den[:, 0:4].rearrange("p (a b) -> p a b", b=2)
                link(dve.scalar_tensor_tensor(out=o_, in0=d_, scalar=-1.0, in1=m_, op0=ALU.mult, op1=ALU.max))
                link(dve.tensor_tensor(o_, o_, d_, ALU.max))
                link(dve.reciprocal(den[:, 4:8], den[:, 0:4]))
                for t in range(TT):
                    at = (h % 2 * 3 + t // 2) * BANK + (t % 2) * (HD + 1)
                    ins = dve.tensor_scalar(y_ml4[:, t, h, :], ps[:, at:at + HD], den[:, 4 + t:5 + t], None, ALU.mult)
                ins.then_inc(num_out, 1)

            decay(0)
            weigh(0)
            decay(1)
            weigh(1)
            for h in range(MLH):
                divide(h)
                if h + 2 < MLH:
                    decay(h + 2)
                    weigh(h + 2)
            dve.wait_ge(num_out, MLH)
            link(dve.tensor_tensor(squares, y_ml, y_ml, ALU.mult))
            dve.tensor_reduce(sums[:, S_ML:S_H], squares.rearrange("p (g c) -> p g c", c=HD), AX.X,
                              ALU.add).then_inc(ml_squared, 1)
            dve.wait_ge(ml_rooted, 1)
            link(dve.reciprocal(rstd[:, S_ML:S_H], roots[:, S_ML:S_H]))
            y_ = y_ml.rearrange("p (g c) -> p g c", c=HD)
            link(dve.tensor_tensor(y_, y_, spread(rstd[:, S_ML:S_H], 16, HD), ALU.mult))
            dve.wait_ge(sig_o, 1)
            dve.tensor_tensor(y_ml, y_ml, ml_o, ALU.mult).then_inc(ml_normed, 1)

            for h in range(NH):
                n4 = (h % 2) * 4
                dve.wait_ge(ms_ready, h + 1)
                dve.tensor_reduce(den[:, n4:n4 + 4], ps[:, (h % 2) * 2 * BANK:(h % 2 + 1) * 2 * BANK].rearrange(
                    "p (t m) -> p t m", m=MEM), AX.X, ALU.max, negate=True).then_inc(mmax_ready, 1)
                dve.wait_ge(mexp_ready, h + 1)
                link(dve.reciprocal(den[:, 16 + n4:20 + n4], den[:, 8 + n4:12 + n4]))
                p_ = probs[h % 2].rearrange("p (t m) -> p t m", m=MEM)
                dve.tensor_tensor(p_, p_, spread(den[:, 16 + n4:20 + n4], 4, MEM), ALU.mult).then_inc(mp_ready, 1)
                dve.wait_ge(my_done, h + 1)
                dve.tensor_copy(yT[2][:, h, :], bank(6 + h % 2)).then_inc(my_out, 1)

            for b in range(3):
                with dve.Fori(0, 4) as i:
                    for s in (1, 3):
                        use = i + (BR_BASE + b * 4)
                        g_ = gate_s3[:, s // 2, :]
                        m_ = mergedT[:, bass.ds((i * 2 + s // 2) * T, T)]
                        dve.wait_ge(t_done[s], use + 1)
                        dve.wait_ge(t_out[s - 1], use + 1)
                        dve.tensor_tensor(g_, bank(s), g_, ALU.mult).then_inc(t_out[s], 1)
                        dve.wait_ge(t_out[s], use + 1)
                        if b == 0:
                            dve.tensor_copy(m_, g_).then_inc(gated[s // 2], 1)
                        else:
                            dve.tensor_tensor(m_, m_, g_, ALU.add).then_inc(gated[s // 2], 1)
            dve.wait_ge(xa_in, 16)
            for b in range(2):
                for t in range(TT):
                    dve.wait_ge(n_done[t], 6 + b)
                    c_ = slice(b * BANK, (b + 1) * BANK)
                    dve.tensor_tensor(h3[:, t, c_], bank(4 + t), xa3[:, t, c_], ALU.add).then_inc(n_out[t], 1)
            dve.wait_ge(h_rooted, 1)
            link(dve.reciprocal(rstd[:, S_H:S_H + TT], roots[:, S_H:S_H + TT]))
            for t in range(TT):
                ins = dve.tensor_scalar(hs3[:, t, :], h3[:, t, :], rstd[:, S_H + t:S_H + t + 1], None, ALU.mult)
            ins.then_inc(h_normed, 1)

            def top16(n, width, src, src2, vals, idx):
                def at(x, g):
                    return x[:, g * width:(g + 1) * width]
                for g in range(n):
                    ins = dve.max(vals[:, g * 16:g * 16 + 8], at(src, g))
                link(ins)
                for g in range(n):
                    dve.max_index(idx[:, g * 16:g * 16 + 8], vals[:, g * 16:g * 16 + 8], at(src, g))
                    ins = dve.match_replace(at(src2, g), vals[:, g * 16:g * 16 + 8], at(src, g), NEG)
                link(ins)
                for g in range(n):
                    ins = dve.max(vals[:, g * 16 + 8:g * 16 + 16], at(src2, g))
                link(ins)
                for g in range(n):
                    ins = dve.max_index(idx[:, g * 16 + 8:g * 16 + 16], vals[:, g * 16 + 8:g * 16 + 16], at(src2, g))
                return ins

            for t in range(TT):
                dve.wait_ge(score_out, t + 1)
                link(top16(2 * PH, NKEYS, sc3[:, t % 2, :], top_in, top_v, top_i))
                dve.tensor_copy(top_if, top_i).then_inc(score_used, 1)
                v_ = top_v.rearrange("p (h s i) -> p h s i", s=2, i=TOPK)
                link(dve.tensor_tensor(cand.rearrange("p (h i j) -> p h i j", i=TOPK, j=TOPK),
                                       v_[:, :, 0, :].unsqueeze(3).broadcast_to([P, PH, TOPK, TOPK]),
                                       v_[:, :, 1, :].unsqueeze(2).broadcast_to([P, PH, TOPK, TOPK]), ALU.add))
                link(top16(PH, TOPK * TOPK, cand, cand2, best_v, best_c))
                at_least(dve, list_turned, t)
                b_ = best_v.rearrange("p (h r) -> p h r", r=TOPK)
                dve.tensor_tensor(g_exp.rearrange("p (h r) -> p h r", r=TOPK), b_,
                                  b_[:, :, 0:1].broadcast_to([P, PH, TOPK]), ALU.subtract).then_inc(cand_top, 1)
                dve.tensor_scalar(best_i, best_c, 4, None, ALU.logical_shift_right)
                link(dve.tensor_scalar(best_j, best_c, 15, None, ALU.bitwise_and))
                dve.tensor_copy(best_if, best_i)
                link(dve.tensor_copy(best_jf, best_j))
                i_ = top_if.rearrange("p (h s i) -> p h s i", s=2, i=TOPK)
                for n, place_ in enumerate((best_if, best_jf)):
                    pk = pick.rearrange("p (h r i) -> p h r i", r=TOPK, i=TOPK)
                    link(dve.tensor_tensor(pick.rearrange("p (q i) -> p q i", i=TOPK), spread(place_, P, TOPK),
                                           iota_top[:, :].unsqueeze(1).broadcast_to([P, P, TOPK]), ALU.is_equal))
                    link(dve.tensor_tensor(pk, pk, i_[:, :, n, :].unsqueeze(2).broadcast_to([P, PH, TOPK, TOPK]),
                                           ALU.mult))
                    link(dve.tensor_reduce(lists[:, n, :], pick.rearrange("p (q i) -> p q i", i=TOPK), AX.X, ALU.add))
                dve.wait_ge(cand_exp, t + 1)
                e_ = g_exp.rearrange("p (h r) -> p h r", r=TOPK)
                link(dve.tensor_reduce(g_sum, e_, AX.X, ALU.add))
                link(dve.reciprocal(g_rec, g_sum))
                dve.tensor_tensor(lists[:, 2, :].rearrange("p (h r) -> p h r", r=TOPK), e_, spread(g_rec, PH, TOPK),
                                  ALU.mult).then_inc(list_ready, 1)
                dve.wait_ge(list_turned, t + 1)
                dve.tensor_copy(eT3[:, :, t * P:(t + 1) * P], bank(0)[:, 0:3 * P].rearrange("p (n t) -> p n t", t=P)
                                ).then_inc(list_out, 1)
            dve.wait_ge(list_out, TT)
            gb = act_g.bitcast(BF16)[:, 0:T]
            link(dve.tensor_copy(gb, eT3[:, 2, :]))
            link(dve.tensor_copy(gate_hi[:, :], gb))
            link(dve.tensor_tensor(gate_lo[:, :], eT3[:, 2, :], gate_hi[:, :], ALU.subtract))

            for half in range(2):
                def one_hots(j, s):
                    n = j * 2 + (half * HALF // 4 + s)
                    at_least(dve, gate_done, n - 1)
                    for q in range(4):
                        t = j * 8 + (half * HALF + s * 4 + q)
                        dve.tensor_scalar(oh[:, s, q, 0, :], iota_key[:, :], eT[:, bass.ds(t, 1)], None, ALU.is_equal)
                        dve.tensor_scalar(oh[:, s, q, 1, :], iota_key[:, :], eT[:, bass.ds(t + T, 1)],
                                          gate_hi[:, bass.ds(t, 1)], ALU.is_equal, ALU.mult)
                        ins = dve.tensor_scalar(oh[:, s, q, 2, :], iota_key[:, :], eT[:, bass.ds(t + T, 1)],
                                                gate_lo[:, bass.ds(t, 1)], ALU.is_equal, ALU.mult)
                    ins.then_inc(oh_ready, 1)

                for s in range(2):
                    one_hots(0, s)
                with dve.Fori(1, HALF // 8) as j:
                    for s in range(2):
                        one_hots(j, s)

                dve.wait_ge(gate_out, (half + 1) * HALF // 4)

                def gate_act(j, s):
                    n = j * 2 + (half * NKEYS + s)
                    dve.wait_ge(gelu_done, n + 1)
                    at_least(dve, v_done, n - 1)
                    dve.tensor_tensor(gw[:, s, :], ga[:, s, :], G[:, bass.ds((j * 2 + s) * HALF, HALF)],
                                      ALU.mult).then_inc(gated_act, 1)

                for s in range(2):
                    gate_act(0, s)
                with dve.Fori(1, NKEYS // 2) as j:
                    for s in range(2):
                        gate_act(j, s)
                dve.wait_ge(v_done, (half + 1) * NKEYS)
                for t in range(2):
                    h_ = h3[:, half * 2 + t, :]
                    dve.tensor_tensor(h_, bank(4 + 2 * t, 2), h_, ALU.add).then_inc(out_ready, 1)


def layouts(I):
    def f(n):
        return np.asarray(I[n])

    def cols(v):
        return v.reshape(-1, P).T

    def t_blocks(w):
        k, g = w.shape[0] // P, w.shape[1] // P
        return w.reshape(k, P, g, P).transpose(2, 1, 0, 3)

    def n_blocks(w):
        k, b = w.shape[0] // P, w.shape[1] // BANK
        return w.reshape(k, P, b, BANK).transpose(2, 1, 0, 3)

    w = f("w_in")[0]
    parts = np.split(w, np.cumsum([512] * 6 + [MLH, MLH, 512, 512]), axis=1)
    sq, sk, sv, mq, mk, mv, wi, wf, mo, eq, wg = parts
    conv_w = f("conv_w")[0].reshape(4, 8, P).transpose(2, 1, 0).reshape(P, 32)
    par = [cols(f("g_mix")[0]), cols(f("mem_norm_g")[0]), cols(f("g_ffn")[0]), cols(f("b_gate")[0]), conv_w,
           cols(f("conv_b")[0]), cols(f("ml_norm_g")[0]), cols(f("q_norm_g")[0]), cols(f("k_norm_g")[0])]
    keys = np.stack([f("peer_k1")[0], f("peer_k2")[0]], axis=1)
    L = {
        "x": f("x")[0], "mem": f("mem")[0], "cols": np.concatenate(par, axis=1),
        "bif": np.stack([f("b_igate")[0], f("b_fgate")[0]], axis=1),
        "w_t": t_blocks(np.concatenate([sq, sk, mq, mk], axis=1)),
        "w_n": n_blocks(np.concatenate([sv, mv, mo, eq], axis=1)),
        "w_if": np.concatenate([wi, wf], axis=1).reshape(KD, P, 8).transpose(1, 0, 2),
        "w_kv": n_blocks(f("w_mem_kv")[0]),
        "w_gate": t_blocks(wg),
        "w_br": np.concatenate([t_blocks(f(n)[0]) for n in ("w_sb_o", "w_ml_o", "w_mem_o")]),
        "w_out": n_blocks(f("w_out")[0]),
        "w_pq": t_blocks(f("w_peer_q")[0]),
        "keysT": keys.transpose(3, 0, 1, 2).reshape(P, 2 * PH, NKEYS),
        "u": f("peer_u")[0].reshape(NKEYS, NKEYS, KD, P).transpose(1, 3, 2, 0),
        "v": f("peer_v")[0].reshape(NKEYS, NKEYS, D).transpose(1, 0, 2),
    }
    return {n: np.ascontiguousarray(a) for n, a in L.items()}


def kernel(**inputs):
    import concourse.bacc as bacc
    from concourse.bass_utils import run_bass_kernel_spmd

    nc = bacc.Bacc("TRN2", target_bir_lowering=False, num_devices=1)
    arrays = layouts(inputs)
    aps = {n: nc.dram_tensor(f"in_{n}", a.shape, mybir.dt.from_np(a.dtype), kind="ExternalInput").ap()
           for n, a in arrays.items()}
    out = nc.dram_tensor("out_h", (T, D), F32, kind="ExternalOutput").ap()
    build(nc, aps, out)
    r = run_bass_kernel_spmd(nc, [{f"in_{n}": a for n, a in arrays.items()}], core_ids=[0])
    return r.results[0]["out_h"].reshape(1, T, D)
```

```python
from contextlib import ExitStack

import concourse.bass as bass
import numpy as np
from concourse import mybir

F32 = mybir.dt.float32
BF16 = mybir.dt.bfloat16
U32 = mybir.dt.uint32
ALU = mybir.AluOpType
ACT = mybir.ActivationFunctionType
AX = mybir.AxisListType

P = 128
T = 512
TT = T // P
D = 1024
KD = D // P
MEM = 256
MT = MEM // P
SBH, SBD = 8, 64
MLH = 4
NH = 4
HD = 128
BANK = 512
CAUSAL_AT = [0, 512, 1024, 896]
CAUSAL = 1280
EPS = 1e-6
HD_SCALE = HD ** -0.5
PH = 8
TOPK = 16
NKEYS = 128
NEG = -3.0e38
GT = 8
BLK = 64
NBLK = T // BLK
CH = 4
NCH = NKEYS // CH
AHEAD = 8
NPRE = AHEAD * CH

C_MIX, C_MEM, C_FFN, C_BGATE, C_CONVW, C_CONVB, C_MLG, C_QG, C_KG, NCOLS = 0, 8, 16, 24, 48, 80, 88, 89, 90, 91


def at_least(eng, sem, value):
    if isinstance(value, int) and value <= 0:
        return
    eng.wait_ge(sem, value)


def build(nc, A, out, gates_dram):
    ctx = ExitStack()
    with ctx:
        def sb(name, cols, dt=F32, rows=P):
            return ctx.enter_context(nc.sbuf_tensor(name, [rows, cols], dt))

        def sem(name):
            return ctx.enter_context(nc.semaphore(name))

        ident = sb("ident", P)
        neg_tri = sb("neg_tri", P)
        neg_ones = sb("neg_ones", P)
        iota_top = sb("iota_top", TOPK)
        eps_col = sb("eps_col", 1)
        cols = sb("cols", NCOLS)
        qg_scaled = sb("qg_scaled", 1)
        bif = sb("bif", 2, rows=4)
        sums = sb("sums", 64)
        roots = sb("roots", 64)
        rstd = sb("rstd", 64)
        key_cols = sb("key_cols", 32)
        thr_cols = sb("thr_cols", 16)
        den = sb("den", 32)

        STORE = 52240
        store = sb("store", STORE)
        place = {}

        def carve(name, at, size):
            assert at + size <= STORE, (name, at + size)
            place[name] = store[:, at:at + size]
            return place[name]

        xs = carve("xs", 0, 4096)
        mems = carve("mems", 4096, 2048)
        xT = carve("xT", 6144, 4096)
        wt = carve("wt", 10240, 4096)
        wn = carve("wn", 14336, 8192)
        projT = carve("projT", 22528, 8192)
        sb_v = carve("sb_v", 30720, 2048)
        ml_v = carve("ml_v", 32768, TT * MLH * (HD + 1))
        ml_o = carve("ml_o", 34832, 2048)
        mem_q = carve("mem_q", 36880, 2048)
        y_sbT = carve("y_sbT", 38928, 2048)
        y_mlT = carve("y_mlT", 40976, 2048)
        y_memT = carve("y_memT", 43024, 2048)
        rows = carve("rows", 40976, 4096)
        work = carve("work", 45072, 5120)
        memT = carve("memT", 50192, 2048)
        mem_qT = carve("mem_qT", 0, 2048)
        mem_kT = carve("mem_kT", 2048, 1024)
        mem_k = carve("mem_k", 3072, 1024)
        mem_v = carve("mem_v", 4096, 1024)
        gate_s = carve("gate_s", 5120, 1024)
        qk_squares = carve("qk_squares", 0, 3072)
        y_ml = carve("y_ml", 14336, 2048)
        squares = carve("squares", 16384, 2048)
        mergedT = carve("mergedT", 22528, 4096)
        x_again = carve("x_again", 26624, 4096)
        h_res = carve("h_res", 0, 4096)
        x_hl = carve("x_hl", 4096, 4096)
        uraw = carve("uraw", 10240, 4096)
        u_hl = carve("u_hl", 8192, 2048)
        vraw = carve("vraw", 14336, 4096)
        acts = carve("acts", 18432, 16384)
        LATE = 34816
        hT = carve("hT", LATE, 4096)
        h_scaled = carve("h_scaled", LATE + 4096, 4096)
        junk = carve("junk", LATE + 8192, 1024)
        qryT = carve("qryT", 26624, 8192)
        keysT = carve("keysT", 14336, 2048)
        scores = carve("scores", LATE, 4096)
        top_in = carve("top_in", LATE + 4096, 2048)
        cand = carve("cand", LATE + 6144, 2048)
        picks = carve("picks", LATE + 8192, 4096)
        top_small = carve("top_small", LATE + 12288, 4096)
        stage = carve("stage", LATE, 16384)
        e_rows = carve("e_rows", LATE + 16384, 1024)
        onehots = carve("onehots", 14336, 3584)
        iota_exp = carve("iota_exp", 17920, 512)
        v_hl = carve("v_hl", LATE, 8192)
        g_in = carve("g_in", LATE + 8192, 4096)
        w_f = carve("w_f", LATE + 12288, 1024)
        w_hl = carve("w_hl", LATE + 13312, 4096)

        xs3 = xs.rearrange("p (t d) -> p t d", d=D)
        mems3 = mems.rearrange("p (t d) -> p t d", d=D)
        xT3 = xT.rearrange("p (k t) -> p k t", t=T)
        memT3 = memT.rearrange("p (k t) -> p k t", t=MEM)
        hT3 = hT.rearrange("p (k t) -> p k t", t=T)
        h3 = h_res.rearrange("p (t d) -> p t d", d=D)
        hs3 = h_scaled.rearrange("p (t d) -> p t d", d=D)
        xa3 = x_again.rearrange("p (t d) -> p t d", d=D)
        wt4 = wt.rearrange("p (s k c) -> p s k c", s=4, c=P)
        wn4 = wn.rearrange("p (s k c) -> p s k c", s=2, c=BANK)
        projT3 = projT.rearrange("p (g t) -> p g t", t=T)
        mergedT3 = mergedT.rearrange("p (g t) -> p g t", t=T)
        qryT3 = qryT.rearrange("p (g t) -> p g t", t=T)
        keysT3 = keysT.rearrange("p (g k) -> p g k", k=NKEYS)
        sb_v3 = sb_v.rearrange("p (t c) -> p t c", c=512)
        ml_v4 = ml_v.rearrange("p (t h c) -> p t h c", t=TT, c=HD + 1)
        ml_o3 = ml_o.rearrange("p (t c) -> p t c", c=512)
        mem_q3 = mem_q.rearrange("p (t c) -> p t c", c=512)
        mem_k3 = mem_k.rearrange("p (t c) -> p t c", c=512)
        mem_v3 = mem_v.rearrange("p (t c) -> p t c", c=512)
        mem_qT3 = mem_qT.rearrange("p (h t) -> p h t", t=T)
        mem_kT3 = mem_kT.rearrange("p (h t) -> p h t", t=MEM)
        y_ml4 = y_ml.rearrange("p (t h c) -> p t h c", t=TT, c=HD)
        y_ml3 = y_ml.rearrange("p (t c) -> p t c", c=512)
        yT = [y.rearrange("p (g t) -> p g t", t=T) for y in (y_sbT, y_mlT, y_memT)]
        gate_s3 = gate_s.rearrange("p (s t) -> p s t", t=T)
        w_if = work[:, 2048:2048 + KD * 8].rearrange("p (k c) -> p k c", c=8)
        conv_out = work[:, 0:1024].rearrange("p (s t) -> p s t", t=T)

        lk = [work[:, 0:CAUSAL], work[:, CAUSAL:2 * CAUSAL]]
        aw = [work[:, 2 * CAUSAL:3 * CAUSAL], work[:, 3 * CAUSAL:4 * CAUSAL]]
        probs = [work[:, 0:1024], work[:, 1024:2048]]
        probsT = work[:, 2048:4096].rearrange("p (s m t) -> p s m t", s=2, t=T)

        def row(n):
            return rows[0:4, n * T:(n + 1) * T]
        r_abs, r_f, r_lf, r_b, r_a, r_max, r_m, r_zero = (row(n) for n in range(8))
        sel = store[0:4, 50192:50192 + 4 * P]
        sel3 = sel.rearrange("p (h c) -> p h c", c=P)

        S_X, S_Q, S_K, S_ML, S_H = 0, 6, 22, 30, 46
        sc3 = scores.rearrange("p (s c) -> p s c", c=16 * NKEYS)
        cand2 = top_in
        pick = [picks[:, n * 2048:(n + 1) * 2048] for n in range(2)]
        top_v = top_small[:, 0:256]
        top_i = top_small[:, 256:512].bitcast(U32)
        best_v = top_small[:, 512:640]
        best_c = top_small[:, 640:768].bitcast(U32)
        best_i = top_small[:, 768:896].bitcast(U32)
        best_j = top_small[:, 896:1024].bitcast(U32)
        g_sum = top_small[:, 1024:1032]
        g_rec = top_small[:, 1032:1040]

        class Lists:
            def __init__(self, n):
                b = 1152 + n * 1024
                self.top = top_small[:, b:b + 256]
                self.best = [top_small[:, b + 256 + k * P:b + 256 + (k + 1) * P] for k in range(2)]
                self.gate = top_small[:, b + 512:b + 640]
                self.out = top_small[:, b + 640:b + 1024].rearrange("p (s c) -> p s c", c=P)
        lists = [Lists(0), Lists(1)]
        xh, xl = [x_hl[:, n * 2048:(n + 1) * 2048].bitcast(BF16).rearrange("p (k t) -> p k t", t=T) for n in range(2)]
        ur = uraw.rearrange("p (s c) -> p s c", c=D)
        vr = vraw.rearrange("p (s c) -> p s c", c=D)
        uhl = u_hl.bitcast(BF16).rearrange("p (s w c) -> p s w c", s=2, w=2)
        vhl = v_hl.bitcast(BF16).rearrange("p (s n w c) -> p s n w c", s=2, n=CH, w=2)
        whl = w_hl.bitcast(BF16).rearrange("p (s n w t) -> p s n w t", s=2, n=CH, w=2)
        wf = w_f.rearrange("p (s t) -> p s t", t=T)
        g4 = g_in.rearrange("p (s b n t) -> p s b n t", s=2, b=NBLK, n=CH)
        acts3 = acts.rearrange("p (n t) -> p n t", t=T)
        stage4 = stage.rearrange("p (s k t) -> p s k t", s=2, t=BLK)
        e_bf = e_rows.bitcast(BF16).rearrange("p (n t) -> p n t", t=T)
        ohb = onehots.bitcast(BF16).rearrange("p (n k t) -> p n k t", n=7, t=GT)
        iota3 = iota_exp.bitcast(BF16).rearrange("p (k t) -> p k t", t=GT)

        ps = ctx.enter_context(nc.psum_tensor("ps", [P, 8 * BANK], F32))

        def bank(b, n=1):
            return ps[:, b * BANK:(b + n) * BANK]

        const_set, const_made = sem("const_set"), sem("const_made")
        sel_made = sem("sel_made")
        params_in, wif_in, keys_in, xa_in = sem("params_in"), sem("wif_in"), sem("keys_in"), sem("xa_in")
        x_in = [sem(f"x_in{i}") for i in range(TT)]
        mem_in = sem("mem_in")
        squared, rooted, scaled = sem("squared"), sem("rooted"), sem("scaled")
        turned, xT_out, memT_out = sem("turned"), sem("xT_out"), sem("memT_out")
        act_step, dve_step, pool_step = sem("act_step"), sem("dve_step"), sem("pool_step")
        wt_in = [sem(f"wt_in{s}") for s in range(4)]
        t_done = [sem(f"t_done{s}") for s in range(4)]
        t_out = [sem(f"t_out{s}") for s in range(4)]
        wn_in = [sem(f"wn_in{s}") for s in range(2)]
        n_done = [sem(f"n_done{s}") for s in range(4)]
        n_out = [sem(f"n_out{s}") for s in range(4)]
        if_done, if_ln = sem("if_done"), sem("if_ln")
        rows_made, thr_made, cols_turned, cols_out = sem("rows_made"), sem("thr_made"), sem("cols_turned"), sem("cols_out")
        q_scaled, conv_done, silu_done, sig_o = sem("q_scaled"), sem("conv_done"), sem("silu_done"), sem("sig_o")
        qk_squared, qk_rooted, qk_normed = sem("qk_squared"), sem("qk_rooted"), sem("qk_normed")
        z_ready, ln_ready, keep_ready, keep_masked = sem("z_ready"), sem("ln_ready"), sem("keep_ready"), sem("keep_masked")
        suffix_done, a_ready, a_masked, y_done, y_out = (
            sem("suffix_done"), sem("a_ready"), sem("a_masked"), sem("y_done"), sem("y_out"))
        s_ready, d_ready, e_ready, w_ready, w_masked, num_done, num_out = (
            sem("s_ready"), sem("d_ready"), sem("e_ready"), sem("w_ready"), sem("w_masked"), sem("num_done"),
            sem("num_out"))
        ml_squared, ml_rooted, ml_normed, mlT_done, mlT_out = (
            sem("ml_squared"), sem("ml_rooted"), sem("ml_normed"), sem("mlT_done"), sem("mlT_out"))
        qkT_done, qkT_out = sem("qkT_done"), sem("qkT_out")
        ms_ready, mmax_ready, mexp_ready, mp_ready, mpT_done, mpT_out, my_done, my_out = (
            sem("ms_ready"), sem("mmax_ready"), sem("mexp_ready"), sem("mp_ready"), sem("mpT_done"),
            sem("mpT_out"), sem("my_done"), sem("my_out"))
        gated = [sem(f"gated{s}") for s in range(2)]
        h_squared, h_rooted, h_normed, hT_done, hT_out = (
            sem("h_squared"), sem("h_rooted"), sem("h_normed"), sem("hT_done"), sem("hT_out"))
        score_done, score_out, score_used = sem("score_done"), sem("score_out"), sem("score_used")
        cand_top, cand_exp, list_ready, list_turned, list_out = (
            sem("cand_top"), sem("cand_exp"), sem("list_ready"), sem("list_turned"), sem("list_out"))
        idx_ready, pick_done = sem("idx_ready"), sem("pick_done")
        oh_ready, e2_ready, gate_done, gate_out = sem("oh_ready"), sem("e2_ready"), sem("gate_done"), sem("gate_out")
        block_stored = [sem(f"block_stored{s}") for s in range(2)]
        x_split, hi_split = sem("x_split"), sem("hi_split")
        u_in = [sem(f"u_in{s}") for s in range(4)]
        v_in = [sem(f"v_in{s}") for s in range(4)]
        g_read = [sem(f"g_read{s}") for s in range(2)]
        u_hi, u_lo, u_done, gelu_done = sem("u_hi"), sem("u_lo"), sem("u_done"), sem("gelu_done")
        v_hi, v_lo, w_full, w_hi, w_lo = sem("v_hi"), sem("v_lo"), sem("w_full"), sem("w_hi"), sem("w_lo")
        down_done, flushed, stored = sem("down_done"), sem("flushed"), sem("stored")

        PROJ_I = 4
        BR_I = 12
        PQ_I = 4
        BR_BASE, PQ_BASE = PROJ_I, PROJ_I + BR_I
        CONSTS = 5

        block = ctx.enter_context(nc.Block())

        @block.gpsimd
        def _(pool):
            pool.memset(ident[:, :], 0.0).then_inc(const_set, 1)
            pool.memset(neg_tri[:, :], -1.0).then_inc(const_set, 1)
            pool.memset(neg_ones[:, :], -1.0).then_inc(const_set, 1)
            pool.memset(eps_col[:, :], EPS).then_inc(const_set, 1)
            pool.memset(ml_v4[:, :, :, HD:HD + 1], 1.0).then_inc(const_set, 1)
            pool.wait_ge(const_set, CONSTS)
            pool.affine_select(out=ident[:, :], in_=ident[:, :], compare_op=ALU.not_equal, fill=1.0, base=0,
                               pattern=[[-1, P]], channel_multiplier=1).then_inc(const_made, 1)
            pool.affine_select(out=neg_tri[:, :], in_=neg_tri[:, :], compare_op=ALU.is_ge, fill=0.0, base=0,
                               pattern=[[-1, P]], channel_multiplier=1).then_inc(const_made, 1)
            pool.iota(iota_top[:, :], pattern=[[1, TOPK]], base=0, channel_multiplier=0,
                      allow_small_or_imprecise_dtypes=True).then_inc(const_made, 1)

            def keep_causal(buf, strict, done):
                for kt in range(TT):
                    block_ = buf[:, CAUSAL_AT[kt]:CAUSAL_AT[kt] + P]
                    ins = pool.affine_select(out=block_, in_=block_, compare_op=ALU.is_gt if strict else ALU.is_ge,
                                             fill=0.0, base=0, pattern=[[1, P]], channel_multiplier=-1)
                ins.then_inc(done, 1)

            def mask_keep(h):
                pool.wait_ge(keep_ready, h + 1)
                keep_causal(lk[h % 2], True, keep_masked)

            def mask_a(h):
                pool.wait_ge(a_ready, h + 1)
                keep_causal(aw[h % 2], True, a_masked)

            pool.wait_ge(n_done[3], 5)
            pool.wait_ge(n_done[1], 5)
            pool.memset(sel, 0.0).then_inc(sel_made, 1)
            pool.wait_ge(sel_made, 1)
            pool.affine_select(out=sel3, in_=sel3, compare_op=ALU.not_equal, fill=1.0, base=0,
                               pattern=[[-1, 4], [0, P]], channel_multiplier=1).then_inc(sel_made, 1)
            mask_keep(0)
            mask_keep(1)
            for h in range(SBH):
                mask_a(h)
                if h + 2 < SBH:
                    mask_keep(h + 2)
            for h in range(MLH):
                pool.wait_ge(w_ready, h + 1)
                keep_causal(lk[h % 2], False, w_masked)

            pool.wait_ge(x_split, 1)
            pool.iota(iota3, pattern=[[1, NKEYS], [0, GT]], base=0, channel_multiplier=0,
                      allow_small_or_imprecise_dtypes=True).then_inc(const_made, 1)

            def low_u(n):
                pool.wait_ge(u_hi, n + 1)
                pool.tensor_tensor(uhl[:, n % 2, 1, :], ur[:, n % 4, :], uhl[:, n % 2, 0, :],
                                   ALU.subtract).then_inc(u_lo, 1)

            for n in range(4):
                low_u(n)
            for t in range(TT):
                L = lists[t % 2]
                pool.wait_ge(idx_ready, t + 1)
                i_ = L.top.rearrange("p (h s i) -> p h s i", s=2, i=TOPK)
                for n in range(2):
                    pk = pick[n].rearrange("p (h r i) -> p h r i", r=TOPK, i=TOPK)
                    ins = pool.tensor_tensor(pk, pk, i_[:, :, n, :].unsqueeze(2).broadcast_to([P, PH, TOPK, TOPK]),
                                             ALU.mult)
                ins.then_inc(pick_done, 1)
                for n in range(t * 4 + 4, t * 4 + 8):
                    low_u(n)
            for n in range(20, NPRE):
                low_u(n)

        @block.sync
        def _(sp):
            for i in range(TT):
                sp.dma_start(xs3[:, i, :], A["x"][i * P:(i + 1) * P, :]).then_inc(x_in[i], 16)
            sp.dma_start(mems3, A["mem"].rearrange("(t p) d -> p t d", p=P)).then_inc(mem_in, 16)
            sp.dma_start(cols[:, :], A["cols"]).then_inc(params_in, 16)
            sp.dma_start(bif[:, :], A["bif"]).then_inc(params_in, 16)

            def load_t(s, use, src, k=KD):
                at_least(sp, t_done[s], use)
                sp.dma_start(wt4[:, s, 0:k, :], src).then_inc(wt_in[s], 16)

            def load_n(b, src):
                sp.dma_start(wn4[:, b, :, :], src).then_inc(wn_in[b], 16)

            for s in range(4):
                load_t(s, 0, A["w_t"][s])
            sp.dma_start(w_if, A["w_if"]).then_inc(wif_in, 16)
            load_n(0, A["w_n"][0])
            load_n(1, A["w_n"][1])
            with sp.Fori(1, PROJ_I) as i:
                for s in range(4):
                    load_t(s, i, A["w_t"][i * 4 + s])
            for n, src in enumerate((A["w_n"][2], A["w_n"][3], A["w_kv"][0], A["w_kv"][1])):
                sp.wait_ge(n_done[3], n + 1)
                load_n(n % 2, src)
            for b in range(3):
                with sp.Fori(0, 4) as i:
                    for s in range(4):
                        src = A["w_gate"] if s % 2 == 0 else A["w_br"]
                        load_t(s, i + (BR_BASE + b * 4), src[i * 2 + (b * 8 + s // 2)], KD if s % 2 == 0 else 4)
            sp.wait_ge(my_done, NH)
            sp.dma_start(xa3, A["x"].rearrange("(t p) d -> p t d", p=P)).then_inc(xa_in, 16)
            sp.wait_ge(mlT_done, MLH)
            load_n(0, A["w_out"][0])
            load_n(1, A["w_out"][1])
            with sp.Fori(0, PQ_I) as i:
                for s in range(4):
                    load_t(s, i + PQ_BASE, A["w_pq"][i * 4 + s])
            sp.wait_ge(n_done[3], 7)
            sp.dma_start(keysT3, A["keysT"]).then_inc(keys_in, 16)

            def load_u(n, s):
                at_least(sp, u_lo, n - 3)
                sp.dma_start(ur[:, s, :], A["u"][n]).then_inc(u_in[s], 16)

            def load_v(n, s):
                at_least(sp, v_lo, n - 3)
                sp.dma_start(vr[:, s, :], A["v"][n]).then_inc(v_in[s], 16)

            def load_g(c, s):
                at_least(sp, w_full, (c - 1) * CH)
                sp.dma_start(g_in[:, s * 2048:(s + 1) * 2048].rearrange("p (b n) -> p b n", b=NBLK), gates_dram[:, :, bass.ds(c * CH * BLK, CH * BLK)].rearrange(
                    "b p n -> p b n")).then_inc(g_read[s], 16)

            for s in range(4):
                sp.wait_ge(t_done[s], PQ_BASE + PQ_I)
            for n in range(20):
                load_u(n, n % 4)
            with sp.Fori(0, NBLK // 2) as j:
                for s in range(2):
                    for q in range(2):
                        load_u(j * 4 + (20 + 2 * s + q), 2 * s + q)
                    sp.wait_ge(gate_out, j * 16 + 8 * (s + 1))
                    sp.dma_start(gates_dram[j * 2 + s], stage[:, s * NKEYS * BLK:(s + 1) * NKEYS * BLK]).then_inc(block_stored[s], 16)
            sp.wait_ge(gate_done, T // GT)
            for n in range(4):
                load_v(n, n)
            for s in range(2):
                sp.wait_ge(block_stored[s], 16 * NBLK // 2)
            load_g(0, 0)
            load_g(1, 1)
            def load_chunk(j, s, with_u=True):
                for q in range(CH):
                    if with_u:
                        load_u(j * 8 + (NPRE + (s + 1) * CH + q), q)
                    load_v(j * 8 + ((s + 1) * CH + q), q)
                load_g(j * 2 + (s + 2), s)

            last = (NCH - AHEAD) // 2 - 1
            with sp.Fori(0, last) as j:
                for s in range(2):
                    load_chunk(j, s)
            load_chunk(last, 0)
            load_chunk(last, 1, with_u=False)
            for c in range(NCH - AHEAD, NCH - 1):
                for q in range(CH):
                    load_v((c + 1) * CH + q, q)
                if c + 2 < NCH:
                    load_g(c + 2, c % 2)
            for t in range(TT):
                sp.wait_ge(flushed, (NCH - 1) * CH + t + 1)
                sp.dma_start(out[t * P:(t + 1) * P, :], h3[:, t, :]).then_inc(stored, 16)
            sp.wait_ge(stored, 16 * TT)

        @block.tensor
        def _(pe):
            def turn(dst, src, rows_=P):
                return pe.transpose(dst, src, ident[0:rows_, 0:rows_])

            def t_group(s, use, k, act):
                pe.wait_ge(wt_in[s], (use + 1) * 16)
                at_least(pe, t_out[s], use)
                for n in range(k):
                    ins = pe.matmul(bank(s), wt4[:, s, n, :], act[:, n, :], start=n == 0, stop=n == k - 1)
                ins.then_inc(t_done[s], 1)

            def n_group(t, use, b, act, tile):
                at_least(pe, n_out[t], use)
                for n in range(KD):
                    ins = pe.matmul(bank(4 + t), act[:, n, tile * P:(tile + 1) * P], wn4[:, b, n, :],
                                    start=n == 0, stop=n == KD - 1)
                ins.then_inc(n_done[t], 1)

            pe.wait_ge(const_set, CONSTS)
            pe.wait_ge(const_made, 3)
            pe.wait_ge(scaled, TT)
            for k in range(KD):
                for i in range(TT):
                    ins = turn(bank(k)[:, i * P:(i + 1) * P], xs3[:, i, k * P:(k + 1) * P])
                ins.then_inc(turned, 1)
            pe.wait_ge(scaled, TT + MT)
            for k in range(KD):
                pe.wait_ge(xT_out, k + 1)
                for i in range(MT):
                    ins = turn(bank(k)[:, i * P:(i + 1) * P], mems3[:, i, k * P:(k + 1) * P])
                ins.then_inc(turned, 1)
            pe.wait_ge(memT_out, KD)

            for s in range(4):
                t_group(s, 0, KD, xT3)
            with pe.Fori(1, PROJ_I) as i:
                for s in range(4):
                    t_group(s, i, KD, xT3)
            pe.wait_ge(wif_in, 16)
            for g in range(2):
                pe.wait_ge(t_out[g], PROJ_I)
                for n in range(KD):
                    ins = pe.matmul(bank(g)[0:4, :], w_if[:, n, g * 4:(g + 1) * 4], xT3[:, n, :],
                                    start=n == 0, stop=n == KD - 1)
            ins.then_inc(if_done, 1)
            for b in range(4):
                pe.wait_ge(wn_in[b % 2], 16 * (b // 2 + 1))
                for t in range(TT):
                    n_group(t, b, b % 2, xT3, t)
            for b in range(2):
                pe.wait_ge(wn_in[b], 16 * 3)
                for m in range(MT):
                    n_group(b * MT + m, 4, b, memT3, m)
            pe.wait_ge(rows_made, 1)
            pe.wait_ge(thr_made, 1)
            pe.wait_ge(t_out[2], PROJ_I)
            for i, r in enumerate((r_a, r_m)):
                for t in range(TT):
                    ins = turn(bank(2)[:, (i * TT + t) * 4:(i * TT + t) * 4 + 4], r[:, t * P:(t + 1) * P], 4)
            ins.then_inc(cols_turned, 1)
            pe.wait_ge(cols_out, 1)
            pe.wait_ge(t_out[3], PROJ_I)
            for t in range(TT):
                pe.wait_ge(n_out[t], 5)

            def causal(s, kt, q0=None):
                q0 = kt if q0 is None else q0
                at = s * 3 * BANK + CAUSAL_AT[kt] + (q0 - kt) * P
                return ps[:, at:at + T - q0 * P]

            def part(buf, kt, q0=None, q1=TT):
                q0 = kt if q0 is None else q0
                return buf[:, CAUSAL_AT[kt] + (q0 - kt) * P:CAUSAL_AT[kt] + (q1 - kt) * P]

            def sb_scores(h):
                at_least(pe, a_ready, h - 1)
                r = slice(SBD * (h % 2), SBD * (h % 2) + SBD)
                for kt in range(TT):
                    ins = pe.matmul(causal(h % 2, kt), projT3[r, 4 + h // 2, kt * P:(kt + 1) * P],
                                    projT3[r, h // 2, kt * P:T], start=kt != 3, stop=False, skip_group_check=True)
                ins.then_inc(z_ready, 1)

            def sb_suffix(h):
                pe.wait_ge(keep_masked, h + 1)
                for kt in range(TT):
                    for k2 in range(kt, TT):
                        ins = pe.matmul(causal(h % 2, kt, k2), neg_tri[:, :] if k2 == kt else neg_ones[:, :],
                                        part(lk[h % 2], k2), start=False, stop=k2 == TT - 1, skip_group_check=True)
                ins.then_inc(suffix_done, 1)

            def sb_values(h):
                pe.wait_ge(a_masked, h + 1)
                at_least(pe, y_out, h - 1)
                r = slice(SBD * (h % 2), SBD * (h % 2) + SBD)
                for kt in range(TT):
                    ins = pe.matmul(bank(6 + h % 2)[r, kt * P:T], sb_v3[:, kt, h * SBD:(h + 1) * SBD],
                                    part(aw[h % 2], kt), start=kt == 0, stop=kt == TT - 1)
                ins.then_inc(y_done, 1)

            sb_scores(0)
            sb_scores(1)
            for h in range(SBH):
                sb_suffix(h)
                if h >= 1:
                    sb_values(h - 1)
                    if h + 1 < SBH:
                        sb_scores(h + 1)
            sb_values(SBH - 1)

            pe.wait_ge(silu_done, 8)
            pe.wait_ge(sel_made, 2)
            pe.wait_ge(y_out, SBH)

            def ml_scores(h):
                at_least(pe, num_out, h - 1)
                at_least(pe, d_ready, h - 1)
                pe.matmul(bank(6 + h % 2), sel3[:, h, :], r_max, start=True, stop=True)
                for kt in range(TT):
                    ins = pe.matmul(causal(h % 2, kt), projT3[:, 12 + h, kt * P:(kt + 1) * P],
                                    projT3[:, 8 + h, kt * P:T], start=kt != 3, stop=True, skip_group_check=True)
                ins.then_inc(s_ready, 1)

            def ml_values(h):
                pe.wait_ge(w_masked, h + 1)
                for t in range(TT):
                    at = (h % 2 * 3 + t // 2) * BANK + (t % 2) * (HD + 1)
                    for kt in range(t + 1):
                        ins = pe.matmul(ps[:, at:at + HD + 1], part(lk[h % 2], kt, t, t + 1), ml_v4[:, kt, h, :],
                                        start=kt == 0, stop=kt == t)
                ins.then_inc(num_done, 1)

            ml_scores(0)
            ml_scores(1)
            for h in range(MLH):
                ml_values(h)
                if h + 2 < MLH:
                    ml_scores(h + 2)
            pe.wait_ge(num_out, MLH)
            pe.wait_ge(ml_normed, 1)
            for h in range(MLH):
                for t in range(TT):
                    ins = turn(bank(h)[:, t * P:(t + 1) * P], y_ml4[:, t, h, :])
                ins.then_inc(mlT_done, 1)

            pe.wait_ge(qk_normed, 1)
            for h in range(NH):
                pe.wait_ge(mlT_out, h + 1)
                for t in range(TT):
                    ins = turn(bank(h)[:, t * P:(t + 1) * P], mem_q3[:, t, h * HD:(h + 1) * HD])
                ins.then_inc(qkT_done, 1)
            for h in range(NH):
                for t in range(MT):
                    ins = turn(bank(4 + h // 2)[:, (h % 2 * MT + t) * P:(h % 2 * MT + t + 1) * P],
                               mem_k3[:, t, h * HD:(h + 1) * HD])
            ins.then_inc(qkT_done, 1)
            pe.wait_ge(qkT_out, NH + 1)

            def mem_scores(h):
                at_least(pe, mexp_ready, h - 1)
                for t in range(TT):
                    at = (h % 2) * 2 * BANK + t * MEM
                    ins = pe.matmul(ps[:, at:at + MEM], mem_qT3[:, h, t * P:(t + 1) * P], mem_kT3[:, h, :],
                                    start=True, stop=True)
                ins.then_inc(ms_ready, 1)

            mem_scores(0)
            for h in range(NH):
                if h + 1 < NH:
                    mem_scores(h + 1)
                pe.wait_ge(mp_ready, h + 1)
                at_least(pe, mpT_out, h)
                for m in range(MT):
                    for t in range(TT):
                        ins = turn(bank(4 + m)[:, t * P:(t + 1) * P],
                                   probs[h % 2][:, t * MEM + m * P:t * MEM + (m + 1) * P])
                ins.then_inc(mpT_done, 1)
                pe.wait_ge(mpT_out, h + 1)
                at_least(pe, my_out, h - 1)
                for m in range(MT):
                    ins = pe.matmul(bank(6 + h % 2), mem_v3[:, m, h * HD:(h + 1) * HD], probsT[:, h % 2, m, :],
                                    start=m == 0, stop=m == MT - 1)
                ins.then_inc(my_done, 1)
            pe.wait_ge(my_out, NH)

            for b in range(3):
                with pe.Fori(0, 4) as i:
                    for s in range(4):
                        t_group(s, i + (BR_BASE + b * 4), KD if s % 2 == 0 else 4, xT3 if s % 2 == 0 else yT[b])
            for s in range(2):
                pe.wait_ge(gated[s], BR_I)
            for b in range(2):
                pe.wait_ge(wn_in[b], 16 * 4)
                for t in range(TT):
                    n_group(t, 5 + b, b, mergedT3, t)

            pe.wait_ge(h_normed, 1)
            for s in range(4):
                pe.wait_ge(t_out[s], BR_BASE + BR_I)
            for k in range(KD):
                for i in range(TT):
                    ins = turn(bank(k)[:, i * P:(i + 1) * P], hs3[:, i, k * P:(k + 1) * P])
                ins.then_inc(hT_done, 1)
            pe.wait_ge(hT_out, KD)
            with pe.Fori(0, PQ_I) as i:
                for s in range(4):
                    t_group(s, i + PQ_BASE, KD, hT3)
            pe.wait_ge(keys_in, 16)
            for s in range(4):
                pe.wait_ge(t_out[s], PQ_BASE + PQ_I)

            def key_scores(t):
                at_least(pe, score_out, t)
                for g in range(2 * PH):
                    ins = pe.matmul(ps[:, 4 * BANK + g * NKEYS:4 * BANK + (g + 1) * NKEYS],
                                    qryT3[:, g, t * P:(t + 1) * P], keysT3[:, g, :], start=True, stop=True)
                ins.then_inc(score_done, 1)

            def turn_lists(t):
                pe.wait_ge(list_ready, t + 1)
                at_least(pe, list_out, t)
                for n in range(3):
                    ins = turn(bank(2)[:, n * P:(n + 1) * P], lists[t % 2].out[:, n, :])
                ins.then_inc(list_turned, 1)

            PARTS = ((0, 0), (0, 1), (1, 0))

            def up(n, s, quarter=None):
                steps_ = [(k, w) for k in range(KD) for w in PARTS]
                if quarter is None or quarter == 0:
                    pe.wait_ge(u_lo, n + 1)
                    at_least(pe, gelu_done, n - 1)
                chosen = range(24) if quarter is None else range(quarter * 6, quarter * 6 + 6)
                for i in chosen:
                    k, (wu, wx) = steps_[i]
                    ins = pe.matmul(bank(s), uhl[:, s, wu, k * P:(k + 1) * P], (xh, xl)[wx][:, k, :],
                                    start=i == 0, stop=i == 23, skip_group_check=True)
                if chosen[-1] == 23:
                    ins.then_inc(u_done, 1)

            def down(c, par, q):
                if q == 0:
                    pe.wait_ge(v_lo, (c + 1) * CH)
                    pe.wait_ge(w_lo, (c + 1) * CH)
                at_least(pe, flushed, c * CH + (q - 1))
                for i in range(CH):
                    for ww, wv in PARTS:
                        for h in range(2):
                            ins = pe.matmul(bank(4 + 2 * (q % 2) + h), whl[:, par, i, ww, q * P:(q + 1) * P],
                                            vhl[:, par, i, wv, h * BANK:(h + 1) * BANK],
                                            start=i == 0 and (ww, wv) == (0, 0), stop=i == CH - 1 and ww == 1)
                ins.then_inc(down_done, 1)

            pe.wait_ge(x_split, 1)
            key_scores(0)
            key_scores(1)
            up(0, 0)
            key_scores(2)
            for n in range(1, 4):
                up(n, n % 2)
            key_scores(3)
            turn_lists(0)
            for t in range(1, TT):
                for n in range(4 * t, 4 * t + 4):
                    up(n, n % 2)
                turn_lists(t)
            pe.wait_ge(score_out, TT)

            def gate_group(g, s):
                pe.wait_ge(oh_ready, g + 1)
                at_least(pe, gate_out, g - 1)
                for q in range(GT):
                    for w in range(2):
                        at = (2 + 4 * s) * BANK + q * P
                        ins = pe.matmul(ps[:, at:at + P], ohb[:, 3 * s, :, q], ohb[:, 3 * s + 1 + w, :, q],
                                        start=w == 0, stop=w == 1)
                ins.then_inc(gate_done, 1)

            def gate_blocks(j):
                for i in range(16):
                    gate_group(j * 16 + i, i % 2)
                    up(j * 4 + (16 + i // 4), (i // 4) % 2, i % 4)

            gate_blocks(0)
            with pe.Fori(1, NBLK // 2) as j:
                gate_blocks(j)

            def chunk_pair(j, with_u):
                for par in range(2):
                    for q in range(CH):
                        if with_u:
                            up(j * 8 + (NPRE + par * CH + q), q % 2)
                        down(j * 2 + par, par, q)

            pe.wait_ge(gate_out, T // GT)
            chunk_pair(0, True)
            with pe.Fori(1, (NCH - AHEAD) // 2) as j:
                chunk_pair(j, True)
            with pe.Fori((NCH - AHEAD) // 2, NCH // 2) as j:
                chunk_pair(j, False)

        @block.scalar
        def _(act):
            steps = [0]

            def link(ins):
                steps[0] += 1
                ins.then_inc(act_step, 1)
                act.wait_ge(act_step, steps[0])

            act.wait_ge(const_set, CONSTS)
            for i in range(TT):
                act.wait_ge(x_in[i], 16)
                link(act.activation(work[:, 0:D], xs3[:, i, :], ACT.Square, accum_out=sums[:, i:i + 1]))
            act.wait_ge(mem_in, 16)
            for i in range(MT):
                link(act.activation(work[:, 0:D], mems3[:, i, :], ACT.Square, accum_out=sums[:, TT + i:TT + i + 1]))
            act.activation(roots[:, S_X:S_Q], sums[:, S_X:S_Q], ACT.Sqrt, bias=eps_col[:, :],
                           scale=1.0 / D).then_inc(rooted, 1)
            act.wait_ge(params_in, 32)
            for k in range(KD):
                act.wait_ge(turned, k + 1)
                act.activation(xT3[:, k, :], bank(k), ACT.Copy,
                               scale=cols[:, C_MIX + k:C_MIX + k + 1]).then_inc(xT_out, 1)
            for s in range(4):
                act.wait_ge(t_done[s], 1)
                act.activation(projT3[:, s, :], bank(s), ACT.Copy, scale=SBD ** -0.5).then_inc(t_out[s], 1)
            with act.Fori(1, PROJ_I) as i:
                for s in range(4):
                    act.wait_ge(t_done[s], i + 1)
                    act.activation(projT[:, bass.ds((i * 4 + s) * T, T)], bank(s), ACT.Copy).then_inc(t_out[s], 1)
            act.wait_ge(if_done, 1)
            link(act.activation(r_abs, bank(1)[0:4, :], ACT.Abs, bias=bif[:, 1:2]))
            link(act.activation(r_abs, r_abs, ACT.Exp, scale=-1.0))
            act.activation(r_abs, r_abs, ACT.Ln, bias=1.0).then_inc(if_ln, 1)
            for g in range(8):
                act.wait_ge(conv_done, g + 1)
                act.activation(projT3[:, 8 + g, :], conv_out[:, g % 2, :], ACT.Silu).then_inc(silu_done, 1)
            for t in range(TT):
                act.wait_ge(n_out[t], 3)
            act.activation(ml_o, ml_o, ACT.Sigmoid).then_inc(sig_o, 1)
            act.wait_ge(rows_made, 1)
            act.activation(r_m, r_m, ACT.Exp, scale=-1.0).then_inc(thr_made, 1)
            act.wait_ge(qk_squared, 1)
            act.activation(roots[:, S_Q:S_ML], sums[:, S_Q:S_ML], ACT.Sqrt, bias=eps_col[:, :],
                           scale=1.0 / HD).then_inc(qk_rooted, 1)

            def region(s):
                return ps[:, s * 3 * BANK:s * 3 * BANK + CAUSAL]

            def ln_part(h):
                act.wait_ge(z_ready, h + 1)
                at_least(act, suffix_done, h - 1)
                link(act.activation(lk[h % 2], region(h % 2), ACT.Abs))
                link(act.activation(lk[h % 2], lk[h % 2], ACT.Exp, scale=-1.0))
                act.activation(lk[h % 2], lk[h % 2], ACT.Ln, bias=1.0).then_inc(ln_ready, 1)

            ln_part(0)
            ln_part(1)
            for h in range(SBH):
                act.wait_ge(suffix_done, h + 1)
                at_least(act, y_done, h - 1)
                act.activation(aw[h % 2], region(h % 2), ACT.Exp).then_inc(a_ready, 1)
                if h + 2 < SBH:
                    ln_part(h + 2)

            for h in range(MLH):
                act.wait_ge(d_ready, h + 1)
                act.activation(lk[h % 2], lk[h % 2], ACT.Exp, scale=-1.0).then_inc(e_ready, 1)
            act.wait_ge(ml_squared, 1)
            act.activation(roots[:, S_ML:S_H], sums[:, S_ML:S_H], ACT.Sqrt, bias=eps_col[:, :],
                           scale=1.0 / HD).then_inc(ml_rooted, 1)
            for h in range(MLH):
                act.wait_ge(mlT_done, h + 1)
                act.activation(yT[1][:, h, :], bank(h), ACT.Copy, scale=cols[:, C_MLG:C_MLG + 1]).then_inc(mlT_out, 1)
            act.wait_ge(qk_normed, 1)
            for h in range(NH):
                act.wait_ge(qkT_done, h + 1)
                act.activation(mem_qT3[:, h, :], bank(h), ACT.Copy, scale=qg_scaled[:, 0:1]).then_inc(qkT_out, 1)
            act.wait_ge(qkT_done, NH + 1)
            act.activation(mem_kT, bank(4, 2), ACT.Copy, scale=cols[:, C_KG:C_KG + 1]).then_inc(qkT_out, 1)
            for h in range(NH):
                act.wait_ge(mmax_ready, h + 1)
                at_least(act, mpT_done, h - 1)
                for t in range(TT):
                    at = (h % 2) * 2 * BANK + t * MEM
                    d = 8 + (h % 2) * 4 + t
                    ins = act.activation(probs[h % 2][:, t * MEM:(t + 1) * MEM], ps[:, at:at + MEM], ACT.Exp,
                                         bias=den[:, (h % 2) * 4 + t:(h % 2) * 4 + t + 1], accum_out=den[:, d:d + 1])
                ins.then_inc(mexp_ready, 1)
                act.wait_ge(mpT_done, h + 1)
                at_least(act, my_done, h - 1)
                act.activation(probsT[:, h % 2, :, :], bank(4, 2).rearrange("p (m t) -> p m t", t=T),
                               ACT.Copy).then_inc(mpT_out, 1)

            def branch_gates(b, i):
                for s in (0, 2):
                    act.wait_ge(t_done[s], i + (BR_BASE + b * 4 + 1))
                    at_least(act, gated[s // 2], i + b * 4)
                    act.activation(gate_s3[:, s // 2, :], bank(s), ACT.Sigmoid,
                                   bias=cols[:, bass.ds(i * 2 + (C_BGATE + b * 8 + s // 2), 1)]).then_inc(t_out[s], 1)

            branch_gates(0, 0)
            for b in range(3):
                with act.Fori(1 if b == 0 else 0, 4) as i:
                    branch_gates(b, i)

            for t in range(TT):
                act.wait_ge(n_out[t], 7)
                link(act.activation(junk, h3[:, t, :], ACT.Square, accum_out=sums[:, S_H + t:S_H + t + 1]))
            act.activation(roots[:, S_H:S_H + TT], sums[:, S_H:S_H + TT], ACT.Sqrt, bias=eps_col[:, :],
                           scale=1.0 / D).then_inc(h_rooted, 1)
            for k in range(KD):
                act.wait_ge(hT_done, k + 1)
                act.activation(hT3[:, k, :], bank(k), ACT.Copy,
                               scale=cols[:, C_FFN + k:C_FFN + k + 1]).then_inc(hT_out, 1)
            with act.Fori(0, PQ_I) as i:
                for s in range(4):
                    act.wait_ge(t_done[s], i + (PQ_BASE + 1))
                    act.activation(qryT[:, bass.ds((i * 4 + s) * T, T)], bank(s), ACT.Copy).then_inc(t_out[s], 1)
            def score_copy(t):
                act.wait_ge(score_done, t + 1)
                at_least(act, score_used, t - 1)
                act.activation(sc3[:, t % 2, :], bank(4, 4), ACT.Copy).then_inc(score_out, 1)

            def high_u(n, s):
                act.wait_ge(u_in[s], (n - s) * 4 + 16 if isinstance(n, int) else n * 4 + (16 - 4 * s))
                at_least(act, u_done, n - 1)
                act.activation(uhl[:, s % 2, 0, :], ur[:, s, :], ACT.Copy).then_inc(u_hi, 1)

            def gelu(n, s, slot, first=False):
                act.wait_ge(u_done, n + 1)
                if not first:
                    at_least(act, w_full, n - (NPRE - 1))
                act.activation(acts3[:, slot, :] if isinstance(slot, int) else acts[:, bass.ds(slot * T, T)],
                               bank(s % 2), ACT.Gelu).then_inc(gelu_done, 1)

            def gate_exp(t):
                act.wait_ge(cand_top, t + 1)
                act.activation(lists[t % 2].gate, lists[t % 2].gate, ACT.Exp).then_inc(cand_exp, 1)

            act.activation(x_hl[:, 0:2048].bitcast(BF16), hT, ACT.Copy).then_inc(hi_split, 1)
            high_u(0, 0)
            high_u(1, 1)
            act.wait_ge(x_split, 1)
            score_copy(0)
            score_copy(1)
            gelu(0, 0, 0)
            high_u(2, 2)
            for n in range(1, 3):
                gelu(n, n % 2, n)
                high_u(n + 2, (n + 2) % 4)
            score_copy(2)
            gelu(3, 1, 3)
            high_u(5, 1)
            gate_exp(0)
            score_copy(3)
            for t in range(1, TT):
                for n in range(4 * t, 4 * t + 4):
                    gelu(n, n % 2, n)
                    high_u(n + 2, (n + 2) % 4)
                gate_exp(t)

            def gate_copy(g, i):
                act.wait_ge(gate_done, g + 1)
                act.activation(stage4[:, i // 8, :, (i % 8) * GT:(i % 8 + 1) * GT],
                               bank(2 + 4 * (i % 2), 2).rearrange("p (q k) -> p k q", k=NKEYS),
                               ACT.Copy).then_inc(gate_out, 1)

            def gate_blocks(j):
                for i in range(16):
                    if i % 8 == 0:
                        at_least(act, block_stored[i // 8], j * 16)
                    gate_copy(j * 16 + i, i)
                    if i % 4 == 3:
                        n = j * 4 + (16 + i // 4)
                        gelu(n, i // 4, n, first=True)
                        high_u(n + 2, (i // 4 + 2) % 4)

            act.wait_ge(list_ready, TT)
            act.wait_ge(list_turned, TT)
            gate_blocks(0)
            with act.Fori(1, NBLK // 2) as j:
                gate_blocks(j)

            def prepare(c, par, q):
                act.wait_ge(v_in[q], c * 16 + 16)
                if q == 0:
                    at_least(act, down_done, (c - 1) * CH)
                act.activation(vhl[:, par, q, 0, :], vr[:, q, :], ACT.Copy).then_inc(v_hi, 1)
                act.wait_ge(w_full, c * CH + q + 1)
                act.activation(whl[:, par, q, 0, :], wf[:, q % 2, :], ACT.Copy).then_inc(w_hi, 1)

            for s in range(2):
                act.wait_ge(block_stored[s], 16 * NBLK // 2)
            for q in range(CH):
                prepare(0, 0, q)

            def chunks(o, first_c, count, with_u):
                for i in range(count):
                    c = o * AHEAD + (first_c + i)
                    for q in range(CH):
                        prepare(c + 1, (first_c + i + 1) % 2, q)
                        if with_u:
                            n = o * NPRE + (NPRE + i * CH + q)
                            gelu(n, q % 2, i * CH + q)
                            high_u(n + 2, (q + 2) % 4)

            chunks(0, 0, AHEAD, True)
            with act.Fori(1, NCH // AHEAD - 2) as o:
                chunks(o, 0, AHEAD, True)
            for i in range(AHEAD):
                c = NCH - 2 * AHEAD + i
                for q in range(CH):
                    prepare(c + 1, (c + 1) % 2, q)
                    n = NCH * CH - NPRE + i * CH + q
                    gelu(n, q % 2, i * CH + q)
                    if n + 2 < NCH * CH:
                        high_u(n + 2, (q + 2) % 4)
            for c in range(NCH - AHEAD, NCH - 1):
                for q in range(CH):
                    prepare(c + 1, (c + 1) % 2, q)

        @block.vector
        def _(dve):
            steps = [0]

            def link(ins):
                steps[0] += 1
                ins.then_inc(dve_step, 1)
                dve.wait_ge(dve_step, steps[0])

            dve.wait_ge(rooted, 1)
            link(dve.reciprocal(rstd[:, S_X:S_Q], roots[:, S_X:S_Q]))
            for i in range(TT):
                dve.tensor_scalar(xs3[:, i, :], xs3[:, i, :], rstd[:, i:i + 1], None, ALU.mult).then_inc(scaled, 1)
            for i in range(MT):
                dve.tensor_scalar(mems3[:, i, :], mems3[:, i, :], rstd[:, TT + i:TT + i + 1], None,
                                  ALU.mult).then_inc(scaled, 1)
            dve.wait_ge(params_in, 32)
            dve.tensor_scalar(qg_scaled[:, :], cols[:, C_QG:C_QG + 1], HD_SCALE, None, ALU.mult).then_inc(q_scaled, 1)
            for k in range(KD):
                dve.wait_ge(turned, KD + k + 1)
                dve.tensor_scalar(memT3[:, k, :], bank(k)[:, 0:MEM], cols[:, C_MEM + k:C_MEM + k + 1], None,
                                  ALU.mult).then_inc(memT_out, 1)

            def conv(g):
                dve.wait_ge(t_out[g % 4], (8 + g) // 4 + 1)
                at_least(dve, silu_done, g - 1)
                x_, y_ = projT3[:, 8 + g, :], conv_out[:, g % 2, :]
                w = [cols[:, C_CONVW + g * 4 + k:C_CONVW + g * 4 + k + 1] for k in range(4)]
                link(dve.tensor_scalar(y_, x_, w[3], cols[:, C_CONVB + g:C_CONVB + g + 1], ALU.mult, ALU.add))
                for k in range(3):
                    lag = 3 - k
                    ins = dve.scalar_tensor_tensor(out=y_[:, lag:T], in0=x_[:, 0:T - lag], scalar=w[k],
                                                   in1=y_[:, lag:T], op0=ALU.mult, op1=ALU.add)
                    if k < 2:
                        link(ins)
                ins.then_inc(conv_done, 1)

            natural = [sb_v3, None, ml_o3, mem_q3]
            for b in range(4):
                for t in range(TT):
                    dve.wait_ge(n_done[t], b + 1)
                    if b == 1:
                        ins = dve.tensor_copy(ml_v4[:, t, :, 0:HD], bank(4 + t).rearrange("p (h c) -> p h c", c=HD))
                    else:
                        ins = dve.tensor_copy(natural[b][:, t, :], bank(4 + t))
                    ins.then_inc(n_out[t], 1)
                conv(2 * b)
                conv(2 * b + 1)
            dve.wait_ge(if_ln, 1)
            dve.memset(r_zero, 0.0)
            link(dve.tensor_scalar(r_f, bank(1)[0:4, :], bif[:, 1:2], 0.0, ALU.add, ALU.min))
            link(dve.tensor_tensor(r_lf, r_f, r_abs, ALU.subtract))
            link(dve.tensor_tensor_scan(r_b, r_lf, r_zero, 0.0, ALU.add, ALU.add))
            link(dve.scalar_tensor_tensor(out=r_a, in0=bank(0)[0:4, :], scalar=bif[:, 0:1], in1=r_b,
                                          op0=ALU.add, op1=ALU.subtract))
            link(dve.tensor_tensor_scan(r_max, r_a, r_a, 0.0, ALU.max, ALU.max))
            dve.tensor_tensor(r_m, r_b, r_max, ALU.add).then_inc(rows_made, 1)
            for t in range(TT):
                dve.wait_ge(n_done[t], 5)
                dst = mem_k3 if t < MT else mem_v3
                dve.tensor_copy(dst[:, t % MT, :], bank(4 + t)).then_inc(n_out[t], 1)
            dve.wait_ge(n_out[3], 5)
            dve.tensor_tensor(qk_squares[:, 0:2048], mem_q, mem_q, ALU.mult)
            link(dve.tensor_tensor(qk_squares[:, 2048:3072], mem_k, mem_k, ALU.mult))
            dve.tensor_reduce(sums[:, S_Q:S_ML], qk_squares.rearrange("p (g c) -> p g c", c=HD), AX.X,
                              ALU.add).then_inc(qk_squared, 1)
            dve.wait_ge(qk_rooted, 1)
            link(dve.reciprocal(rstd[:, S_Q:S_ML], roots[:, S_Q:S_ML]))

            def spread(col, n, m):
                return col.unsqueeze(2).broadcast_to([P, n, m])

            q_ = mem_q.rearrange("p (g c) -> p g c", c=HD)
            k_ = mem_k.rearrange("p (g c) -> p g c", c=HD)
            dve.tensor_tensor(q_, q_, spread(rstd[:, S_Q:S_K], 16, HD), ALU.mult)
            dve.tensor_tensor(k_, k_, spread(rstd[:, S_K:S_ML], 8, HD), ALU.mult).then_inc(qk_normed, 1)
            dve.wait_ge(cols_turned, 1)
            dve.tensor_copy(key_cols[:, :], bank(2)[:, 0:32]).then_inc(cols_out, 1)

            def region(s):
                return ps[:, s * 3 * BANK:s * 3 * BANK + CAUSAL]

            def keep(h):
                dve.wait_ge(ln_ready, h + 1)
                dve.scalar_tensor_tensor(out=lk[h % 2], in0=region(h % 2), scalar=0.0, in1=lk[h % 2],
                                         op0=ALU.max, op1=ALU.add).then_inc(keep_ready, 1)

            keep(0)
            keep(1)
            for h in range(SBH):
                r = slice(SBD * (h % 2), SBD * (h % 2) + SBD)
                dve.wait_ge(y_done, h + 1)
                dve.tensor_copy(yT[0][r, h // 2, :], bank(6 + h % 2)[r, :]).then_inc(y_out, 1)
                if h + 2 < SBH:
                    keep(h + 2)

            def decay(h):
                dve.wait_ge(s_ready, h + 1)
                at_least(dve, num_done, h - 1)
                for kt in range(TT):
                    ins = dve.tensor_scalar(lk[h % 2][:, CAUSAL_AT[kt]:CAUSAL_AT[kt] + T - kt * P],
                                            bank(6 + h % 2)[:, kt * P:T],
                                            key_cols[:, kt * 4 + h:kt * 4 + h + 1], 0.0, ALU.subtract, ALU.max)
                ins.then_inc(d_ready, 1)

            def weigh(h):
                dve.wait_ge(e_ready, h + 1)
                dve.scalar_tensor_tensor(out=lk[h % 2], in0=region(h % 2), scalar=HD_SCALE, in1=lk[h % 2],
                                         op0=ALU.mult, op1=ALU.mult).then_inc(w_ready, 1)

            def divide(h):
                dve.wait_ge(num_done, h + 1)
                base = h % 2 * 3 * BANK
                d_ = ps[:, base:base + 2 * BANK].rearrange("p (a b) -> p a b", b=BANK)[:, :, HD:2 * HD + 2:HD + 1]
                m_ = key_cols[:, 16 + h:32:4].rearrange("p (a b) -> p a b", b=2)
                o_ = den[:, 0:4].rearrange("p (a b) -> p a b", b=2)
                link(dve.scalar_tensor_tensor(out=o_, in0=d_, scalar=-1.0, in1=m_, op0=ALU.mult, op1=ALU.max))
                link(dve.tensor_tensor(o_, o_, d_, ALU.max))
                link(dve.reciprocal(den[:, 4:8], den[:, 0:4]))
                for t in range(TT):
                    at = (h % 2 * 3 + t // 2) * BANK + (t % 2) * (HD + 1)
                    ins = dve.tensor_scalar(y_ml4[:, t, h, :], ps[:, at:at + HD], den[:, 4 + t:5 + t], None, ALU.mult)
                ins.then_inc(num_out, 1)

            decay(0)
            weigh(0)
            decay(1)
            weigh(1)
            for h in range(MLH):
                divide(h)
                if h + 2 < MLH:
                    decay(h + 2)
                    weigh(h + 2)
            dve.wait_ge(num_out, MLH)
            link(dve.tensor_tensor(squares, y_ml, y_ml, ALU.mult))
            dve.tensor_reduce(sums[:, S_ML:S_H], squares.rearrange("p (g c) -> p g c", c=HD), AX.X,
                              ALU.add).then_inc(ml_squared, 1)
            dve.wait_ge(ml_rooted, 1)
            link(dve.reciprocal(rstd[:, S_ML:S_H], roots[:, S_ML:S_H]))
            y_ = y_ml.rearrange("p (g c) -> p g c", c=HD)
            link(dve.tensor_tensor(y_, y_, spread(rstd[:, S_ML:S_H], 16, HD), ALU.mult))
            dve.wait_ge(sig_o, 1)
            dve.tensor_tensor(y_ml, y_ml, ml_o, ALU.mult).then_inc(ml_normed, 1)

            for h in range(NH):
                n4 = (h % 2) * 4
                dve.wait_ge(ms_ready, h + 1)
                dve.tensor_reduce(den[:, n4:n4 + 4], ps[:, (h % 2) * 2 * BANK:(h % 2 + 1) * 2 * BANK].rearrange(
                    "p (t m) -> p t m", m=MEM), AX.X, ALU.max, negate=True).then_inc(mmax_ready, 1)
                dve.wait_ge(mexp_ready, h + 1)
                link(dve.reciprocal(den[:, 16 + n4:20 + n4], den[:, 8 + n4:12 + n4]))
                p_ = probs[h % 2].rearrange("p (t m) -> p t m", m=MEM)
                dve.tensor_tensor(p_, p_, spread(den[:, 16 + n4:20 + n4], 4, MEM), ALU.mult).then_inc(mp_ready, 1)
                dve.wait_ge(my_done, h + 1)
                dve.tensor_copy(yT[2][:, h, :], bank(6 + h % 2)).then_inc(my_out, 1)

            for b in range(3):
                with dve.Fori(0, 4) as i:
                    for s in (1, 3):
                        use = i + (BR_BASE + b * 4)
                        g_ = gate_s3[:, s // 2, :]
                        m_ = mergedT[:, bass.ds((i * 2 + s // 2) * T, T)]
                        dve.wait_ge(t_done[s], use + 1)
                        dve.wait_ge(t_out[s - 1], use + 1)
                        dve.tensor_tensor(g_, bank(s), g_, ALU.mult).then_inc(t_out[s], 1)
                        dve.wait_ge(t_out[s], use + 1)
                        if b == 0:
                            dve.tensor_copy(m_, g_).then_inc(gated[s // 2], 1)
                        else:
                            dve.tensor_tensor(m_, m_, g_, ALU.add).then_inc(gated[s // 2], 1)
            dve.wait_ge(xa_in, 16)
            for b in range(2):
                for t in range(TT):
                    dve.wait_ge(n_done[t], 6 + b)
                    c_ = slice(b * BANK, (b + 1) * BANK)
                    dve.tensor_tensor(h3[:, t, c_], bank(4 + t), xa3[:, t, c_], ALU.add).then_inc(n_out[t], 1)
            dve.wait_ge(h_rooted, 1)
            link(dve.reciprocal(rstd[:, S_H:S_H + TT], roots[:, S_H:S_H + TT]))
            for t in range(TT):
                ins = dve.tensor_scalar(hs3[:, t, :], h3[:, t, :], rstd[:, S_H + t:S_H + t + 1], None, ALU.mult)
            ins.then_inc(h_normed, 1)

            def top16(n, width, src, src2, vals, idx):
                def at(x, g):
                    return x[:, g * width:(g + 1) * width]
                for g in range(n):
                    ins = dve.max(vals[:, g * 16:g * 16 + 8], at(src, g))
                link(ins)
                for g in range(n):
                    dve.max_index(idx[:, g * 16:g * 16 + 8], vals[:, g * 16:g * 16 + 8], at(src, g))
                    ins = dve.match_replace(at(src2, g), vals[:, g * 16:g * 16 + 8], at(src, g), NEG)
                link(ins)
                for g in range(n):
                    ins = dve.max(vals[:, g * 16 + 8:g * 16 + 16], at(src2, g))
                link(ins)
                for g in range(n):
                    ins = dve.max_index(idx[:, g * 16 + 8:g * 16 + 16], vals[:, g * 16 + 8:g * 16 + 16], at(src2, g))
                return ins

            def first_lists(t):
                dve.wait_ge(score_out, t + 1)
                link(top16(2 * PH, NKEYS, sc3[:, t % 2, :], top_in, top_v, top_i))
                dve.tensor_copy(lists[t % 2].top, top_i).then_inc(score_used, 1)
                v_ = top_v.rearrange("p (h s i) -> p h s i", s=2, i=TOPK)
                link(dve.tensor_tensor(cand.rearrange("p (h i j) -> p h i j", i=TOPK, j=TOPK),
                                       v_[:, :, 0, :].unsqueeze(3).broadcast_to([P, PH, TOPK, TOPK]),
                                       v_[:, :, 1, :].unsqueeze(2).broadcast_to([P, PH, TOPK, TOPK]), ALU.add))

            def second_lists(t):
                L = lists[t % 2]
                link(top16(PH, TOPK * TOPK, cand, cand2, best_v, best_c))
                b_ = best_v.rearrange("p (h r) -> p h r", r=TOPK)
                dve.tensor_tensor(L.gate.rearrange("p (h r) -> p h r", r=TOPK), b_,
                                  b_[:, :, 0:1].broadcast_to([P, PH, TOPK]), ALU.subtract).then_inc(cand_top, 1)
                dve.tensor_scalar(best_i, best_c, 4, None, ALU.logical_shift_right)
                link(dve.tensor_scalar(best_j, best_c, 15, None, ALU.bitwise_and))
                dve.tensor_copy(L.best[0], best_i)
                link(dve.tensor_copy(L.best[1], best_j))
                for n in range(2):
                    ins = dve.tensor_tensor(pick[n].rearrange("p (q i) -> p q i", i=TOPK), spread(L.best[n], P, TOPK),
                                            iota_top[:, :].unsqueeze(1).broadcast_to([P, P, TOPK]), ALU.is_equal)
                ins.then_inc(idx_ready, 1)

            def finish_lists(t):
                L = lists[t % 2]
                dve.wait_ge(pick_done, t + 1)
                for n in range(2):
                    dve.tensor_reduce(L.out[:, n, :], pick[n].rearrange("p (q i) -> p q i", i=TOPK), AX.X, ALU.add)
                dve.wait_ge(cand_exp, t + 1)
                e_ = L.gate.rearrange("p (h r) -> p h r", r=TOPK)
                link(dve.tensor_reduce(g_sum, e_, AX.X, ALU.add))
                link(dve.reciprocal(g_rec, g_sum))
                dve.tensor_tensor(L.out[:, 2, :].rearrange("p (h r) -> p h r", r=TOPK), e_, spread(g_rec, PH, TOPK),
                                  ALU.mult).then_inc(list_ready, 1)

            def take_lists(t):
                c_ = slice(t * P, (t + 1) * P)
                dve.wait_ge(list_turned, t + 1)
                dve.tensor_copy(e_bf[:, 0:2, c_], bank(2)[:, 0:2 * P].rearrange("p (n t) -> p n t", t=P))
                link(dve.tensor_copy(e_bf[:, 2, c_], bank(2)[:, 2 * P:3 * P]))
                dve.tensor_tensor(e_bf[:, 3, c_], bank(2)[:, 2 * P:3 * P], e_bf[:, 2, c_],
                                  ALU.subtract).then_inc(list_out, 1)

            dve.wait_ge(hi_split, 1)
            dve.tensor_tensor(x_hl[:, 2048:4096].bitcast(BF16), hT, x_hl[:, 0:2048].bitcast(BF16),
                              ALU.subtract).then_inc(x_split, 1)
            for t in range(TT):
                first_lists(t)
                if t >= 1:
                    finish_lists(t - 1)
                second_lists(t)
                if t >= 1:
                    take_lists(t - 1)
            finish_lists(TT - 1)
            take_lists(TT - 1)
            dve.wait_ge(list_out, TT)
            dve.wait_ge(const_made, 4)

            def one_hots(g, i):
                s, t0 = i % 2, g * GT
                at_least(dve, gate_done, g - 1)
                def rows_of(n):
                    return e_rows.bitcast(BF16)[:, bass.ds(t0 + n * T, GT)].unsqueeze(1).broadcast_to([P, NKEYS, GT])
                dve.tensor_tensor(ohb[:, 3 * s, :, :], iota3, rows_of(0), ALU.is_equal)
                at_least(dve, oh_ready, g)
                dve.tensor_tensor(ohb[:, 6, :, :], iota3, rows_of(1), ALU.is_equal).then_inc(e2_ready, 1)
                dve.wait_ge(e2_ready, g + 1)
                dve.tensor_tensor(ohb[:, 3 * s + 1, :, :], ohb[:, 6, :, :], rows_of(2), ALU.mult)
                dve.tensor_tensor(ohb[:, 3 * s + 2, :, :], ohb[:, 6, :, :], rows_of(3), ALU.mult).then_inc(oh_ready, 1)

            for i in range(2):
                one_hots(i, i)
            with dve.Fori(1, T // GT // 2) as j:
                for i in range(2):
                    one_hots(j * 2 + i, i)

            def low_u(n, s):
                dve.wait_ge(u_hi, n + 1)
                dve.tensor_tensor(uhl[:, s % 2, 1, :], ur[:, s, :], uhl[:, s % 2, 0, :], ALU.subtract).then_inc(u_lo, 1)

            def prepare(c, par, q, slot):
                if q == 0:
                    dve.wait_ge(g_read[par], c * 8 + (16 - 8 * par) if not isinstance(c, int) else (c // 2 + 1) * 16)
                at_least(dve, w_lo, c * CH + q - 1)
                dve.tensor_tensor(wf[:, q % 2, :].rearrange("p (b t) -> p b t", t=BLK),
                                  acts3[:, slot, :].rearrange("p (b t) -> p b t", t=BLK), g4[:, par, :, q, :],
                                  ALU.mult).then_inc(w_full, 1)
                dve.wait_ge(v_hi, c * CH + q + 1)
                dve.tensor_tensor(vhl[:, par, q, 1, :], vr[:, q, :], vhl[:, par, q, 0, :],
                                  ALU.subtract).then_inc(v_lo, 1)
                dve.wait_ge(w_hi, c * CH + q + 1)
                dve.tensor_tensor(whl[:, par, q, 1, :], wf[:, q % 2, :], whl[:, par, q, 0, :],
                                  ALU.subtract).then_inc(w_lo, 1)

            def flush(c, q):
                dve.wait_ge(down_done, c * CH + q + 1)
                at_least(dve, flushed, (c - 1) * CH + q + 1)
                dve.tensor_tensor(h3[:, q, :], bank(4 + 2 * (q % 2), 2), h3[:, q, :], ALU.add).then_inc(flushed, 1)

            for s in range(2):
                dve.wait_ge(block_stored[s], 16 * NBLK // 2)
            for q in range(CH):
                dve.wait_ge(gelu_done, q + 1)
                prepare(0, 0, q, q)

            def chunks(o, with_u, prep_last=True):
                for i in range(AHEAD):
                    c = o * AHEAD + i
                    for q in range(CH):
                        if with_u:
                            low_u(o * NPRE + (NPRE + i * CH + q), q)
                        if prep_last or i < AHEAD - 1:
                            dve.wait_ge(gelu_done, (c + 1) * CH + q + 1)
                            prepare(c + 1, (i + 1) % 2, q, (i + 1) % AHEAD * CH + q)
                        if q > 0:
                            flush(c, q - 1)
                        elif not (isinstance(c, int) and c == 0):
                            flush(c - 1, CH - 1)

            dve.wait_ge(u_lo, NPRE)
            chunks(0, True)
            with dve.Fori(1, NCH // AHEAD - 1) as o:
                chunks(o, True)
            chunks(NCH // AHEAD - 1, False, prep_last=False)
            flush(NCH - 1, CH - 1)


def layouts(I):
    def f(n):
        return np.asarray(I[n])

    def cols(v):
        return v.reshape(-1, P).T

    def t_blocks(w):
        k, g = w.shape[0] // P, w.shape[1] // P
        return w.reshape(k, P, g, P).transpose(2, 1, 0, 3)

    def n_blocks(w):
        k, b = w.shape[0] // P, w.shape[1] // BANK
        return w.reshape(k, P, b, BANK).transpose(2, 1, 0, 3)

    w = f("w_in")[0]
    parts = np.split(w, np.cumsum([512] * 6 + [MLH, MLH, 512, 512]), axis=1)
    sq, sk, sv, mq, mk, mv, wi, wf, mo, eq, wg = parts
    conv_w = f("conv_w")[0].reshape(4, 8, P).transpose(2, 1, 0).reshape(P, 32)
    par = [cols(f("g_mix")[0]), cols(f("mem_norm_g")[0]), cols(f("g_ffn")[0]), cols(f("b_gate")[0]), conv_w,
           cols(f("conv_b")[0]), cols(f("ml_norm_g")[0]), cols(f("q_norm_g")[0]), cols(f("k_norm_g")[0])]
    keys = np.stack([f("peer_k1")[0], f("peer_k2")[0]], axis=1)
    L = {
        "x": f("x")[0], "mem": f("mem")[0], "cols": np.concatenate(par, axis=1),
        "bif": np.stack([f("b_igate")[0], f("b_fgate")[0]], axis=1),
        "w_t": t_blocks(np.concatenate([sq, sk, mq, mk], axis=1)),
        "w_n": n_blocks(np.concatenate([sv, mv, mo, eq], axis=1)),
        "w_if": np.concatenate([wi, wf], axis=1).reshape(KD, P, 8).transpose(1, 0, 2),
        "w_kv": n_blocks(f("w_mem_kv")[0]),
        "w_gate": t_blocks(wg),
        "w_br": np.concatenate([t_blocks(f(n)[0]) for n in ("w_sb_o", "w_ml_o", "w_mem_o")]),
        "w_out": n_blocks(f("w_out")[0]),
        "w_pq": t_blocks(f("w_peer_q")[0]),
        "keysT": keys.transpose(3, 0, 1, 2).reshape(P, 2 * PH, NKEYS),
        "u": f("peer_u")[0].reshape(NKEYS, NKEYS, KD, P).transpose(1, 3, 2, 0).reshape(NKEYS, P, D),
        "v": f("peer_v")[0].reshape(NKEYS, NKEYS, D).transpose(1, 0, 2),
    }
    return {n: np.ascontiguousarray(a) for n, a in L.items()}


def kernel(**inputs):
    import concourse.bacc as bacc
    from concourse.bass_utils import run_bass_kernel_spmd

    nc = bacc.Bacc("TRN2", target_bir_lowering=False, num_devices=1)
    arrays = layouts(inputs)
    aps = {n: nc.dram_tensor(f"in_{n}", a.shape, mybir.dt.from_np(a.dtype), kind="ExternalInput").ap()
           for n, a in arrays.items()}
    out = nc.dram_tensor("out_h", (T, D), F32, kind="ExternalOutput").ap()
    gates_dram = nc.dram_tensor("gates", (NBLK, P, NKEYS * BLK), F32, kind="Internal").ap()
    build(nc, aps, out, gates_dram)
    r = run_bass_kernel_spmd(nc, [{f"in_{n}": a for n, a in arrays.items()}], core_ids=[0])
    return r.results[0]["out_h"].reshape(1, T, D)
```

```python
from contextlib import ExitStack

import concourse.bass as bass
import numpy as np
from concourse import mybir

F32 = mybir.dt.float32
F32R = mybir.dt.float32r
BF16 = mybir.dt.bfloat16
U32 = mybir.dt.uint32
ALU = mybir.AluOpType
ACT = mybir.ActivationFunctionType
AX = mybir.AxisListType

P = 128
T = 512
TT = T // P
D = 1024
KD = D // P
MEM = 256
MT = MEM // P
SBH, SBD = 8, 64
MLH = 4
NH = 4
HD = 128
BANK = 512
CAUSAL_AT = [0, 512, 1024, 896]
CAUSAL = 1280
EPS = 1e-6
HD_SCALE = HD ** -0.5
PH = 8
TOPK = 16
NKEYS = 128
NEG = -3.0e38
GT = 8
BLK = 32
NBLK = T // BLK
CH = 4
NCH = NKEYS // CH
AHEAD = 8
RING = AHEAD * CH
N_TOP, N_GATE, N_PRE = 28, 60, 64

I_T, I_IF, I_N, I_KV, I_G, I_BR, I_OUT, I_PQ = 0, 16, 18, 34, 42, 66, 78, 86
ITEMS = 102
PARTS = ((0, 0), (0, 1), (1, 0))

PICK_AFTER, EXP_AFTER, TURN_AFTER = (5, 11, 16, 22), (4, 9, 15, 21), (9, 15, 21, 26)

C_MIX, C_MEM, C_FFN, C_BGATE, C_CONVW, C_CONVB, C_MLG, C_QG, C_KG, NCOLS = 0, 8, 16, 24, 48, 80, 88, 89, 90, 91


def at_least(eng, sem, value):
    if isinstance(value, int) and value <= 0:
        return
    eng.wait_ge(sem, value)


def build(nc, A, out, gates_dram, pre_dram, acts_dram):
    ctx = ExitStack()
    with ctx:
        def sb(name, cols, dt=F32, rows=P):
            return ctx.enter_context(nc.sbuf_tensor(name, [rows, cols], dt))

        def sem(name):
            return ctx.enter_context(nc.semaphore(name))

        ident = sb("ident", P)
        neg_tri = sb("neg_tri", P)
        neg_ones = sb("neg_ones", P)
        iota_top = sb("iota_top", TOPK)
        eps_col = sb("eps_col", 1)
        cols = sb("cols", NCOLS)
        qg_scaled = sb("qg_scaled", 1)
        bif = sb("bif", 2, rows=4)
        sums = sb("sums", 64)
        roots = sb("roots", 64)
        rstd = sb("rstd", 64)
        key_cols = sb("key_cols", 32)
        den = sb("den", 32)

        STORE = 52240
        place = {}

        def carve(name, at, size, dt=F32):
            assert at + size <= STORE, (name, at + size)
            with ExitStack() as held:
                if at:
                    held.enter_context(nc.sbuf_tensor("before_" + name, [P, at], F32))
                place[name] = held.enter_context(nc.sbuf_tensor(name, [P, size], dt))
            return place[name][:, :]

        def carve_r(name, at, size):
            return carve(name, at, size, F32R)

        xs = carve("xs", 0, 4096)
        mems = carve("mems", 4096, 2048)
        xT_r = carve_r("xT_r", 6144, 8192)
        w_raw = carve("w_raw", 14336, 4096)
        w_r = carve_r("w_r", 18432, 4096)
        projT = carve("projT", 22528, 8192)
        sb_v = carve("sb_v", 30720, 2048)
        ml_v = carve("ml_v", 32768, TT * MLH * (HD + 1))
        ml_o = carve("ml_o", 34832, 2048)
        mem_q = carve("mem_q", 36880, 2048)
        y_sbT = carve("y_sbT", 38928, 2048)
        y_mlT = carve("y_mlT", 40976, 2048)
        y_memT = carve("y_memT", 43024, 2048)
        rows = carve("rows", 40976, 4096)
        work = carve("work", 45072, 5120)
        memT_r = carve_r("memT_r", 46096, 4096)
        sel = carve("sel", 50192, 512)[0:4, :]
        mem_qT = carve("mem_qT", 0, 2048)
        mem_kT = carve("mem_kT", 2048, 1024)
        mem_k = carve("mem_k", 3072, 1024)
        mem_v = carve("mem_v", 4096, 1024)
        qk_squares = carve("qk_squares", 0, 3072)
        pre_stage = carve("pre_stage", 5120, 1024)
        y_ml = carve("y_ml", 22528, 2048)
        squares = carve("squares", 24576, 2048)
        mergedT = carve("mergedT", 22528, 4096)
        x_again = carve("x_again", 26624, 4096)
        y_r = carve_r("y_r", 30720, 12288)
        gate_s = carve("gate_s", 45072, 4096)
        merged_r = carve_r("merged_r", 30720, 8192)
        h_res = carve("h_res", 0, 4096)
        x_hl = carve("x_hl", 4096, 4096)
        uraw = carve("uraw", 10240, 4096)
        u_hl = carve("u_hl", 8192, 2048)
        vraw = carve("vraw", 14336, 4096)
        acts = carve("acts", 18432, 16384)
        LATE = 34816
        hT_r = carve_r("hT_r", LATE, 8192)
        h_scaled = carve("h_scaled", 22528, 4096)
        junk = carve("junk", LATE + 8192, 1024)
        qryT = carve("qryT", 26624, 2048)
        keysT = carve("keysT", 28672, 2048)
        scores = carve("scores", 30720, 1024)
        top_in = carve("top_in", 31744, 512)
        cand = carve("cand", LATE, 4096)
        cand_in = carve("cand_in", LATE + 4096, 2048)
        picks = carve("picks", LATE + 8192, 4096)
        top_small = carve("top_small", LATE + 12288, 3200)
        top_lists = carve("top_lists", 32256, 2048)
        stage = carve("stage", LATE, 8192)
        act_stage = carve("act_stage", LATE + 10240, 2048)
        e_rows = carve("e_rows", LATE + 16384, 1024)
        onehots = carve("onehots", 14336, 3584)
        iota_exp = carve("iota_exp", 17920, 512)
        v_hl = carve("v_hl", LATE, 8192)
        g_in = carve("g_in", LATE + 8192, 4096)
        w_f = carve("w_f", LATE + 12288, 1024)
        w_hl = carve("w_hl", LATE + 13312, 4096)

        xs3 = xs.rearrange("p (t d) -> p t d", d=D)
        mems3 = mems.rearrange("p (t d) -> p t d", d=D)
        def parts(x, k, t):
            return x.rearrange("p (w k t) -> p w k t", w=2, k=k, t=t)

        xr4 = parts(xT_r, KD, T)
        mr4 = parts(memT_r, KD, MEM)
        gr4 = parts(merged_r, KD, T)
        hr4 = parts(hT_r, KD, T)
        h3 = h_res.rearrange("p (t d) -> p t d", d=D)
        hs3 = h_scaled.rearrange("p (t d) -> p t d", d=D)
        xa3 = x_again.rearrange("p (t d) -> p t d", d=D)
        raw3 = w_raw.rearrange("p (s c) -> p s c", c=D)
        wr4 = w_r.rearrange("p (s w c) -> p s w c", s=2, w=2)
        projT3 = projT.rearrange("p (g t) -> p g t", t=T)
        mergedT3 = mergedT.rearrange("p (g t) -> p g t", t=T)
        qryT3 = qryT.rearrange("p (g t) -> p g t", t=T)
        keysT3 = keysT.rearrange("p (g k) -> p g k", k=NKEYS)
        sb_v3 = sb_v.rearrange("p (t c) -> p t c", c=512)
        ml_v4 = ml_v.rearrange("p (t h c) -> p t h c", t=TT, c=HD + 1)
        ml_o3 = ml_o.rearrange("p (t c) -> p t c", c=512)
        mem_q3 = mem_q.rearrange("p (t c) -> p t c", c=512)
        mem_k3 = mem_k.rearrange("p (t c) -> p t c", c=512)
        mem_v3 = mem_v.rearrange("p (t c) -> p t c", c=512)
        mem_qT3 = mem_qT.rearrange("p (h t) -> p h t", t=T)
        mem_kT3 = mem_kT.rearrange("p (h t) -> p h t", t=MEM)
        y_ml4 = y_ml.rearrange("p (t h c) -> p t h c", t=TT, c=HD)
        y_ml3 = y_ml.rearrange("p (t c) -> p t c", c=512)
        yT = [y.rearrange("p (g t) -> p g t", t=T) for y in (y_sbT, y_mlT, y_memT)]
        gate_s3 = gate_s.rearrange("p (s c) -> p s c", c=2 * T)
        conv_out = work[:, 0:1024].rearrange("p (s t) -> p s t", t=T)

        lk = [work[:, 0:CAUSAL], work[:, CAUSAL:2 * CAUSAL]]
        aw = [work[:, 2 * CAUSAL:3 * CAUSAL], work[:, 3 * CAUSAL:4 * CAUSAL]]
        probs = [work[:, 0:1024], work[:, 1024:2048]]
        probsT = work[:, 2048:4096].rearrange("p (s m t) -> p s m t", s=2, t=T)

        def row(n):
            return rows[0:4, n * T:(n + 1) * T]
        r_abs, r_f, r_lf, r_b, r_a, r_max, r_m, r_zero = (row(n) for n in range(8))
        sel3 = sel.rearrange("p (h c) -> p h c", c=P)

        S_X, S_Q, S_K, S_ML, S_H = 0, 6, 22, 30, 46
        sc3 = scores.rearrange("p (s c) -> p s c", c=TT * NKEYS)
        pick = [picks[:, n * 2048:(n + 1) * 2048] for n in range(2)]
        top_v = top_lists[:, 0:1024].rearrange("p (t c) -> p t c", t=TT)
        top_i = top_lists[:, 1024:2048].bitcast(U32).rearrange("p (t c) -> p t c", t=TT)
        best_v = top_small[:, 512:640]
        best_c = top_small[:, 640:768].bitcast(U32)
        best_i = top_small[:, 768:896].bitcast(U32)
        best_j = top_small[:, 896:1024].bitcast(U32)
        g_sum = top_small[:, 1024:1032]
        g_rec = top_small[:, 1032:1040]

        class Lists:
            def __init__(self, n):
                b = 1152 + n * 1024
                self.top = top_small[:, b:b + 256]
                self.best = [top_small[:, b + 256 + k * P:b + 256 + (k + 1) * P] for k in range(2)]
                self.gate = top_small[:, b + 512:b + 640]
                self.out = top_small[:, b + 640:b + 1024].rearrange("p (s c) -> p s c", c=P)
        lists = [Lists(0), Lists(1)]
        xh, xl = [x_hl[:, n * 2048:(n + 1) * 2048].bitcast(BF16).rearrange("p (k t) -> p k t", t=T) for n in range(2)]
        ur = uraw.rearrange("p (s c) -> p s c", c=D)
        vr = vraw.rearrange("p (s c) -> p s c", c=D)
        uhl = u_hl.bitcast(BF16).rearrange("p (s w c) -> p s w c", s=2, w=2)
        vhl = v_hl.bitcast(BF16).rearrange("p (s n w c) -> p s n w c", s=2, n=CH, w=2)
        whl = w_hl.bitcast(BF16).rearrange("p (s n w t) -> p s n w t", s=2, n=CH, w=2)
        wf = w_f.rearrange("p (s t) -> p s t", t=T)
        g4 = g_in.rearrange("p (s b n t) -> p s b n t", s=2, b=NBLK, n=CH)
        as3 = act_stage.rearrange("p (s t) -> p s t", t=T)
        acts3 = acts.rearrange("p (n t) -> p n t", t=T)
        stage4 = stage.rearrange("p (s k t) -> p s k t", s=2, t=BLK)
        e_bf = e_rows.bitcast(BF16).rearrange("p (n t) -> p n t", t=T)
        ohb = onehots.bitcast(BF16).rearrange("p (n k t) -> p n k t", n=7, t=GT)
        iota3 = iota_exp.bitcast(BF16).rearrange("p (k t) -> p k t", t=GT)

        ps = ctx.enter_context(nc.psum_tensor("ps", [P, 8 * BANK], F32))

        def bank(b, n=1):
            return ps[:, b * BANK:(b + n) * BANK]

        const_set, const_made = sem("const_set"), sem("const_made")
        sel_made = sem("sel_made")
        params_in, keys_in, xa_in = sem("params_in"), sem("keys_in"), sem("xa_in")
        x_in = [sem(f"x_in{i}") for i in range(TT)]
        mem_in = sem("mem_in")
        squared, rooted, scaled = sem("squared"), sem("rooted"), sem("scaled")
        turned, xT_hi, xT_out, memT_hi, memT_out = (
            sem("turned"), sem("xT_hi"), sem("xT_out"), sem("memT_hi"), sem("memT_out"))
        act_step, dve_step, pool_step = sem("act_step"), sem("dve_step"), sem("pool_step")
        w_in = [sem(f"w_in{s}") for s in range(4)]
        w_hi_ready, w_lo_ready, item_done = sem("w_hi_ready"), sem("w_lo_ready"), sem("item_done")
        proj_out, n_out, pq_out, h_out = sem("proj_out"), sem("n_out"), sem("pq_out"), sem("h_out")
        pre_out, sig_done, br_used, gated = sem("pre_out"), sem("sig_done"), sem("br_used"), sem("gated")
        pre_stored = [sem(f"pre_stored{s}") for s in range(2)]
        pre_back = [sem(f"pre_back{s}") for s in range(4)]
        y_hi, y_lo, m_zero, m_hi, m_lo = sem("y_hi"), sem("y_lo"), sem("m_zero"), sem("m_hi"), sem("m_lo")
        if_ln = sem("if_ln")
        rows_made, thr_made, cols_turned, cols_out = sem("rows_made"), sem("thr_made"), sem("cols_turned"), sem("cols_out")
        q_scaled, conv_done, silu_done, sig_o = sem("q_scaled"), sem("conv_done"), sem("silu_done"), sem("sig_o")
        qk_squared, qk_rooted, qk_normed = sem("qk_squared"), sem("qk_rooted"), sem("qk_normed")
        z_ready, ln_ready, keep_ready, keep_masked = sem("z_ready"), sem("ln_ready"), sem("keep_ready"), sem("keep_masked")
        suffix_done, a_ready, a_masked, y_done, y_out = (
            sem("suffix_done"), sem("a_ready"), sem("a_masked"), sem("y_done"), sem("y_out"))
        s_ready, d_ready, e_ready, w_ready, w_masked, num_done, num_out = (
            sem("s_ready"), sem("d_ready"), sem("e_ready"), sem("w_ready"), sem("w_masked"), sem("num_done"),
            sem("num_out"))
        ml_squared, ml_rooted, ml_normed, mlT_done, mlT_out = (
            sem("ml_squared"), sem("ml_rooted"), sem("ml_normed"), sem("mlT_done"), sem("mlT_out"))
        qkT_done, qkT_out = sem("qkT_done"), sem("qkT_out")
        ms_ready, mmax_ready, mexp_ready, mp_ready, mpT_done, mpT_out, my_done, my_out = (
            sem("ms_ready"), sem("mmax_ready"), sem("mexp_ready"), sem("mp_ready"), sem("mpT_done"),
            sem("mpT_out"), sem("my_done"), sem("my_out"))
        h_rooted, h_normed, hT_done, hT_hi, hT_out = (
            sem("h_rooted"), sem("h_normed"), sem("hT_done"), sem("hT_hi"), sem("hT_out"))
        score_done, score_out, score_used = sem("score_done"), sem("score_out"), sem("score_used")
        cand_top, cand_exp, list_ready, list_turned, list_out = (
            sem("cand_top"), sem("cand_exp"), sem("list_ready"), sem("list_turned"), sem("list_out"))
        idx_ready, pick_done = sem("idx_ready"), sem("pick_done")
        oh_ready, e2_ready, gate_done, gate_out = sem("oh_ready"), sem("e2_ready"), sem("gate_done"), sem("gate_out")
        block_stored = [sem(f"block_stored{s}") for s in range(2)]
        act_stored = [sem(f"act_stored{s}") for s in range(4)]
        act_back = [sem(f"act_back{s}") for s in range(4)]
        u_in = [sem(f"u_in{s}") for s in range(4)]
        v_in = [sem(f"v_in{s}") for s in range(4)]
        g_read = [sem(f"g_read{s}") for s in range(2)]
        u_hi, u_lo, u_done, gelu_done = sem("u_hi"), sem("u_lo"), sem("u_done"), sem("gelu_done")
        v_hi, v_lo, w_full, w_hi, w_lo = sem("v_hi"), sem("v_lo"), sem("w_full"), sem("w_hi"), sem("w_lo")
        down_done, flushed, stored = sem("down_done"), sem("flushed"), sem("stored")

        CONSTS = 5

        block = ctx.enter_context(nc.Block())

        @block.gpsimd
        def _(pool):
            pool.memset(ident[:, :], 0.0).then_inc(const_set, 1)
            pool.memset(neg_tri[:, :], -1.0).then_inc(const_set, 1)
            pool.memset(neg_ones[:, :], -1.0).then_inc(const_set, 1)
            pool.memset(eps_col[:, :], EPS).then_inc(const_set, 1)
            pool.memset(ml_v4[:, :, :, HD:HD + 1], 1.0).then_inc(const_set, 1)
            pool.wait_ge(const_set, CONSTS)
            pool.affine_select(out=ident[:, :], in_=ident[:, :], compare_op=ALU.not_equal, fill=1.0, base=0,
                               pattern=[[-1, P]], channel_multiplier=1).then_inc(const_made, 1)
            pool.affine_select(out=neg_tri[:, :], in_=neg_tri[:, :], compare_op=ALU.is_ge, fill=0.0, base=0,
                               pattern=[[-1, P]], channel_multiplier=1).then_inc(const_made, 1)
            pool.iota(iota_top[:, :], pattern=[[1, TOPK]], base=0, channel_multiplier=0,
                      allow_small_or_imprecise_dtypes=True).then_inc(const_made, 1)

            def keep_causal(buf, strict, done):
                for kt in range(TT):
                    block_ = buf[:, CAUSAL_AT[kt]:CAUSAL_AT[kt] + P]
                    ins = pool.affine_select(out=block_, in_=block_, compare_op=ALU.is_gt if strict else ALU.is_ge,
                                             fill=0.0, base=0, pattern=[[1, P]], channel_multiplier=-1)
                ins.then_inc(done, 1)

            def mask_keep(h):
                pool.wait_ge(keep_ready, h + 1)
                keep_causal(lk[h % 2], True, keep_masked)

            def mask_a(h):
                pool.wait_ge(a_ready, h + 1)
                keep_causal(aw[h % 2], True, a_masked)

            def low_ws(base, count):
                def four(o, m):
                    for q in range(m):
                        n = base + q
                        pool.wait_ge(w_hi_ready, o * 4 + (n + 1))
                        pool.tensor_tensor(wr4[:, n % 2, 1, :], raw3[:, n % 4, :], wr4[:, n % 2, 0, :].bitcast(F32),
                                           ALU.subtract).then_inc(w_lo_ready, 1)
                if count >= 4:
                    with pool.Fori(0, count // 4) as o:
                        four(o, 4)
                if count % 4:
                    four(count // 4, count % 4)

            pool.memset(sel, 0.0).then_inc(sel_made, 1)
            pool.wait_ge(sel_made, 1)
            pool.affine_select(out=sel3, in_=sel3, compare_op=ALU.not_equal, fill=1.0, base=0,
                               pattern=[[-1, 4], [0, P]], channel_multiplier=1).then_inc(sel_made, 1)
            low_ws(0, I_G + 2)
            mask_keep(0)
            low_ws(I_G + 2, 1)
            for h in range(SBH):
                if h + 1 < SBH:
                    mask_keep(h + 1)
                mask_a(h)
                low_ws(I_G + 2 * h + 3, 2)
            for h in range(MLH):
                pool.wait_ge(w_ready, h + 1)
                keep_causal(lk[h % 2], False, w_masked)
                if h >= 1:
                    low_ws(I_G + 18 + h, 1)
            low_ws(I_G + 22, 4)

            pool.wait_ge(mlT_done, MLH)
            pool.memset(mergedT, 0.0).then_inc(m_zero, 1)
            low_ws(I_BR + 2, ITEMS - I_BR - 2)
            pool.iota(iota3, pattern=[[1, NKEYS], [0, GT]], base=0, channel_multiplier=0,
                      allow_small_or_imprecise_dtypes=True).then_inc(const_made, 1)

            def low_u(n):
                pool.wait_ge(u_hi, n + 1)
                pool.tensor_tensor(uhl[:, n % 2, 1, :], ur[:, n % 4, :], uhl[:, n % 2, 0, :],
                                   ALU.subtract).then_inc(u_lo, 1)

            def pick_keys(t, n, half):
                pool.wait_ge(idx_ready, t + 1)
                h_ = slice(half * PH // 2, (half + 1) * PH // 2)
                i_ = lists[t % 2].top.rearrange("p (h s i) -> p h s i", s=2, i=TOPK)[:, h_, n, :]
                pk = pick[n].rearrange("p (h r i) -> p h r i", r=TOPK, i=TOPK)[:, h_, :, :]
                pool.tensor_tensor(pk, pk, i_.unsqueeze(2).broadcast_to([P, PH // 2, TOPK, TOPK]),
                                   ALU.mult).then_inc(pick_done, 1)

            for n in range(30):
                low_u(n)
                for t, first in enumerate(PICK_AFTER):
                    if 0 <= n - first < 4:
                        pick_keys(t, (n - first) // 2, (n - first) % 2)
            low_u(30)
            low_u(31)
            with pool.Fori(8, N_PRE // 4) as o:
                for q in range(4):
                    pool.wait_ge(u_hi, o * 4 + (q + 1))
                    pool.tensor_tensor(uhl[:, q % 2, 1, :], ur[:, q, :], uhl[:, q % 2, 0, :],
                                       ALU.subtract).then_inc(u_lo, 1)

        @block.sync
        def _(sp):
            for i in range(TT):
                sp.dma_start(xs3[:, i, :], A["x"][i * P:(i + 1) * P, :]).then_inc(x_in[i], 16)
            sp.dma_start(mems3, A["mem"].rearrange("(t p) d -> p t d", p=P)).then_inc(mem_in, 16)
            sp.dma_start(cols[:, :], A["cols"]).then_inc(params_in, 16)
            sp.dma_start(bif[:, :], A["bif"]).then_inc(params_in, 16)

            def load_item(n, s):
                at_least(sp, w_lo_ready, n - 3)
                sp.dma_start(raw3[:, s, :], A["w"][n]).then_inc(w_in[s], 16)

            for s in range(4):
                load_item(s, s)
            with sp.Fori(1, (I_G + 2) // 4) as i:
                for s in range(4):
                    load_item(i * 4 + s, s)
            load_item(I_G + 2, 0)
            load_item(I_G + 3, 1)
            for m in range(24):
                load_item(I_G + m + 4, (I_G + m) % 4)
                sp.wait_ge(pre_out, m + 1)
                sp.dma_start(pre_dram[m // 2, :, (m % 2) * T:(m % 2 + 1) * T],
                             pre_stage[:, (m % 2) * T:(m % 2 + 1) * T]).then_inc(pre_stored[m % 2], 16)
            sp.wait_ge(my_done, NH)
            for s in range(2):
                sp.wait_ge(pre_stored[s], 12 * 16)

            def load_pre(p):
                at_least(sp, gated, 2 * p - 6)
                sp.dma_start(gate_s3[:, p % 4, :], pre_dram[p]).then_inc(pre_back[p % 4], 16)

            for p in range(4):
                load_pre(p)
            sp.dma_start(xa3, A["x"].rearrange("(t p) d -> p t d", p=P)).then_inc(xa_in, 16)
            for p in range(4, 12):
                load_item(I_BR + p, (I_BR + p) % 4)
                load_pre(p)
            def load_items(first, last):
                with sp.Fori((first - I_OUT) // 4, (last - I_OUT) // 4) as i:
                    for s in range(4):
                        load_item(i * 4 + (I_OUT + s), (I_OUT + s) % 4)

            load_items(I_OUT, I_PQ + 4)
            sp.wait_ge(h_out, 2 * TT)
            sp.dma_start(keysT3, A["keysT"]).then_inc(keys_in, 16)
            load_items(I_PQ + 4, ITEMS)

            def load_u(n, s):
                at_least(sp, u_lo, n - 3)
                sp.dma_start(ur[:, s, :], A["u"][n]).then_inc(u_in[s], 16)

            def load_v(n, s):
                at_least(sp, v_lo, n - 3)
                sp.dma_start(vr[:, s, :], A["v"][n]).then_inc(v_in[s], 16)

            def load_g(c, s):
                at_least(sp, w_full, (c - 1) * CH)
                sp.dma_start(g_in[:, s * 2048:(s + 1) * 2048].rearrange("p (b n) -> p b n", b=NBLK), gates_dram[:, :, bass.ds(c * CH * BLK, CH * BLK)].rearrange(
                    "b p n -> p b n")).then_inc(g_read[s], 16)

            sp.wait_ge(item_done, I_OUT)
            for n in range(4):
                load_u(n, n)
            for n in range(4, RING):
                load_u(n, n % 4)
            def spill(n, s):
                sp.wait_ge(gelu_done, n + 1)
                sp.dma_start(acts_dram[n - RING], as3[:, s, :]).then_inc(act_stored[s], 16)

            def gate_blocks(j):
                for m in range(8):
                    load_u(j * 8 + (N_TOP + 4 + m), m % 4)
                    if m >= 4 or not isinstance(j, int):
                        spill(j * 8 + (N_TOP + m), m % 4)
                    if m % 2:
                        b = m // 2
                        sp.wait_ge(gate_out, j * 16 + 4 * (b + 1))
                        sp.dma_start(gates_dram[j * 4 + b], stage[:, b % 2 * NKEYS * BLK:(b % 2 + 1) * NKEYS * BLK]
                                     ).then_inc(block_stored[b % 2], 16)

            gate_blocks(0)
            with sp.Fori(1, NBLK // 4) as j:
                gate_blocks(j)
            sp.wait_ge(gate_done, T // GT)
            for n in range(4):
                load_v(n, n)
            spill(N_GATE, 0)
            load_u(N_PRE, 0)
            for s in range(2):
                sp.wait_ge(block_stored[s], 16 * NBLK // 2)
            load_g(0, 0)
            for q in range(1, 4):
                spill(N_GATE + q, q)
                load_u(N_PRE + q, q)
            for s in range(4):
                sp.wait_ge(act_stored[s], 16 * (N_PRE - RING) // 4)
            load_g(1, 1)
            def load_chunk(j, s, with_a=False, with_u=False):
                for q in range(CH):
                    if with_a:
                        sp.wait_ge(w_full, j * 8 + (s * CH + q + 1))
                        sp.dma_start(acts[:, bass.ds(j * 8 * T + (s * CH + q) * T, T)],
                                     acts_dram[j * 8 + (s * CH + q)]).then_inc(act_back[q], 16)
                    if with_u:
                        load_u(j * 8 + (RING + (s + 1) * CH + q), q)
                    load_v(j * 8 + ((s + 1) * CH + q), q)
                load_g(j * 2 + (s + 2), s)

            half = AHEAD // 2
            last = (NCH - AHEAD) // 2 - 1
            with sp.Fori(0, half) as j:
                for s in range(2):
                    load_chunk(j, s, with_a=True)
            with sp.Fori(half, last) as j:
                for s in range(2):
                    load_chunk(j, s, with_u=True)
            load_chunk(last, 0, with_u=True)
            load_chunk(last, 1)
            for c in range(NCH - AHEAD, NCH - 1):
                for q in range(CH):
                    load_v((c + 1) * CH + q, q)
                if c + 2 < NCH:
                    load_g(c + 2, c % 2)
            for t in range(TT):
                sp.wait_ge(flushed, (NCH - 1) * CH + t + 1)
                sp.dma_start(out[t * P:(t + 1) * P, :], h3[:, t, :]).then_inc(stored, 16)
            sp.wait_ge(stored, 16 * TT)

        @block.tensor
        def _(pe):
            def turn(dst, src, rows_=P):
                return pe.transpose(dst, src, ident[0:rows_, 0:rows_])

            def take_item(n):
                pe.wait_ge(w_lo_ready, n + 1)

            def t_item(n, s, b, act, landed=None):
                take_item(n)
                for k in range(KD):
                    if landed is not None:
                        pe.wait_ge(landed, k + 1)
                    for ww, wa in PARTS:
                        ins = pe.matmul(bank(b), wr4[:, s, ww, k * P:(k + 1) * P], act[:, wa, k, :],
                                        start=k == 0 and ww + wa == 0, stop=k == KD - 1 and ww == 1)
                ins.then_inc(item_done, 1)

            def n_item(n, s, j, b0, act, tiles, landed=None):
                take_item(n)
                for k in range(2):
                    if landed is not None:
                        pe.wait_ge(landed, (2 * j + k) // 2 + 1)
                    for t in range(tiles):
                        for ww, wa in PARTS:
                            ins = pe.matmul(bank(b0 + t), act[:, wa, 2 * j + k, t * P:(t + 1) * P],
                                            wr4[:, s, ww, k * BANK:(k + 1) * BANK],
                                            start=j == 0 and k == 0 and ww + wa == 0,
                                            stop=j == 3 and k == 1 and ww == 1, skip_group_check=True)
                ins.then_inc(item_done, 1)

            pe.wait_ge(const_set, CONSTS)
            pe.wait_ge(const_made, 3)
            pe.wait_ge(scaled, TT)
            for k in range(KD):
                for i in range(TT):
                    ins = turn(bank(k)[:, i * P:(i + 1) * P], xs3[:, i, k * P:(k + 1) * P])
                ins.then_inc(turned, 1)
            for n in range(4):
                t_item(n, n % 2, n, xr4, landed=xT_out if n == 0 else None)
            pe.wait_ge(scaled, TT + MT)
            for k in range(KD):
                for i in range(MT):
                    ins = turn(bank(4 + k // 2)[:, (k % 2 * MT + i) * P:(k % 2 * MT + i + 1) * P],
                               mems3[:, i, k * P:(k + 1) * P])
                ins.then_inc(turned, 1)
            with pe.Fori(1, I_IF // 4) as i:
                for s in range(4):
                    pe.wait_ge(proj_out, i * 4 + (s - 3))
                    t_item(i * 4 + s, s % 2, s, xr4)
            for g in range(2):
                pe.wait_ge(proj_out, I_IF - 3 + g)
                t_item(I_IF + g, g, g, xr4)
            for b in range(4):
                if b == 0:
                    pe.wait_ge(memT_out, KD)
                elif b == 1:
                    pe.wait_ge(proj_out, I_IF)
                    pe.wait_ge(rows_made, 1)
                elif b >= 2:
                    pe.wait_ge(n_out, (b - 1) * TT)
                for j in range(4):
                    n = I_N + 4 * b + j
                    n_item(n, n % 2, j, 4 * (1 - b % 2), xr4, TT)
            pe.wait_ge(n_out, 3 * TT)
            for b in range(2):
                for j in range(4):
                    n = I_KV + 4 * b + j
                    n_item(n, n % 2, j, 4 + MT * b, mr4, MT)
            pe.wait_ge(thr_made, 1)
            pe.wait_ge(n_out, 4 * TT)
            for i, r in enumerate((r_a, r_m)):
                for t in range(TT):
                    ins = turn(bank(2)[:, (i * TT + t) * 4:(i * TT + t) * 4 + 4], r[:, t * P:(t + 1) * P], 4)
            ins.then_inc(cols_turned, 1)
            pe.wait_ge(cols_out, 1)
            pe.wait_ge(n_out, 5 * TT)

            def causal(s, kt, q0=None):
                q0 = kt if q0 is None else q0
                at = s * 3 * BANK + CAUSAL_AT[kt] + (q0 - kt) * P
                return ps[:, at:at + T - q0 * P]

            def part(buf, kt, q0=None, q1=TT):
                q0 = kt if q0 is None else q0
                return buf[:, CAUSAL_AT[kt] + (q0 - kt) * P:CAUSAL_AT[kt] + (q1 - kt) * P]

            def sb_scores(h):
                at_least(pe, a_ready, h - 1)
                r = slice(SBD * (h % 2), SBD * (h % 2) + SBD)
                for kt in range(TT):
                    ins = pe.matmul(causal(h % 2, kt), projT3[r, 4 + h // 2, kt * P:(kt + 1) * P],
                                    projT3[r, h // 2, kt * P:T], start=kt != 3, stop=False, skip_group_check=True)
                ins.then_inc(z_ready, 1)

            def sb_suffix(h):
                pe.wait_ge(keep_masked, h + 1)
                for kt in range(TT):
                    for k2 in range(kt, TT):
                        ins = pe.matmul(causal(h % 2, kt, k2), neg_tri[:, :] if k2 == kt else neg_ones[:, :],
                                        part(lk[h % 2], k2), start=False, stop=k2 == TT - 1, skip_group_check=True)
                ins.then_inc(suffix_done, 1)

            def sb_values(h):
                pe.wait_ge(a_masked, h + 1)
                at_least(pe, y_out, h - 1)
                r = slice(SBD * (h % 2), SBD * (h % 2) + SBD)
                for kt in range(TT):
                    ins = pe.matmul(bank(6)[r, kt * P:T], sb_v3[:, kt, h * SBD:(h + 1) * SBD],
                                    part(aw[h % 2], kt), start=kt == 0, stop=kt == TT - 1)
                ins.then_inc(y_done, 1)

            def gate_item(m):
                at_least(pe, pre_out, m)
                n = I_G + m
                t_item(n, n % 2, 7, xr4)

            sb_scores(0)
            gate_item(0)
            for h in range(SBH):
                sb_suffix(h)
                if h + 1 < SBH:
                    sb_scores(h + 1)
                gate_item(2 * h + 1)
                if h >= 1:
                    sb_values(h - 1)
                gate_item(2 * h + 2)
            sb_values(SBH - 1)

            pe.wait_ge(silu_done, 8)
            pe.wait_ge(sel_made, 2)
            pe.wait_ge(y_out, SBH)

            def ml_scores(h):
                at_least(pe, num_out, h - 1)
                at_least(pe, d_ready, h)
                pe.matmul(bank(6), sel3[:, h, :], r_max, start=True, stop=True)
                for kt in range(TT):
                    ins = pe.matmul(causal(h % 2, kt), projT3[:, 12 + h, kt * P:(kt + 1) * P],
                                    projT3[:, 8 + h, kt * P:T], start=kt != 3, stop=True, skip_group_check=True)
                ins.then_inc(s_ready, 1)

            def ml_values(h):
                pe.wait_ge(w_masked, h + 1)
                for t in range(TT):
                    at = (h % 2 * 3 + t // 2) * BANK + (t % 2) * (HD + 1)
                    for kt in range(t + 1):
                        ins = pe.matmul(ps[:, at:at + HD + 1], part(lk[h % 2], kt, t, t + 1), ml_v4[:, kt, h, :],
                                        start=kt == 0, stop=kt == t)
                ins.then_inc(num_done, 1)

            ml_scores(0)
            ml_scores(1)
            gate_item(17)
            for h in range(MLH):
                ml_values(h)
                if h + 2 < MLH:
                    ml_scores(h + 2)
                gate_item(18 + h)

            pe.wait_ge(qk_normed, 1)
            pe.wait_ge(num_out, MLH)
            for h in range(NH):
                for t in range(TT):
                    ins = turn(bank(h)[:, t * P:(t + 1) * P], mem_q3[:, t, h * HD:(h + 1) * HD])
                ins.then_inc(qkT_done, 1)
            for h in range(NH):
                for t in range(MT):
                    ins = turn(bank(4 + h // 2)[:, (h % 2 * MT + t) * P:(h % 2 * MT + t + 1) * P],
                               mem_k3[:, t, h * HD:(h + 1) * HD])
            ins.then_inc(qkT_done, 1)
            gate_item(22)
            pe.wait_ge(qkT_out, NH + 1)

            def mem_scores(h):
                at_least(pe, mexp_ready, h - 1)
                for t in range(TT):
                    at = (h % 2) * 2 * BANK + t * MEM
                    ins = pe.matmul(ps[:, at:at + MEM], mem_qT3[:, h, t * P:(t + 1) * P], mem_kT3[:, h, :],
                                    start=True, stop=True)
                ins.then_inc(ms_ready, 1)

            mem_scores(0)
            for h in range(NH):
                if h + 1 < NH:
                    mem_scores(h + 1)
                if h == 0:
                    gate_item(23)
                pe.wait_ge(mp_ready, h + 1)
                at_least(pe, mpT_out, h)
                for m in range(MT):
                    for t in range(TT):
                        ins = turn(bank(4 + m)[:, t * P:(t + 1) * P],
                                   probs[h % 2][:, t * MEM + m * P:t * MEM + (m + 1) * P])
                ins.then_inc(mpT_done, 1)
                pe.wait_ge(mpT_out, h + 1)
                at_least(pe, my_out, h)
                for m in range(MT):
                    ins = pe.matmul(bank(6), mem_v3[:, m, h * HD:(h + 1) * HD], probsT[:, h % 2, m, :],
                                    start=m == 0, stop=m == MT - 1)
                ins.then_inc(my_done, 1)
            pe.wait_ge(ml_normed, 1)
            pe.wait_ge(mexp_ready, NH)
            for h in range(MLH):
                for t in range(TT):
                    ins = turn(bank(h)[:, t * P:(t + 1) * P], y_ml4[:, t, h, :])
                ins.then_inc(mlT_done, 1)

            def branch(b):
                pe.wait_ge(y_lo, b + 1)
                for i in range(4):
                    n, b0 = I_BR + i, (4 + 2 * i) % 8
                    take_item(b * 4 + n)
                    if isinstance(b, int) and b == 0:
                        pe.wait_ge(*((mpT_out, NH), (my_out, NH), (mlT_out, 2), (mlT_out, MLH))[i])
                    else:
                        pe.wait_ge(br_used, b * 8 + (2 * i - 6))
                    for e in range(2):
                        for k in range(4):
                            for ww, wa in PARTS:
                                at = (wa * 4 + k) * T
                                act = y_r[:, at:at + T] if isinstance(b, int) else y_r[:, bass.ds(b * 8 * T + at, T)]
                                ins = pe.matmul(bank(b0 + e), wr4[:, n % 2, ww, (e * 4 + k) * P:(e * 4 + k + 1) * P],
                                                act, start=k == 0 and ww + wa == 0, stop=k == 3 and ww == 1)
                    ins.then_inc(item_done, 1)

            branch(0)
            with pe.Fori(1, 3) as b:
                branch(b)
            pe.wait_ge(gated, 24)
            for b in range(2):
                for j in range(4):
                    n = I_OUT + 4 * b + j
                    n_item(n, n % 2, j, 4 * b, gr4, TT, landed=m_lo if b == 0 else None)

            pe.wait_ge(h_normed, 1)
            for k in range(KD):
                for i in range(TT):
                    ins = turn(bank(k)[:, i * P:(i + 1) * P], hs3[:, i, k * P:(k + 1) * P])
                ins.then_inc(hT_done, 1)
            def key_scores(g, s):
                pe.wait_ge(pq_out, g + 1)
                at_least(pe, score_out, g - 1)
                for t in range(TT):
                    ins = pe.matmul(bank(4 + s % 2)[:, t * P:(t + 1) * P], qryT3[:, s, t * P:(t + 1) * P],
                                    keysT3[:, g, :] if isinstance(g, int) else keysT[:, bass.ds(g * NKEYS, NKEYS)],
                                    start=True, stop=True)
                ins.then_inc(score_done, 1)

            pe.wait_ge(keys_in, 16)
            for n in range(4):
                if n:
                    pe.wait_ge(hT_out, n + 1)
                t_item(I_PQ + n, n % 2, n, hr4, landed=hT_out if n == 0 else None)
                if n:
                    key_scores(n - 1, n - 1)
            with pe.Fori(1, 4) as i:
                for s in range(4):
                    pe.wait_ge(pq_out, i * 4 + (s - 3))
                    t_item(i * 4 + (I_PQ + s), s % 2, s, hr4)
                    key_scores(i * 4 + (s - 1), (s - 1) % 4)
            key_scores(15, 3)

            def turn_lists(t):
                pe.wait_ge(list_ready, t + 1)
                at_least(pe, list_out, t)
                for n in range(3):
                    ins = turn(bank(2)[:, n * P:(n + 1) * P], lists[t % 2].out[:, n, :])
                ins.then_inc(list_turned, 1)

            def up(n, s, half=None):
                steps_ = [(k, w) for k in range(KD) for w in PARTS]
                if half is None or half == 0:
                    pe.wait_ge(u_lo, n + 1)
                    at_least(pe, gelu_done, n - 1)
                chosen = range(24) if half is None else range(half * 12, half * 12 + 12)
                for i in chosen:
                    k, (wu, wx) = steps_[i]
                    ins = pe.matmul(bank(s), uhl[:, s, wu, k * P:(k + 1) * P], (xh, xl)[wx][:, k, :],
                                    start=i == 0, stop=i == 23, skip_group_check=True)
                if chosen[-1] == 23:
                    ins.then_inc(u_done, 1)

            def down(c, par, q):
                if q == 0:
                    pe.wait_ge(v_lo, (c + 1) * CH)
                    pe.wait_ge(w_lo, (c + 1) * CH)
                at_least(pe, flushed, c * CH + (q - 1))
                for i in range(CH):
                    for ww, wv in PARTS:
                        for h in range(2):
                            ins = pe.matmul(bank(4 + 2 * (q % 2) + h), whl[:, par, i, ww, q * P:(q + 1) * P],
                                            vhl[:, par, i, wv, h * BANK:(h + 1) * BANK],
                                            start=i == 0 and (ww, wv) == (0, 0), stop=i == CH - 1 and ww == 1)
                ins.then_inc(down_done, 1)

            for n in range(N_TOP):
                up(n, n % 2)
                if n in TURN_AFTER:
                    turn_lists(TURN_AFTER.index(n))

            def gate_group(g, s):
                pe.wait_ge(oh_ready, g + 1)
                at_least(pe, gate_out, g - 1)
                for q in range(GT):
                    for w in range(2):
                        at = (2 + 4 * s) * BANK + q * P
                        ins = pe.matmul(ps[:, at:at + P], ohb[:, 3 * s, :, q], ohb[:, 3 * s + 1 + w, :, q],
                                        start=w == 0, stop=w == 1)
                ins.then_inc(gate_done, 1)

            def gate_blocks(j):
                for i in range(16):
                    gate_group(j * 16 + i, i % 2)
                    up(j * 8 + (N_TOP + i // 2), (i // 2) % 2, i % 2)

            gate_blocks(0)
            with pe.Fori(1, NBLK // 4) as j:
                gate_blocks(j)
            for n in range(N_GATE, N_PRE):
                up(n, n % 2)

            def chunk_pair(j, with_u):
                for par in range(2):
                    for q in range(CH):
                        if with_u:
                            up(j * 8 + (RING + par * CH + q), q % 2)
                        down(j * 2 + par, par, q)

            pe.wait_ge(gate_out, T // GT)
            chunk_pair(0, False)
            with pe.Fori(1, AHEAD // 2) as j:
                chunk_pair(j, False)
            with pe.Fori(AHEAD // 2, (NCH - AHEAD) // 2) as j:
                chunk_pair(j, True)
            with pe.Fori((NCH - AHEAD) // 2, NCH // 2) as j:
                chunk_pair(j, False)

        @block.scalar
        def _(act):
            steps = [0]

            def link(ins):
                steps[0] += 1
                ins.then_inc(act_step, 1)
                act.wait_ge(act_step, steps[0])

            act.wait_ge(const_set, CONSTS)
            for i in range(TT):
                act.wait_ge(x_in[i], 16)
                link(act.activation(work[:, 0:D], xs3[:, i, :], ACT.Square, accum_out=sums[:, i:i + 1]))
            act.activation(roots[:, S_X:TT], sums[:, S_X:TT], ACT.Sqrt, bias=eps_col[:, :],
                           scale=1.0 / D).then_inc(rooted, 1)
            act.wait_ge(mem_in, 16)
            for i in range(MT):
                link(act.activation(work[:, 0:D], mems3[:, i, :], ACT.Square, accum_out=sums[:, TT + i:TT + i + 1]))
            act.activation(roots[:, TT:S_Q], sums[:, TT:S_Q], ACT.Sqrt, bias=eps_col[:, :],
                           scale=1.0 / D).then_inc(rooted, 1)
            def high_w(n, q):
                act.wait_ge(w_in[q], (n // 4 + 1) * 16 if isinstance(n, int) else n * 4 + (16 - 4 * q))
                at_least(act, item_done, n - 1)
                act.activation(wr4[:, q % 2, 0, :], raw3[:, q, :], ACT.Copy).then_inc(w_hi_ready, 1)

            high_w(0, 0)
            high_w(1, 1)
            act.wait_ge(params_in, 32)
            for k in range(KD):
                act.wait_ge(turned, k + 1)
                act.activation(xr4[:, 0, k, :], bank(k), ACT.Copy,
                               scale=cols[:, C_MIX + k:C_MIX + k + 1]).then_inc(xT_hi, 1)
            for n in range(4):
                act.wait_ge(item_done, n + 1)
                act.activation(projT3[:, n, :], bank(n), ACT.Copy, scale=SBD ** -0.5).then_inc(proj_out, 1)
                high_w(n + 2, (n + 2) % 4)
            with act.Fori(1, I_IF // 4) as i:
                for s in range(4):
                    act.wait_ge(item_done, i * 4 + (s + 1))
                    act.activation(projT[:, bass.ds((i * 4 + s) * T, T)], bank(s), ACT.Copy).then_inc(proj_out, 1)
                    high_w(i * 4 + (s + 2), (s + 2) % 4)
            high_w(I_N, I_N % 4)
            high_w(I_N + 1, (I_N + 1) % 4)
            act.wait_ge(item_done, I_N)
            link(act.activation(r_abs, bank(1)[0:4, :], ACT.Abs, bias=bif[:, 1:2]))
            link(act.activation(r_abs, r_abs, ACT.Exp, scale=-1.0))
            act.activation(r_abs, r_abs, ACT.Ln, bias=1.0).then_inc(if_ln, 1)
            for b in range(4):
                for j in range(4):
                    n = I_N + 4 * b + j + 2
                    high_w(n, n % 4)
                    if j >= 2:
                        g = 2 * b + j - 2
                        act.wait_ge(conv_done, g + 1)
                        act.activation(projT3[:, 8 + g, :], conv_out[:, g % 2, :], ACT.Silu).then_inc(silu_done, 1)
            for n in range(I_KV + 2, I_G + 2):
                high_w(n, n % 4)
            act.wait_ge(n_out, 3 * TT)
            act.activation(ml_o, ml_o, ACT.Sigmoid).then_inc(sig_o, 1)
            act.wait_ge(rows_made, 1)
            act.activation(r_m, r_m, ACT.Exp, scale=-1.0).then_inc(thr_made, 1)
            act.wait_ge(qk_squared, 1)
            act.activation(roots[:, S_Q:S_ML], sums[:, S_Q:S_ML], ACT.Sqrt, bias=eps_col[:, :],
                           scale=1.0 / HD).then_inc(qk_rooted, 1)

            def region(s):
                return ps[:, s * 3 * BANK:s * 3 * BANK + CAUSAL]

            def ln_part(h):
                act.wait_ge(z_ready, h + 1)
                at_least(act, suffix_done, h - 1)
                link(act.activation(lk[h % 2], region(h % 2), ACT.Abs))
                link(act.activation(lk[h % 2], lk[h % 2], ACT.Exp, scale=-1.0))
                act.activation(lk[h % 2], lk[h % 2], ACT.Ln, bias=1.0).then_inc(ln_ready, 1)

            def high_ws(*ns):
                for n in ns:
                    high_w(n, n % 4)

            ln_part(0)
            high_ws(I_G + 2)
            for h in range(SBH):
                act.wait_ge(suffix_done, h + 1)
                at_least(act, y_done, h - 1)
                act.activation(aw[h % 2], region(h % 2), ACT.Exp).then_inc(a_ready, 1)
                if h + 1 < SBH:
                    ln_part(h + 1)
                high_ws(I_G + 2 * h + 3, I_G + 2 * h + 4)

            for h in range(MLH):
                act.wait_ge(d_ready, h + 1)
                act.activation(lk[h % 2], lk[h % 2], ACT.Exp, scale=-1.0).then_inc(e_ready, 1)
                if h >= 1:
                    high_ws(I_G + 18 + h)
            high_ws(I_G + 22, I_G + 23)
            act.wait_ge(ml_squared, 1)
            act.activation(roots[:, S_ML:S_H], sums[:, S_ML:S_H], ACT.Sqrt, bias=eps_col[:, :],
                           scale=1.0 / HD).then_inc(ml_rooted, 1)
            act.wait_ge(qk_normed, 1)
            for h in range(NH):
                act.wait_ge(qkT_done, h + 1)
                act.activation(mem_qT3[:, h, :], bank(h), ACT.Copy, scale=qg_scaled[:, 0:1]).then_inc(qkT_out, 1)
            act.wait_ge(qkT_done, NH + 1)
            act.activation(mem_kT, bank(4, 2), ACT.Copy, scale=cols[:, C_KG:C_KG + 1]).then_inc(qkT_out, 1)
            act.wait_ge(y_out, SBH)
            act.activation(y_r[:, 0:2048], y_sbT, ACT.Copy).then_inc(y_hi, 1)
            high_ws(I_G + 24)
            for h in range(NH):
                act.wait_ge(mmax_ready, h + 1)
                at_least(act, mpT_done, h - 1)
                for t in range(TT):
                    at = (h % 2) * 2 * BANK + t * MEM
                    d = 8 + (h % 2) * 4 + t
                    ins = act.activation(probs[h % 2][:, t * MEM:(t + 1) * MEM], ps[:, at:at + MEM], ACT.Exp,
                                         bias=den[:, (h % 2) * 4 + t:(h % 2) * 4 + t + 1], accum_out=den[:, d:d + 1])
                ins.then_inc(mexp_ready, 1)
                act.wait_ge(mpT_done, h + 1)
                at_least(act, my_done, h - 1)
                act.activation(probsT[:, h % 2, :, :], bank(4, 2).rearrange("p (m t) -> p m t", t=T),
                               ACT.Copy).then_inc(mpT_out, 1)
                if h == 0:
                    high_ws(I_G + 25)

            for h in range(MLH):
                act.wait_ge(mlT_done, h + 1)
                act.activation(yT[1][:, h, :], bank(h), ACT.Copy, scale=cols[:, C_MLG:C_MLG + 1]).then_inc(mlT_out, 1)

            act.wait_ge(mlT_out, MLH)
            act.activation(y_r[:, 4096:6144], y_mlT, ACT.Copy).then_inc(y_hi, 1)
            act.wait_ge(my_out, NH)
            act.wait_ge(y_lo, 2)
            act.activation(y_r[:, 8192:10240], y_memT, ACT.Copy).then_inc(y_hi, 1)

            with act.Fori(0, 3) as b:
                for i in range(4):
                    act.wait_ge(pre_back[i], b * 16 + 16)
                    act.activation(gate_s3[:, i, :], gate_s3[:, i, :], ACT.Sigmoid).then_inc(sig_done, 1)
                    high_w(b * 4 + (I_BR + i + 2), (I_BR + i + 2) % 4)
            act.wait_ge(gated, 24)
            for q in range(4):
                act.activation(merged_r[:, q * D:(q + 1) * D], mergedT[:, q * D:(q + 1) * D], ACT.Copy).then_inc(m_hi, 1)
            for n in range(I_OUT + 2, I_PQ + 2):
                high_w(n, n % 4)

            for t in range(TT):
                act.wait_ge(h_out, TT + t + 1)
                link(act.activation(junk, h3[:, t, :], ACT.Square, accum_out=sums[:, S_H + t:S_H + t + 1]))
            act.activation(roots[:, S_H:S_H + TT], sums[:, S_H:S_H + TT], ACT.Sqrt, bias=eps_col[:, :],
                           scale=1.0 / D).then_inc(h_rooted, 1)
            for k in range(KD):
                act.wait_ge(hT_done, k + 1)
                g_ = cols[:, C_FFN + k:C_FFN + k + 1]
                act.activation(hr4[:, 0, k, :], bank(k), ACT.Copy, scale=g_).then_inc(hT_hi, 1)
                act.activation(xh[:, k, :], bank(k), ACT.Copy, scale=g_).then_inc(hT_hi, 1)

            def score_copy(g, s):
                act.wait_ge(score_done, g + 1)
                at_least(act, score_used, g - 1)
                act.activation(sc3[:, s % 2, :], bank(4 + s % 2), ACT.Copy).then_inc(score_out, 1)

            def queries(i, last=False):
                for s in range(4):
                    act.wait_ge(item_done, i * 4 + (I_PQ + s + 1))
                    at_least(act, score_done, i * 4 + (s - 3))
                    act.activation(qryT3[:, s, :], bank(s), ACT.Copy).then_inc(pq_out, 1)
                    if not last or s < 2:
                        high_w(i * 4 + (I_PQ + s + 2), (I_PQ + s + 2) % 4)
                    if not (isinstance(i, int) and i == 0 and s == 0):
                        score_copy(i * 4 + (s - 1), s - 1)

            queries(0)
            with act.Fori(1, 3) as i:
                queries(i)
            queries(3, last=True)
            score_copy(15, 15)

            def high_u(n, s):
                act.wait_ge(u_in[s], (n - s) * 4 + 16 if isinstance(n, int) else n * 4 + (16 - 4 * s))
                at_least(act, u_done, n - 1)
                act.activation(uhl[:, s % 2, 0, :], ur[:, s, :], ACT.Copy).then_inc(u_hi, 1)

            def gelu(n, s, dst, first=False):
                act.wait_ge(u_done, n + 1)
                if not first:
                    at_least(act, w_full, n - (RING - 1))
                act.activation(dst, bank(s % 2), ACT.Gelu).then_inc(gelu_done, 1)

            def gelu_out(n, s, before):
                at_least(act, act_stored[s], before * 16)
                gelu(n, s, as3[:, s, :], first=True)

            def gate_exp(t):
                act.wait_ge(cand_top, t + 1)
                act.activation(lists[t % 2].gate, lists[t % 2].gate, ACT.Exp).then_inc(cand_exp, 1)

            high_u(0, 0)
            high_u(1, 1)
            for n in range(N_TOP):
                gelu(n, n % 2, acts3[:, n, :])
                high_u(n + 2, (n + 2) % 4)
                if n in EXP_AFTER:
                    gate_exp(EXP_AFTER.index(n))

            def gate_copy(g, i):
                act.wait_ge(gate_done, g + 1)
                act.activation(stage4[:, i // 4 % 2, :, (i % 4) * GT:(i % 4 + 1) * GT],
                               bank(2 + 4 * (i % 2), 2).rearrange("p (q k) -> p k q", k=NKEYS),
                               ACT.Copy).then_inc(gate_out, 1)

            def gate_blocks(j):
                for i in range(16):
                    if i % 4 == 0:
                        at_least(act, block_stored[i // 4 % 2], j * 32 + (i // 8) * 16)
                    gate_copy(j * 16 + i, i)
                    if i % 2:
                        m = i // 2
                        n = j * 8 + (N_TOP + m)
                        if isinstance(j, int) and m < 4:
                            gelu(n, m, acts3[:, n, :], first=True)
                        else:
                            gelu_out(n, m % 4, j * 2 + (m // 4 - 1))
                        high_u(n + 2, (m + 2) % 4)

            act.wait_ge(list_ready, TT)
            act.wait_ge(list_turned, TT)
            gate_blocks(0)
            with act.Fori(1, NBLK // 4) as j:
                gate_blocks(j)

            def prepare(c, par, q):
                act.wait_ge(v_in[q], c * 16 + 16)
                if q == 0:
                    at_least(act, down_done, (c - 1) * CH)
                act.activation(vhl[:, par, q, 0, :], vr[:, q, :], ACT.Copy).then_inc(v_hi, 1)
                act.wait_ge(w_full, c * CH + q + 1)
                act.activation(whl[:, par, q, 0, :], wf[:, q % 2, :], ACT.Copy).then_inc(w_hi, 1)

            for n in range(N_GATE, N_PRE):
                gelu_out(n, n % 4, (n - RING) // 4)
                high_u(n + 2, (n + 2) % 4)
                if n == N_PRE - 3:
                    for s in range(2):
                        act.wait_ge(block_stored[s], 16 * NBLK // 2)
                if n >= N_PRE - 3:
                    prepare(0, 0, n - N_PRE + 3)
            prepare(0, 0, 3)

            def chunk_pair(j, with_u=False, first=0, last=False):
                for i in range(2):
                    for q in range(CH):
                        if not (last and not with_u and i == 1):
                            prepare(j * 2 + (i + 1), (i + 1) % 2, q)
                        if with_u:
                            n = j * 8 + (RING + i * CH + q)
                            slot = j * 8 + (i * CH + q - first * CH)
                            gelu(n, q % 2, acts3[:, slot, :] if isinstance(j, int) else acts[:, bass.ds(slot * T, T)])
                            if not (last and i == 1 and q >= 2):
                                high_u(n + 2, (q + 2) % 4)

            with act.Fori(0, 4) as j:
                chunk_pair(j)
            with act.Fori(4, 8) as j:
                chunk_pair(j, with_u=True, first=8)
            with act.Fori(8, 11) as j:
                chunk_pair(j, with_u=True, first=16)
            chunk_pair(11, with_u=True, first=16, last=True)
            with act.Fori(12, 15) as j:
                chunk_pair(j)
            chunk_pair(15, last=True)

        @block.vector
        def _(dve):
            steps = [0]

            def link(ins):
                steps[0] += 1
                ins.then_inc(dve_step, 1)
                dve.wait_ge(dve_step, steps[0])

            dve.wait_ge(rooted, 1)
            link(dve.reciprocal(rstd[:, S_X:TT], roots[:, S_X:TT]))
            for i in range(TT):
                dve.tensor_scalar(xs3[:, i, :], xs3[:, i, :], rstd[:, i:i + 1], None, ALU.mult).then_inc(scaled, 1)
            dve.wait_ge(rooted, 2)
            link(dve.reciprocal(rstd[:, TT:S_Q], roots[:, TT:S_Q]))
            for i in range(MT):
                dve.tensor_scalar(mems3[:, i, :], mems3[:, i, :], rstd[:, TT + i:TT + i + 1], None,
                                  ALU.mult).then_inc(scaled, 1)
            dve.wait_ge(params_in, 32)
            dve.tensor_scalar(qg_scaled[:, :], cols[:, C_QG:C_QG + 1], HD_SCALE, None, ALU.mult).then_inc(q_scaled, 1)
            for k in range(KD):
                dve.wait_ge(xT_hi, k + 1)
                dve.scalar_tensor_tensor(out=xr4[:, 1, k, :], in0=bank(k), scalar=cols[:, C_MIX + k:C_MIX + k + 1],
                                         in1=xr4[:, 0, k, :].bitcast(F32), op0=ALU.mult,
                                         op1=ALU.subtract).then_inc(xT_out, 1)
            for k in range(KD):
                g_ = cols[:, C_MEM + k:C_MEM + k + 1]
                dve.wait_ge(turned, KD + k // 2 * 2 + 2)
                src = bank(4 + k // 2)[:, k % 2 * MEM:(k % 2 + 1) * MEM]
                dve.tensor_scalar(mr4[:, 0, k, :], src, g_, None, ALU.mult).then_inc(memT_hi, 1)
                dve.wait_ge(memT_hi, k + 1)
                dve.scalar_tensor_tensor(out=mr4[:, 1, k, :], in0=src, scalar=g_,
                                         in1=mr4[:, 0, k, :].bitcast(F32), op0=ALU.mult,
                                         op1=ALU.subtract).then_inc(memT_out, 1)

            def conv(g):
                dve.wait_ge(proj_out, 8 + g + 1)
                at_least(dve, silu_done, g - 1)
                x_, y_ = projT3[:, 8 + g, :], conv_out[:, g % 2, :]
                w = [cols[:, C_CONVW + g * 4 + k:C_CONVW + g * 4 + k + 1] for k in range(4)]
                link(dve.tensor_scalar(y_, x_, w[3], cols[:, C_CONVB + g:C_CONVB + g + 1], ALU.mult, ALU.add))
                for k in range(3):
                    lag = 3 - k
                    ins = dve.scalar_tensor_tensor(out=y_[:, lag:T], in0=x_[:, 0:T - lag], scalar=w[k],
                                                   in1=y_[:, lag:T], op0=ALU.mult, op1=ALU.add)
                    if k < 2:
                        link(ins)
                ins.then_inc(conv_done, 1)

            dve.wait_ge(if_ln, 1)
            dve.memset(r_zero, 0.0)
            link(dve.tensor_scalar(r_f, bank(1)[0:4, :], bif[:, 1:2], 0.0, ALU.add, ALU.min))
            link(dve.tensor_tensor(r_lf, r_f, r_abs, ALU.subtract))
            link(dve.tensor_tensor_scan(r_b, r_lf, r_zero, 0.0, ALU.add, ALU.add))
            link(dve.scalar_tensor_tensor(out=r_a, in0=bank(0)[0:4, :], scalar=bif[:, 0:1], in1=r_b,
                                          op0=ALU.add, op1=ALU.subtract))
            link(dve.tensor_tensor_scan(r_max, r_a, r_a, 0.0, ALU.max, ALU.max))
            dve.tensor_tensor(r_m, r_b, r_max, ALU.add).then_inc(rows_made, 1)
            natural = [sb_v3, None, ml_o3, mem_q3]
            for b in range(4):
                conv(2 * b)
                conv(2 * b + 1)
                dve.wait_ge(item_done, I_N + 4 * b + 4)
                for t in range(TT):
                    src = bank(4 * (1 - b % 2) + t)
                    if b == 1:
                        ins = dve.tensor_copy(ml_v4[:, t, :, 0:HD], src.rearrange("p (h c) -> p h c", c=HD))
                    else:
                        ins = dve.tensor_copy(natural[b][:, t, :], src)
                    ins.then_inc(n_out, 1)
            for t in range(TT):
                dve.wait_ge(item_done, I_KV + 4 * (t // MT) + 4)
                dst = mem_k3 if t < MT else mem_v3
                dve.tensor_copy(dst[:, t % MT, :], bank(4 + t)).then_inc(n_out, 1)
            dve.wait_ge(n_out, 5 * TT)
            dve.tensor_tensor(qk_squares[:, 0:2048], mem_q, mem_q, ALU.mult)
            link(dve.tensor_tensor(qk_squares[:, 2048:3072], mem_k, mem_k, ALU.mult))
            dve.tensor_reduce(sums[:, S_Q:S_ML], qk_squares.rearrange("p (g c) -> p g c", c=HD), AX.X,
                              ALU.add).then_inc(qk_squared, 1)
            dve.wait_ge(qk_rooted, 1)
            link(dve.reciprocal(rstd[:, S_Q:S_ML], roots[:, S_Q:S_ML]))

            def spread(col, n, m):
                return col.unsqueeze(2).broadcast_to([P, n, m])

            q_ = mem_q.rearrange("p (g c) -> p g c", c=HD)
            k_ = mem_k.rearrange("p (g c) -> p g c", c=HD)
            dve.tensor_tensor(q_, q_, spread(rstd[:, S_Q:S_K], 16, HD), ALU.mult)
            dve.tensor_tensor(k_, k_, spread(rstd[:, S_K:S_ML], 8, HD), ALU.mult).then_inc(qk_normed, 1)
            dve.wait_ge(cols_turned, 1)
            dve.tensor_copy(key_cols[:, :], bank(2)[:, 0:32]).then_inc(cols_out, 1)

            def region(s):
                return ps[:, s * 3 * BANK:s * 3 * BANK + CAUSAL]

            def keep(h):
                dve.wait_ge(ln_ready, h + 1)
                dve.scalar_tensor_tensor(out=lk[h % 2], in0=region(h % 2), scalar=0.0, in1=lk[h % 2],
                                         op0=ALU.max, op1=ALU.add).then_inc(keep_ready, 1)

            def take_y(h):
                r = slice(SBD * (h % 2), SBD * (h % 2) + SBD)
                dve.wait_ge(y_done, h + 1)
                dve.tensor_copy(yT[0][r, h // 2, :], bank(6)[r, :]).then_inc(y_out, 1)

            def take_gate(m):
                dve.wait_ge(item_done, I_G + m + 1)
                at_least(dve, pre_stored[m % 2], m // 2 * 16)
                dve.tensor_scalar(pre_stage[:, (m % 2) * T:(m % 2 + 1) * T], bank(7),
                                  cols[:, C_BGATE + m:C_BGATE + m + 1], None, ALU.add).then_inc(pre_out, 1)

            keep(0)
            take_gate(0)
            for h in range(SBH):
                take_gate(2 * h + 1)
                if h + 1 < SBH:
                    keep(h + 1)
                if h >= 1:
                    take_y(h - 1)
                take_gate(2 * h + 2)
            take_y(SBH - 1)

            def decay(h):
                dve.wait_ge(s_ready, h + 1)
                at_least(dve, num_done, h - 1)
                for kt in range(TT):
                    ins = dve.tensor_scalar(lk[h % 2][:, CAUSAL_AT[kt]:CAUSAL_AT[kt] + T - kt * P],
                                            bank(6)[:, kt * P:T],
                                            key_cols[:, kt * 4 + h:kt * 4 + h + 1], 0.0, ALU.subtract, ALU.max)
                ins.then_inc(d_ready, 1)

            def weigh(h):
                dve.wait_ge(e_ready, h + 1)
                dve.scalar_tensor_tensor(out=lk[h % 2], in0=region(h % 2), scalar=HD_SCALE, in1=lk[h % 2],
                                         op0=ALU.mult, op1=ALU.mult).then_inc(w_ready, 1)

            def divide(h):
                dve.wait_ge(num_done, h + 1)
                base = h % 2 * 3 * BANK
                d_ = ps[:, base:base + 2 * BANK].rearrange("p (a b) -> p a b", b=BANK)[:, :, HD:2 * HD + 2:HD + 1]
                m_ = key_cols[:, 16 + h:32:4].rearrange("p (a b) -> p a b", b=2)
                o_ = den[:, 0:4].rearrange("p (a b) -> p a b", b=2)
                link(dve.scalar_tensor_tensor(out=o_, in0=d_, scalar=-1.0, in1=m_, op0=ALU.mult, op1=ALU.max))
                link(dve.tensor_tensor(o_, o_, d_, ALU.max))
                link(dve.reciprocal(den[:, 4:8], den[:, 0:4]))
                for t in range(TT):
                    at = (h % 2 * 3 + t // 2) * BANK + (t % 2) * (HD + 1)
                    ins = dve.tensor_scalar(y_ml4[:, t, h, :], ps[:, at:at + HD], den[:, 4 + t:5 + t], None, ALU.mult)
                ins.then_inc(num_out, 1)

            decay(0)
            decay(1)
            weigh(0)
            weigh(1)
            take_gate(17)
            for h in range(MLH):
                divide(h)
                if h + 2 < MLH:
                    decay(h + 2)
                    weigh(h + 2)
                take_gate(18 + h)
            dve.wait_ge(num_out, MLH)
            link(dve.tensor_tensor(squares, y_ml, y_ml, ALU.mult))
            dve.tensor_reduce(sums[:, S_ML:S_H], squares.rearrange("p (g c) -> p g c", c=HD), AX.X,
                              ALU.add).then_inc(ml_squared, 1)
            dve.wait_ge(ml_rooted, 1)
            link(dve.reciprocal(rstd[:, S_ML:S_H], roots[:, S_ML:S_H]))
            y_ = y_ml.rearrange("p (g c) -> p g c", c=HD)
            link(dve.tensor_tensor(y_, y_, spread(rstd[:, S_ML:S_H], 16, HD), ALU.mult))
            dve.wait_ge(sig_o, 1)
            dve.tensor_tensor(y_ml, y_ml, ml_o, ALU.mult).then_inc(ml_normed, 1)

            take_gate(22)
            dve.wait_ge(y_hi, 1)
            dve.tensor_tensor(y_r[:, 2048:4096], y_sbT, y_r[:, 0:2048].bitcast(F32), ALU.subtract).then_inc(y_lo, 1)

            for h in range(NH):
                n4 = (h % 2) * 4
                dve.wait_ge(ms_ready, h + 1)
                dve.tensor_reduce(den[:, n4:n4 + 4], ps[:, (h % 2) * 2 * BANK:(h % 2 + 1) * 2 * BANK].rearrange(
                    "p (t m) -> p t m", m=MEM), AX.X, ALU.max, negate=True).then_inc(mmax_ready, 1)
                if h == 0:
                    take_gate(23)
                dve.wait_ge(mexp_ready, h + 1)
                link(dve.reciprocal(den[:, 16 + n4:20 + n4], den[:, 8 + n4:12 + n4]))
                p_ = probs[h % 2].rearrange("p (t m) -> p t m", m=MEM)
                dve.tensor_tensor(p_, p_, spread(den[:, 16 + n4:20 + n4], 4, MEM), ALU.mult).then_inc(mp_ready, 1)
                dve.wait_ge(my_done, h + 1)
                dve.tensor_copy(yT[2][:, h, :], bank(6)).then_inc(my_out, 1)

            for b in (1, 2):
                dve.wait_ge(y_hi, b + 1)
                dve.tensor_tensor(y_r[:, b * 4096 + 2048:(b + 1) * 4096], (y_sbT, y_mlT, y_memT)[b],
                                  y_r[:, b * 4096:b * 4096 + 2048].bitcast(F32), ALU.subtract).then_inc(y_lo, 1)
            dve.wait_ge(m_zero, 1)
            with dve.Fori(0, 3) as b:
                for i in range(4):
                    dve.wait_ge(item_done, b * 4 + (I_BR + i + 1))
                    dve.wait_ge(sig_done, b * 4 + (i + 1))
                    for e in range(2):
                        g = 2 * i + e
                        g_, m_ = gate_s3[:, i, e * T:(e + 1) * T], mergedT3[:, g, :]
                        dve.tensor_tensor(g_, bank((4 + g) % 8), g_, ALU.mult).then_inc(br_used, 1)
                    for e in range(2):
                        g = 2 * i + e
                        g_, m_ = gate_s3[:, i, e * T:(e + 1) * T], mergedT3[:, g, :]
                        dve.wait_ge(br_used, b * 8 + (g + 1))
                        dve.tensor_tensor(m_, m_, g_, ALU.add).then_inc(gated, 1)
            for q in range(4):
                dve.wait_ge(m_hi, q + 1)
                dve.tensor_tensor(merged_r[:, 4096 + q * D:4096 + (q + 1) * D], mergedT[:, q * D:(q + 1) * D],
                                  merged_r[:, q * D:(q + 1) * D].bitcast(F32), ALU.subtract).then_inc(m_lo, 1)
            dve.wait_ge(xa_in, 16)
            for b in range(2):
                dve.wait_ge(item_done, I_OUT + 4 * b + 4)
                for t in range(TT):
                    c_ = slice(b * BANK, (b + 1) * BANK)
                    dve.tensor_tensor(h3[:, t, c_], bank(4 * b + t), xa3[:, t, c_], ALU.add).then_inc(h_out, 1)
            dve.wait_ge(h_rooted, 1)
            link(dve.reciprocal(rstd[:, S_H:S_H + TT], roots[:, S_H:S_H + TT]))
            for t in range(TT):
                ins = dve.tensor_scalar(hs3[:, t, :], h3[:, t, :], rstd[:, S_H + t:S_H + t + 1], None, ALU.mult)
            ins.then_inc(h_normed, 1)
            for k in range(KD):
                g_ = cols[:, C_FFN + k:C_FFN + k + 1]
                dve.wait_ge(hT_hi, 2 * k + 2)
                dve.scalar_tensor_tensor(out=hr4[:, 1, k, :], in0=bank(k), scalar=g_, in1=hr4[:, 0, k, :].bitcast(F32),
                                         op0=ALU.mult, op1=ALU.subtract)
                dve.scalar_tensor_tensor(out=xl[:, k, :], in0=bank(k), scalar=g_, in1=xh[:, k, :],
                                         op0=ALU.mult, op1=ALU.subtract).then_inc(hT_out, 1)

            def top16(vals, idx, width, src, src2):
                n = len(vals)
                def at(x, g):
                    return x[:, g * width:(g + 1) * width]
                for g in range(n):
                    ins = dve.max(vals[g][:, 0:8], at(src, g))
                link(ins)
                for g in range(n):
                    dve.max_index(idx[g][:, 0:8], vals[g][:, 0:8], at(src, g))
                    ins = dve.match_replace(at(src2, g), vals[g][:, 0:8], at(src, g), NEG)
                link(ins)
                for g in range(n):
                    ins = dve.max(vals[g][:, 8:16], at(src2, g))
                link(ins)
                for g in range(n):
                    ins = dve.max_index(idx[g][:, 8:16], vals[g][:, 8:16], at(src2, g))
                return ins

            def first_lists(g):
                dve.wait_ge(score_out, g + 1)
                def halves(x):
                    return [x[:, t, g * 16:(g + 1) * 16] for t in range(TT)]
                top16(halves(top_v), halves(top_i), NKEYS, sc3[:, g % 2, :], top_in).then_inc(score_used, 1)

            def candidates(t):
                L = lists[t % 2]
                dve.tensor_copy(L.top, top_i[:, t, :])
                v_ = top_v[:, t, :].rearrange("p (h s i) -> p h s i", s=2, i=TOPK)
                link(dve.tensor_tensor(cand[:, t % 2 * 2048:(t % 2 + 1) * 2048].rearrange(
                    "p (h i j) -> p h i j", i=TOPK, j=TOPK),
                                       v_[:, :, 0, :].unsqueeze(3).broadcast_to([P, PH, TOPK, TOPK]),
                                       v_[:, :, 1, :].unsqueeze(2).broadcast_to([P, PH, TOPK, TOPK]), ALU.add))

            def second_lists(t):
                L = lists[t % 2]
                candidates(t)
                def heads(x):
                    return [x[:, g * 16:(g + 1) * 16] for g in range(PH)]
                link(top16(heads(best_v), heads(best_c), TOPK * TOPK, cand[:, t % 2 * 2048:(t % 2 + 1) * 2048], cand_in))

            def winners(t):
                L = lists[t % 2]
                b_ = best_v.rearrange("p (h r) -> p h r", r=TOPK)
                dve.tensor_tensor(L.gate.rearrange("p (h r) -> p h r", r=TOPK), b_,
                                  b_[:, :, 0:1].broadcast_to([P, PH, TOPK]), ALU.subtract).then_inc(cand_top, 1)
                dve.tensor_scalar(best_i, best_c, 4, None, ALU.logical_shift_right)
                link(dve.tensor_scalar(best_j, best_c, 15, None, ALU.bitwise_and))
                dve.tensor_copy(L.best[0], best_i)
                link(dve.tensor_copy(L.best[1], best_j))
                for n in range(2):
                    ins = dve.tensor_tensor(pick[n].rearrange("p (q i) -> p q i", i=TOPK), spread(L.best[n], P, TOPK),
                                            iota_top[:, :].unsqueeze(1).broadcast_to([P, P, TOPK]), ALU.is_equal)
                ins.then_inc(idx_ready, 1)

            def finish_lists(t):
                L = lists[t % 2]
                dve.wait_ge(pick_done, 4 * t + 4)
                for n in range(2):
                    dve.tensor_reduce(L.out[:, n, :], pick[n].rearrange("p (q i) -> p q i", i=TOPK), AX.X, ALU.add)
                dve.wait_ge(cand_exp, t + 1)
                e_ = L.gate.rearrange("p (h r) -> p h r", r=TOPK)
                link(dve.tensor_reduce(g_sum, e_, AX.X, ALU.add))
                link(dve.reciprocal(g_rec, g_sum))
                dve.tensor_tensor(L.out[:, 2, :].rearrange("p (h r) -> p h r", r=TOPK), e_, spread(g_rec, PH, TOPK),
                                  ALU.mult).then_inc(list_ready, 1)

            def take_lists(t):
                c_ = slice(t * P, (t + 1) * P)
                dve.wait_ge(list_turned, t + 1)
                dve.tensor_copy(e_bf[:, 0:2, c_], bank(2)[:, 0:2 * P].rearrange("p (n t) -> p n t", t=P))
                link(dve.tensor_copy(e_bf[:, 2, c_], bank(2)[:, 2 * P:3 * P]))
                dve.tensor_tensor(e_bf[:, 3, c_], bank(2)[:, 2 * P:3 * P], e_bf[:, 2, c_],
                                  ALU.subtract).then_inc(list_out, 1)

            for g in range(2 * PH):
                first_lists(g)
            dve.wait_ge(score_used, 2 * PH)
            for t in range(TT):
                second_lists(t)
                if t >= 1:
                    finish_lists(t - 1)
                winners(t)
                if t >= 1:
                    take_lists(t - 1)
            finish_lists(TT - 1)
            take_lists(TT - 1)
            dve.wait_ge(list_out, TT)
            dve.wait_ge(const_made, 4)

            def one_hots(g, i):
                s, t0 = i % 2, g * GT
                at_least(dve, gate_done, g - 1)
                def rows_of(n):
                    return e_rows.bitcast(BF16)[:, bass.ds(t0 + n * T, GT)].unsqueeze(1).broadcast_to([P, NKEYS, GT])
                dve.tensor_tensor(ohb[:, 3 * s, :, :], iota3, rows_of(0), ALU.is_equal)
                at_least(dve, oh_ready, g)
                dve.tensor_tensor(ohb[:, 6, :, :], iota3, rows_of(1), ALU.is_equal).then_inc(e2_ready, 1)
                dve.wait_ge(e2_ready, g + 1)
                dve.tensor_tensor(ohb[:, 3 * s + 1, :, :], ohb[:, 6, :, :], rows_of(2), ALU.mult)
                dve.tensor_tensor(ohb[:, 3 * s + 2, :, :], ohb[:, 6, :, :], rows_of(3), ALU.mult).then_inc(oh_ready, 1)

            for i in range(2):
                one_hots(i, i)
            with dve.Fori(1, T // GT // 2) as j:
                for i in range(2):
                    one_hots(j * 2 + i, i)

            def low_u(n, s):
                dve.wait_ge(u_hi, n + 1)
                dve.tensor_tensor(uhl[:, s % 2, 1, :], ur[:, s, :], uhl[:, s % 2, 0, :], ALU.subtract).then_inc(u_lo, 1)

            def prepare(c, par, q, tile):
                if q == 0:
                    dve.wait_ge(g_read[par], c * 8 + (16 - 8 * par))
                at_least(dve, w_lo, c * CH + q - 1)
                dve.tensor_tensor(wf[:, q % 2, :].rearrange("p (b t) -> p b t", t=BLK),
                                  tile.rearrange("p (b t) -> p b t", t=BLK), g4[:, par, :, q, :],
                                  ALU.mult).then_inc(w_full, 1)
                dve.wait_ge(v_hi, c * CH + q + 1)
                dve.tensor_tensor(vhl[:, par, q, 1, :], vr[:, q, :], vhl[:, par, q, 0, :],
                                  ALU.subtract).then_inc(v_lo, 1)
                dve.wait_ge(w_hi, c * CH + q + 1)
                dve.tensor_tensor(whl[:, par, q, 1, :], wf[:, q % 2, :], whl[:, par, q, 0, :],
                                  ALU.subtract).then_inc(w_lo, 1)

            def flush(c, q):
                dve.wait_ge(down_done, c * CH + q + 1)
                at_least(dve, flushed, (c - 1) * CH + q + 1)
                dve.tensor_tensor(h3[:, q, :], bank(4 + 2 * (q % 2), 2), h3[:, q, :], ALU.add).then_inc(flushed, 1)

            for s in range(2):
                dve.wait_ge(block_stored[s], 16 * NBLK // 2)
            for q in range(CH):
                dve.wait_ge(gelu_done, q + 1)
                prepare(0, 0, q, acts3[:, q, :])

            def chunk_pair(j, seg, with_u=False, ends=False, last=False):
                for i in range(2):
                    c = j * 2 + i
                    turn_ = seg + 1 if ends and i == 1 else seg
                    for q in range(CH):
                        if with_u:
                            low_u(j * 8 + (RING + i * CH + q), q)
                        if not (last and i == 1):
                            if turn_ == 1:
                                dve.wait_ge(act_back[q], j * 32 + (16 * (i + 2) - 16 * AHEAD))
                            else:
                                dve.wait_ge(gelu_done, j * 8 + ((i + 1) * CH + q + 1))
                            slot = j * 8 + ((i + 1) * CH + q - turn_ * RING)
                            tile = acts3[:, slot, :] if isinstance(j, int) else acts[:, bass.ds(slot * T, T)]
                            prepare(j * 2 + (i + 1), (i + 1) % 2, q, tile)
                        if q > 0:
                            flush(c, q - 1)
                        elif not (isinstance(c, int) and c == 0):
                            flush(j * 2 + (i - 1), CH - 1)

            chunk_pair(0, 0)
            with dve.Fori(1, 3) as j:
                chunk_pair(j, 0)
            chunk_pair(3, 0, ends=True)
            dve.wait_ge(u_lo, N_PRE)
            for turn_ in (1, 2):
                with dve.Fori(turn_ * 4, turn_ * 4 + 3) as j:
                    chunk_pair(j, turn_, with_u=True)
                chunk_pair(turn_ * 4 + 3, turn_, with_u=True, ends=True)
            with dve.Fori(12, 15) as j:
                chunk_pair(j, 3)
            chunk_pair(15, 3, last=True)
            flush(NCH - 1, CH - 1)


def layouts(I):
    def f(n):
        return np.asarray(I[n])

    def cols(v):
        return v.reshape(-1, P).T

    def t_blocks(w):
        k, g = w.shape[0] // P, w.shape[1] // P
        return w.reshape(k, P, g, P).transpose(2, 1, 0, 3)

    def n_blocks(w):
        k, b = w.shape[0] // P, w.shape[1] // BANK
        return w.reshape(k // 2, 2, P, b, BANK).transpose(3, 0, 2, 1, 4)

    w = f("w_in")[0]
    parts = np.split(w, np.cumsum([512] * 6 + [MLH, MLH, 512, 512]), axis=1)
    sq, sk, sv, mq, mk, mv, wi, wf, mo, eq, wg = parts
    conv_w = f("conv_w")[0].reshape(4, 8, P).transpose(2, 1, 0).reshape(P, 32)
    par = [cols(f("g_mix")[0]), cols(f("mem_norm_g")[0]), cols(f("g_ffn")[0]), cols(f("b_gate")[0]), conv_w,
           cols(f("conv_b")[0]), cols(f("ml_norm_g")[0]), cols(f("q_norm_g")[0]), cols(f("k_norm_g")[0])]
    def pad(a):
        return np.pad(a, ((0, 0), (0, P - a.shape[1])))

    def items(a):
        return a.reshape(-1, P, D)

    branches = np.concatenate([t_blocks(f(n)[0]).reshape(4, 2, P, 4, P).transpose(0, 2, 1, 3, 4)
                               for n in ("w_sb_o", "w_ml_o", "w_mem_o")])
    keys = np.stack([f("peer_k1")[0], f("peer_k2")[0]], axis=1)
    L = {
        "x": f("x")[0], "mem": f("mem")[0], "cols": np.concatenate(par, axis=1),
        "bif": np.stack([f("b_igate")[0], f("b_fgate")[0]], axis=1),
        "w": np.concatenate([items(a) for a in (
            t_blocks(np.concatenate([sq, sk, mq, mk, pad(wi), pad(wf)], axis=1)),
            n_blocks(np.concatenate([sv, mv, mo, eq], axis=1)), n_blocks(f("w_mem_kv")[0]),
            t_blocks(wg), branches, n_blocks(f("w_out")[0]), t_blocks(f("w_peer_q")[0]))]),
        "keysT": keys.transpose(3, 0, 1, 2).reshape(P, 2 * PH, NKEYS),
        "u": f("peer_u")[0].reshape(NKEYS, NKEYS, KD, P).transpose(1, 3, 2, 0).reshape(NKEYS, P, D),
        "v": f("peer_v")[0].reshape(NKEYS, NKEYS, D).transpose(1, 0, 2),
    }
    return {n: np.ascontiguousarray(a) for n, a in L.items()}


def kernel(**inputs):
    import concourse.bacc as bacc
    from concourse.bass_utils import run_bass_kernel_spmd

    nc = bacc.Bacc("TRN2", target_bir_lowering=False, num_devices=1)
    arrays = layouts(inputs)
    aps = {n: nc.dram_tensor(f"in_{n}", a.shape, mybir.dt.from_np(a.dtype), kind="ExternalInput").ap()
           for n, a in arrays.items()}
    out = nc.dram_tensor("out_h", (T, D), F32, kind="ExternalOutput").ap()
    gates_dram = nc.dram_tensor("gates", (NBLK, P, NKEYS * BLK), F32, kind="Internal").ap()
    pre_dram = nc.dram_tensor("gates_pre", (12, P, 2 * T), F32, kind="Internal").ap()
    acts_dram = nc.dram_tensor("acts_out", (N_PRE - RING, P, T), F32, kind="Internal").ap()
    build(nc, aps, out, gates_dram, pre_dram, acts_dram)
    r = run_bass_kernel_spmd(nc, [{f"in_{n}": a for n, a in arrays.items()}], core_ids=[0])
    return r.results[0]["out_h"].reshape(1, T, D)
```
